# Optimizing a Trainium2 kernel written in Bass

```python
import math
import jax, jax.numpy as jnp
from jax import lax
import numpy as np

D_MODEL = 1024
BATCH = 1
SEQ = 512
DEPTH = 2

CHUNK = 64
N_META = 16
N_MIXERS = 2
D_FF = 4 * D_MODEL
EPS = 1e-6

M_HEADS = 8
M_DQK = D_MODEL // (2 * M_HEADS)
M_DV = D_MODEL // M_HEADS
M_QK = M_HEADS * M_DQK
M_V = M_HEADS * M_DV
M_IN = 2 * M_QK + 2 * M_V + 2 * M_HEADS
M_CHUNK = 64

A_HEADS = 8
A_DH = D_MODEL // (2 * A_HEADS)
A_DV = 2 * A_DH
Q_BLOCK = 128
SUBLN_EPS = 1e-5

N_MLSTM = (DEPTH + 1) // 2
N_DIFF = DEPTH // 2

kernel_name = "hybrid_mlstm_diffattn_stream_encoder"

def rmsnorm(x, g, eps=EPS):
    xf = x.astype(jnp.float32)
    y = xf * lax.rsqrt(jnp.mean(xf * xf, axis=-1, keepdims=True) + eps)
    return (y * g.astype(jnp.float32)).astype(x.dtype)

def chunk_end(p):
    if p < N_META:
        return N_META
    return N_META + ((p - N_META) // CHUNK + 1) * CHUNK

def mlstm_mixer(h, w_in, b_gate, head_gain, w_out):
    B, L, _ = h.shape
    f32 = jnp.float32
    proj = (h @ w_in).astype(f32)
    q, k, v, o, gates = jnp.split(proj, [M_QK, 2 * M_QK, 2 * M_QK + M_V, 2 * M_QK + 2 * M_V], axis=-1)
    gates = gates + b_gate.astype(f32)
    ig, fg = gates[..., :M_HEADS], gates[..., M_HEADS:]

    pad = (-L) % M_CHUNK
    Lp = L + pad
    nc = Lp // M_CHUNK

    def to_chunks(t, d):
        t = jnp.pad(t, ((0, 0), (0, pad), (0, 0)))
        return t.reshape(B, nc, M_CHUNK, M_HEADS, d).transpose(0, 3, 1, 2, 4)

    def gate_chunks(g):
        g = jnp.pad(g, ((0, 0), (0, pad), (0, 0)))
        return g.reshape(B, nc, M_CHUNK, M_HEADS).transpose(0, 3, 1, 2)

    qc = to_chunks(q, M_DQK) * (M_DQK ** -0.5)
    kc = to_chunks(k, M_DQK)
    vc = to_chunks(v, M_DV)
    igc = gate_chunks(ig)
    lfc = gate_chunks(jax.nn.log_sigmoid(fg))

    b = jnp.cumsum(lfc, axis=-1)
    b_end = b[..., -1]
    a = b_end[..., None] - b + igc

    def step(carry, inp):
        C, n, m = carry
        k_s, v_s, a_s, be = inp
        m_new = jnp.maximum(be + m, jnp.max(a_s, axis=-1))
        decay = jnp.exp(be + m - m_new)
        w = jnp.exp(a_s - m_new[..., None])
        C_new = decay[..., None, None] * C + jnp.einsum('bhs,bhsd,bhse->bhde', w, k_s, v_s)
        n_new = decay[..., None] * n + jnp.einsum('bhs,bhsd->bhd', w, k_s)
        return (C_new, n_new, m_new), (C, n, m)

    init = (jnp.zeros((B, M_HEADS, M_DQK, M_DV), f32),
            jnp.zeros((B, M_HEADS, M_DQK), f32),
            jnp.zeros((B, M_HEADS), f32))
    xs = (kc.transpose(2, 0, 1, 3, 4), vc.transpose(2, 0, 1, 3, 4),
          a.transpose(2, 0, 1, 3), b_end.transpose(2, 0, 1))
    _, (C_prev, n_prev, m_prev) = lax.scan(step, init, xs)
    C_prev = C_prev.transpose(1, 2, 0, 3, 4)
    n_prev = n_prev.transpose(1, 2, 0, 3)
    m_prev = m_prev.transpose(1, 2, 0)

    causal = np.tril(np.ones((M_CHUNK, M_CHUNK), dtype=bool))
    log_d = jnp.where(causal, b[..., :, None] - b[..., None, :] + igc[..., None, :], -jnp.inf)
    m_inter = b + m_prev[..., None]
    m_t = jnp.maximum(m_inter, jnp.max(log_d, axis=-1))
    d_mat = jnp.exp(log_d - m_t[..., None])
    s = jnp.einsum('bhctd,bhcsd->bhcts', qc, kc) * d_mat
    inter = jnp.exp(m_inter - m_t)
    num = (inter[..., None] * jnp.einsum('bhctd,bhcde->bhcte', qc, C_prev)
           + jnp.einsum('bhcts,bhcse->bhcte', s, vc))
    den = inter * jnp.einsum('bhctd,bhcd->bhct', qc, n_prev) + jnp.sum(s, axis=-1)
    hh = num / jnp.maximum(jnp.abs(den), jnp.exp(-m_t))[..., None]

    hh = hh.transpose(0, 2, 3, 1, 4).reshape(B, Lp, M_HEADS, M_DV)[:, :L]
    hh = hh * lax.rsqrt(jnp.mean(hh * hh, axis=-1, keepdims=True) + EPS)
    hh = hh * head_gain.astype(f32).reshape(M_HEADS, M_DV)
    out = (jax.nn.sigmoid(o) * hh.reshape(B, L, M_V)).astype(h.dtype)
    return out @ w_out

def diff_attention(h, w_in, lam_vecs, head_gain, w_out, layer_idx):
    B, L, _ = h.shape
    f32 = jnp.float32
    lambda_init = 0.8 - 0.6 * math.exp(-0.3 * layer_idx)
    proj = h @ w_in
    q, k, v = jnp.split(proj, 3, axis=-1)
    q = (q.astype(f32) * (A_DH ** -0.5)).reshape(B, L, A_HEADS, 2, A_DH)
    k = k.astype(f32).reshape(B, L, A_HEADS, 2, A_DH)
    v = v.astype(f32).reshape(B, L, A_HEADS, A_DV)
    lv = lam_vecs.astype(f32)
    lam = jnp.exp(jnp.sum(lv[0] * lv[1])) - jnp.exp(jnp.sum(lv[2] * lv[3])) + lambda_init

    pos = np.arange(L)
    cid = np.where(pos < N_META, 0, 1 + (pos - N_META) // CHUNK)
    outs = []
    for s0 in range(0, L, Q_BLOCK):
        e0 = min(s0 + Q_BLOCK, L)
        ke = min(L, chunk_end(e0 - 1))
        mask = cid[None, :ke] <= cid[s0:e0, None]
        sc = jnp.einsum('bqhcd,bkhcd->bhcqk', q[:, s0:e0], k[:, :ke])
        p = jax.nn.softmax(jnp.where(mask, sc, -jnp.inf), axis=-1)
        attn = p[:, :, 0] - lam * p[:, :, 1]
        outs.append(jnp.einsum('bhqk,bkhe->bqhe', attn, v[:, :ke]))
    o = jnp.concatenate(outs, axis=1)
    o = o * lax.rsqrt(jnp.mean(o * o, axis=-1, keepdims=True) + SUBLN_EPS)
    o = o * head_gain.astype(f32).reshape(A_HEADS, A_DV) * (1.0 - lambda_init)
    return o.reshape(B, L, A_HEADS * A_DV).astype(h.dtype) @ w_out

def sq_relu_mlp(y, w_up, w_down):
    u = y @ w_up
    return jnp.square(jax.nn.relu(u)) @ w_down

def setup_inputs(seed: int = 0) -> dict:
    key = jax.random.key(seed)
    ks = jax.random.split(key, 16)
    nrm = jax.random.normal
    f32 = jnp.float32
    x = nrm(ks[0], (BATCH, SEQ, D_MODEL), f32)
    meta_tokens = nrm(ks[1], (N_META, D_MODEL), f32)
    norm_gains = 1.0 + 0.02 * nrm(ks[2], (DEPTH, 2, D_MODEL), f32)
    mlstm_w_in = nrm(ks[3], (N_MLSTM, D_MODEL, M_IN), f32) * D_MODEL ** -0.5
    ig_bias = 0.1 * nrm(ks[4], (N_MLSTM, M_HEADS), f32)
    fg_bias = jnp.linspace(3.0, 6.0, M_HEADS, dtype=f32)[None, :] + 0.1 * nrm(ks[5], (N_MLSTM, M_HEADS), f32)
    mlstm_b_gate = jnp.concatenate([ig_bias, fg_bias], axis=-1)
    mlstm_head_gain = 1.0 + 0.02 * nrm(ks[6], (N_MLSTM, M_V), f32)
    mlstm_w_out = nrm(ks[7], (N_MLSTM, M_V, D_MODEL), f32) * M_V ** -0.5
    diff_w_in = nrm(ks[8], (N_DIFF, D_MODEL, 3 * D_MODEL), f32) * D_MODEL ** -0.5
    diff_lambda = 0.1 * nrm(ks[9], (N_DIFF, 4, A_DH), f32)
    diff_head_gain = 1.0 + 0.02 * nrm(ks[10], (N_DIFF, A_HEADS * A_DV), f32)
    diff_w_out = nrm(ks[11], (N_DIFF, A_HEADS * A_DV, D_MODEL), f32) * (A_HEADS * A_DV) ** -0.5
    mlp_w_up = nrm(ks[12], (DEPTH, D_MODEL, D_FF), f32) * D_MODEL ** -0.5
    mlp_w_down = nrm(ks[13], (DEPTH, D_FF, D_MODEL), f32) * D_FF ** -0.5
    final_gain = 1.0 + 0.02 * nrm(ks[14], (D_MODEL,), f32)
    return {"x": x, "meta_tokens": meta_tokens, "norm_gains": norm_gains,
            "mlstm_w_in": mlstm_w_in, "mlstm_b_gate": mlstm_b_gate,
            "mlstm_head_gain": mlstm_head_gain, "mlstm_w_out": mlstm_w_out,
            "diff_w_in": diff_w_in, "diff_lambda": diff_lambda,
            "diff_head_gain": diff_head_gain, "diff_w_out": diff_w_out,
            "mlp_w_up": mlp_w_up, "mlp_w_down": mlp_w_down, "final_gain": final_gain}

def reference(x, meta_tokens, norm_gains, mlstm_w_in, mlstm_b_gate, mlstm_head_gain, mlstm_w_out,
              diff_w_in, diff_lambda, diff_head_gain, diff_w_out, mlp_w_up, mlp_w_down, final_gain):
    B = x.shape[0]
    meta = jnp.broadcast_to(meta_tokens.astype(x.dtype)[None], (B, N_META, D_MODEL))
    h = jnp.concatenate([meta, x], axis=1)
    for i in range(DEPTH):
        j = i // N_MIXERS
        y = rmsnorm(h, norm_gains[i, 0])
        if i % N_MIXERS == 0:
            y = mlstm_mixer(y, mlstm_w_in[j], mlstm_b_gate[j], mlstm_head_gain[j], mlstm_w_out[j])
        else:
            y = diff_attention(y, diff_w_in[j], diff_lambda[j], diff_head_gain[j], diff_w_out[j], i)
        h = h + y
        h = h + sq_relu_mlp(rmsnorm(h, norm_gains[i, 1]), mlp_w_up[i], mlp_w_down[i])
    h = rmsnorm(h, final_gain)
    return h[:, N_META:]


_drawn_inputs = setup_inputs


def setup_inputs(seed=0):
    import zlib

    import numpy as np

    out = dict(_drawn_inputs(seed))
    spreads = {}
    factors = {'mlstm_head_gain': 5.08, 'diff_lambda': 8.0, 'diff_head_gain': 7.245, 'final_gain': 2.853}
    for name, (base, spread) in spreads.items():
        noise = np.random.default_rng([zlib.crc32(name.encode()), seed]).standard_normal(out[name].shape)
        drawn = base * np.exp(spread * noise) if base else spread * noise
        out[name] = __import__('jax').numpy.asarray(drawn.astype(out[name].dtype))
    for name, factor in factors.items():
        out[name] = (out[name] * factor).astype(out[name].dtype)
    return out
```

```python
from contextlib import ExitStack
import math

import concourse.bass as bass
from concourse import mybir

ALU = mybir.AluOpType
ACT = mybir.ActivationFunctionType
AX = mybir.AxisListType
F32 = mybir.dt.float32
F32R = mybir.dt.float32r
BF16 = mybir.dt.bfloat16
ds = bass.ds

P = 128
D = 1024
NMETA = 16
X = 512
T = NMETA + X
HALF = T // 2
CB = D // P
FF = 4096
GROUPS = FF // D
HEADS = 8
DQK = 64
GATE_COL = 3072
FG_ROW = 32
EPS = 1e-6
SUBLN_EPS = 1e-5
LAMBDA_INIT = 0.8 - 0.6 * math.exp(-0.3)
NEG = -1e30
SCORE_SCALE = DQK ** -0.5
NM_MAX = 28.0

RING = 4
RAW = 2
AHEAD = 2
MISSED = [(0, 0), (7, 6)]

U_IN0, U_OUT0, U_MLP0 = 0, 24, 32
U_IN1, U_OUT1, U_MLP1 = 96, 120, 128
U_END = 192

ALL = [(0, HALF), (HALF, HALF)]
SEQ = [(NMETA, X)]

B_NUM, B_DEN, B_TR, B_SUM = 4, 6, 4, 6

QSPLIT = 256
PIECES = [(0, 0, 256, 0, 0), (1, 128, 256, 0, 256),
          (0, 256, 528, 1, 0), (3, 384, 528, 1, 272),
          (1, 256, 528, 2, 0),
          (2, 256, 528, 3, 0), (4, 512, 528, 3, 272)]
DCOL = [sum(q[2] - q[1] for q in PIECES[:n]) for n in range(len(PIECES) + 1)]
DW = DCOL[-1]
D_FULL = DCOL[-2]
P_BANKS = [(0, 384, 0), (1, 416, 384), (2, 272, 800), (3, 272, 1072)]
DIAG = [(DCOL[0], 128), (DCOL[1], 128), (DCOL[5], 128), (DCOL[3], 128), (DCOL[6], 16)]

B_SC, B_TR1, B_PV1 = (2, 4), 6, 7
B_Q1 = 3
TILES0 = [(0, 128), (128, 128), (256, 128), (384, 128), (512, 16)]
TILES1 = [(16, 128), (144, 128), (272, 128), (400, 128), (0, 16)]


def wait(eng, sem, value):
    if not isinstance(value, int) or value > 0:
        eng.wait_ge(sem, value)


def heads_loop(eng, lead, step, tail=1):
    pairs = (HEADS - 1 - lead) // 2
    for h in range(-lead, 1):
        step(h, h % 2, h // 2)
    with eng.Fori(0, pairs) as i:
        step(i * 2 + 1, 1, i)
        step(i * 2 + 2, 0, i + 1)
    for h in range(2 * pairs + 1, HEADS + tail):
        step(h, h % 2, h // 2)


def exists(h):
    return not isinstance(h, int) or 0 <= h < HEADS


def program(nc, a, out):
    with ExitStack() as ctx:
        cursor = [(nc.sbuf_base + 63) // 64 * 64]
        limit = nc.sbuf_usable_end

        def place(name, shape, dt, where, end):
            size = 2 if dt == BF16 else 4
            for n in shape[1:]:
                size *= n
            size = (size + 31) // 32 * 32
            assert where[0] + size <= end, (name, where[0] + size - end)
            t = nc.alloc_sbuf_tensor_at(name, shape, dt, offset=where[0])
            where[0] += size
            return t

        def new(name, shape, dt=F32):
            return place(name, shape, dt, cursor, limit)

        h = new("h", [P, CB, T])
        y_at = cursor[0]
        yh = new("yh", [P, CB, T], F32R)
        yl = new("yl", [P, CB, T], F32R)
        y_end = a_at = cursor[0]
        ah = new("ah", [P, CB, T], F32R)
        al = new("al", [P, CB, T], F32R)
        a_end = cursor[0]
        wh = new("wh", [P, RING, CB, P], F32R)
        wl = new("wl", [P, RING, CB, P], F32R)
        raw = new("raw", [P, RAW, CB, 2 * P])
        tbuf = new("tbuf", [P, T])
        abuf = new("abuf", [P, T])
        acc = new("acc", [P, T])
        rb = new("rb", [P, T])
        ident = new("ident", [P, P])
        ones = new("ones", [P, P])
        causal = new("causal", [P, P])
        head_mean = new("head_mean", [P, P])
        gains = new("gains", [P, 48])
        gain_rows = new("gain_rows", [48, P])
        eps_d = new("eps_d", [P, 1])
        eps_s = new("eps_s", [P, 1])
        bias_i = new("bias_i", [HEADS, 1])
        bias_f = new("bias_f", [64, 1])
        stat = new("stat", [P, 2, 8])
        lam = new("lam", [P, 8])
        ucol = new("ucol", [P, 5, HEADS])
        neg_row = new("neg_row", [1, P], BF16)
        one_row = new("one_row", [1, 64], BF16)
        arena = cursor[0]

        w0 = [arena]
        xin = place("xin", [P, 4, D], F32, w0, limit)
        meta_in = place("meta_in", [NMETA, D], F32, w0, limit)
        w0 = [arena]
        qk = place("qk", [P, CB, T], F32, w0, limit)
        osig = place("osig", [P, CB, T], F32, w0, limit)
        vt0 = place("vt0", [P, 5, HEADS, P], F32, w0, limit)
        vf0 = place("vf0", [P, 2, T], F32, [w0[0]], limit)
        dmat1 = place("dmat1", [P, DW], F32, w0, limit)
        w0 = [y_at]
        ks, qhs, qls, vth0, mbc, nmbc = ([place(f"{name}{par}", shape, dt, w0, y_end) for par in range(2)]
                                         for name, shape, dt in (("ks", [P, T], F32R), ("qhs", [P, T], F32R),
                                                                 ("qls", [P, T], F32R), ("vth0_", [P, 5, P], F32),
                                                                 ("mbc", [P, T], F32), ("nmbc", [P, T], F32)))
        dmat = [place("dmat0", [P, DW], F32, w0, y_end), dmat1]
        w0 = [a_at]
        gx, gabs, gexp, gln, glf, gone = (place(n, [64, T], F32, w0, a_end)
                                          for n in ("gx", "gabs", "gexp", "gln", "glf", "gone"))
        gi, gb, gu, gm, gnm = (place(n, [HEADS, T], F32, w0, a_end) for n in ("gi", "gb", "gu", "gm", "gnm"))
        graw = place("graw", [P, CB, 16], F32, w0, a_end)
        gwh = place("gwh", [P, CB, 40], F32R, w0, a_end)
        gwl = place("gwl", [P, CB, 40], F32R, w0, a_end)
        w0 = [arena]
        qf1 = place("qf1", [P, T], F32, w0, limit)
        kf1 = place("kf1", [P, T], F32, w0, limit)
        vf1 = place("vf1", [P, T], F32, w0, limit)
        qst = [[place(f"qst{par}{c}", [P, X], F32R, w0, limit) for c in range(2)] for par in range(2)]
        khs = [[place(f"khs{par}{c}", [P, T], F32R, w0, limit) for c in range(2)] for par in range(2)]
        kls = [[place(f"kls{par}{c}", [P, T], F32R, w0, limit) for c in range(2)] for par in range(2)]
        vth1 = [place(f"vth1{par}", [P, 5, P], F32, w0, limit) for par in range(2)]
        att = place("att", [P, 4, X], F32, w0, limit)
        att_meta = place("att_meta", [NMETA, X], F32, w0, limit)
        attn = place("attn", [P, 4, T], F32, w0, limit)
        es = [[place("e00", [P, T], F32, w0, limit), place("e01", [P, T], F32, w0, limit)],
              [tbuf, place("e11", [P, T], F32, w0, limit)]]
        zf = place("zf", [P, X], F32, w0, limit)
        lamv = place("lamv", [P, 4, DQK], F32, [a_at], a_end)
        w0 = [arena]
        fin = place("fin", [P, 4, D], F32, w0, limit)
        gfin = place("gfin", [P, D], F32, w0, limit)
        sqf = place("sqf", [P, D], F32, w0, limit)

        ps = ctx.enter_context(nc.psum_tensor("ps", [P, 8, 512], F32))
        gate_rows = nc.dram_tensor("gate_rows", [2 * HEADS, T], F32).ap()

        def sem(name):
            return ctx.enter_context(nc.semaphore(name))

        def sems(names):
            return [sem(n) for n in names.split()]

        raw_in = [sem(f"raw_in{i}") for i in range(RAW)]
        mrow_in = [sem(f"mrow_in{i}") for i in range(2)]
        nrow_in = [sem(f"nrow_in{i}") for i in range(2)]
        x_in, small_in, lamv_in, gfin_in, gate_sent, out_sent = sems("x_in small_in lamv_in gfin_in gate_sent out_sent")
        consts, ident_made, gain_t, gain_rd, gw_zero, gwh_done, gw_ready = sems(
            "consts ident_made gain_t gain_rd gw_zero gwh_done gw_ready")
        x_t, hx_rd, hm_rd = sems("x_t hx_rd hm_rd")
        split_hi, split_lo, unit_done, evac = sems("split_hi split_lo unit_done evac")
        h_ready, yh_done, y_ready, sq_done, acc_done, sum_done, ln_done, rb_ready = sems(
            "h_ready yh_done y_ready sq_done acc_done sum_done ln_done rb_ready")
        relu_done, sqa_done, ah_done, a_ready = sems("relu_done sqa_done ah_done a_ready")
        gate_mm, gate_dve, gate_act, u_t, ucol_rd = sems("gate_mm gate_dve gate_act u_t ucol_rd")
        v_t, vt_rd = sems("v_t vt_rd")
        sig_done, og_done = sems("sig_done og_done")
        stack_hi, stack_lo, vth_rd, dpre, dexp, dready, emn_done = sems(
            "stack_hi stack_lo vth_rd dpre dexp dready emn_done")
        s_done, p_ready, pv_done, den_done, num_rd, den_sq, x_rd, ssq_done, t_rd = sems(
            "s_done p_ready pv_done den_done num_rd den_sq x_rd ssq_done t_rd")
        hln_done, rs_rd, zz_rd, z_mul, zh_rd, z_ready = sems("hln_done rs_rd zz_rd z_mul zh_rd z_ready")
        unit_in = [sem(f"unit_in{i}") for i in range(3)]
        qhi_done, qlo_done, khi_done, klo_done, v_t1, vt_rd1, meta_t, meta_rd = sems(
            "qhi_done qlo_done khi_done klo_done v_t1 vt_rd1 meta_t meta_rd")
        pv_done1, pv_rd1, ssq_done1, hln_done1, rs_rd1, z_mul1, zh_rd1 = sems(
            "pv_done1 pv_rd1 ssq_done1 hln_done1 rs_rd1 z_mul1 zh_rd1")
        sc_done = [sem(f"sc_done{c}") for c in range(2)]
        max_done = [sem(f"max_done{c}") for c in range(2)]
        exp_done = [sem(f"exp_done{c}") for c in range(2)]
        rden_rd, nlam_rd, e1_rd, attn_rd, at_t, at_rd = sems("rden_rd nlam_rd e1_rd attn_rd at_t at_rd")
        lam_dve, lam_act = sems("lam_dve lam_act")
        out_t, fsq, fln, frs, fmul = sems("out_t fsq fln frs fmul")

        w_in0, w_in1 = a["mlstm_w_in"][0], a["diff_w_in"][0]
        w_out0, w_out1 = a["mlstm_w_out"][0], a["diff_w_out"][0]

        def columns(w, c0, n):
            return w.rearrange("(k p) m -> p k m", p=P)[:, :, ds(c0, n)]

        def halves(t):
            return t.rearrange("p (s n) -> p s n", s=2)

        def banks(u, spans):
            b = 2 * (u % 2)
            return ps[:, b:b + 2, 0:HALF] if len(spans) == 2 else ps[:, u % 4, 0:X]

        def tokens(t, spans):
            return halves(t) if len(spans) == 2 else t[:, NMETA:T]

        block = ctx.enter_context(nc.Block())

        @block.sync
        def _(sp):
            sp.dma_start(xin[:, :, :], a["x"][0].rearrange("(i p) d -> p i d", p=P)).then_inc(x_in, 16)
            sp.dma_start(meta_in[:, :], a["meta_tokens"]).then_inc(x_in, 16)
            sp.dma_start(gain_rows[0:32, :], a["norm_gains"].rearrange("l n (c p) -> (l n c) p", p=P)).then_inc(small_in, 16)
            sp.dma_start(gain_rows[32:40, :], a["mlstm_head_gain"].rearrange("l (c p) -> (l c) p", p=P)).then_inc(small_in, 16)
            sp.dma_start(gain_rows[40:48, :], a["diff_head_gain"].rearrange("l (c p) -> (l c) p", p=P)).then_inc(small_in, 16)
            bg = a["mlstm_b_gate"].rearrange("l (g o) -> (l g) o", o=1)
            sp.dma_start(bias_i[:, :], bg[0:HEADS, :]).then_inc(small_in, 16)
            sp.dma_start(bias_f[FG_ROW:FG_ROW + HEADS, :], bg[HEADS:2 * HEADS, :]).then_inc(small_in, 16)
            sp.dma_start(graw[:, :, :], columns(w_in0, GATE_COL, 16)).then_inc(small_in, 16)

            def load(slot, src, split=None):
                if split is not None:
                    sp.wait_ge(split_lo, split)
                sp.dma_start(raw[:, slot, :, :], src).then_inc(raw_in[slot], 16)

            def load_unit(slot, src, split):
                sp.wait_ge(split_lo, split)
                sp.dma_start(raw[:, slot // 2, :, P * (slot % 2):P * (slot % 2) + P], src).then_inc(unit_in[slot], 16)

            def quads(w, base, n):
                if base == 0:
                    for j in range(2):
                        load(j, columns(w, 256 * j, 256))
                with sp.Fori(1 if base == 0 else 0, n) as i:
                    for j in range(2):
                        load(j, columns(w, i * 512 + 256 * j, 256), i * 4 + (base + 2 * j - 2))

            def mlp(layer, base):
                up = a["mlp_w_up"][layer]
                down = a["mlp_w_down"][layer].rearrange("(g k p) m -> g p k m", k=CB, p=P)
                with sp.Fori(0, GROUPS) as g:
                    for j in range(4):
                        load(j % 2, columns(up, g * D + 256 * j, 256), g * 16 + (base + 2 * j - 2))
                    for j in range(4):
                        src = down[ds(g, 1), :, :, 256 * j:256 * j + 256].rearrange("g p k m -> p (g k) m")
                        load(j % 2, src, g * 16 + (base + 8 + 2 * j - 2))

            quads(w_in0, U_IN0, 6)
            quads(w_out0, U_OUT0, 2)
            mlp(0, U_MLP0)
            with sp.Fori(0, HEADS) as i:
                for j in range(3):
                    load_unit(j, columns(w_in1, i * P + D * j, P), i * 3 + (U_IN1 + j - 2))
            for j in range(2):
                load_unit(j, columns(w_out1, P * j, P), U_OUT1 + j - 2)
            load(1, columns(w_out1, 256, 256), U_OUT1)
            for j in range(2):
                load(j, columns(w_out1, 512 + 256 * j, 256), U_OUT1 + 4 + 2 * j - 2)
            mlp(1, U_MLP1)

            for i in range(4):
                sp.wait_ge(fmul, i + 1)
                sp.dma_start(out[0, P * i:P * (i + 1), :], fin[:, i, :]).then_inc(out_sent, 16)
            sp.wait_ge(out_sent, 4 * 16)

        @block.gpsimd
        def _(pool):
            nc.gpsimd.memset(ones[:, :], 1.0).then_inc(consts, 1)
            nc.gpsimd.memset(head_mean[:, :], 1.0 / P).then_inc(consts, 1)
            nc.gpsimd.memset(eps_d[:, :], EPS).then_inc(consts, 1)
            nc.gpsimd.memset(eps_s[:, :], SUBLN_EPS).then_inc(consts, 1)
            nc.gpsimd.memset(one_row[:, :], 1.0).then_inc(consts, 1)
            nc.gpsimd.memset(neg_row[:, 0:64], NEG).then_inc(consts, 1)
            nc.gpsimd.memset(neg_row[:, 64:P], 0.0).then_inc(consts, 1)
            nc.gpsimd.memset(gone[:, :], 1.0).then_inc(consts, 1)
            nc.gpsimd.memset(gwh[:, :, :].bitcast(F32), 0.0).then_inc(gw_zero, 1)
            nc.gpsimd.memset(gwl[:, :, :].bitcast(F32), 0.0).then_inc(gw_zero, 1)
            pool.wait_ge(consts, 8)
            nc.gpsimd.affine_select(out=ident[:, :], in_=ones[:, :], compare_op=ALU.is_equal, fill=0.0, base=0,
                                    pattern=[[-1, P]], channel_multiplier=1).then_inc(ident_made, 1)
            nc.gpsimd.affine_select(out=causal[:, :], in_=ones[:, :], compare_op=ALU.is_ge, fill=0.0, base=0,
                                    pattern=[[1, P]], channel_multiplier=-1).then_inc(ident_made, 1)
            pool.wait_ge(ident_made, 2)

            pool.wait_ge(gate_dve, 10)
            pool.dma_start(gate_rows[0:HEADS, :], gm[:, :]).then_inc(gate_sent, 16)
            pool.dma_start(gate_rows[HEADS:2 * HEADS, :], gnm[:, :]).then_inc(gate_sent, 16)
            pool.wait_ge(gate_sent, 32)
            pool.wait_ge(unit_done, U_OUT0)

            def step0(hd, par, pair):
                nxt, nxt2 = hd + 1, hd + 2
                if exists(nxt):
                    wait(pool, x_rd, hd)
                    row = gate_rows[ds(nxt + HEADS, 1), :]
                    pool.dma_start(nmbc[1 - par][:, :], row.broadcast_to([P, T])).then_inc(nrow_in[1 - par], 16)
                if exists(nxt2):
                    wait(pool, dpre, nxt)
                    row = gate_rows[ds(nxt2, 1), :]
                    pool.dma_start(mbc[par][:, :], row.broadcast_to([P, T])).then_inc(mrow_in[par], 16)
                if exists(hd - 1):
                    pool.wait_ge(num_rd, hd)
                    wait(pool, z_ready, hd - 1)
                    nc.gpsimd.tensor_tensor(tbuf[:, :], rb[:, :], osig[:, ds(hd - 1, 1), :].rearrange("p o t -> p (o t)"),
                                            ALU.mult).then_inc(zz_rd, 1)
                if exists(nxt):
                    wait(pool, pv_done, hd)
                    wait(pool, vt_rd, HEADS)
                    nc.gpsimd.tensor_copy(vth0[1 - par][:, 0:4, :],
                                          vt0[:, 0:4, ds(nxt, 1), :].rearrange("p s o e -> p s (o e)"))
                    nc.gpsimd.tensor_copy(vth0[1 - par][0:16, 4, :],
                                          vt0[0:16, 4, ds(nxt, 1), :].rearrange("p o e -> p (o e)")).then_inc(vth_rd, 1)
                if exists(nxt2):
                    pool.wait_ge(dexp, hd + 3)
                    for c0, w in DIAG:
                        blk = dmat[par][0:w, c0:c0 + w]
                        last = nc.gpsimd.tensor_tensor(blk, blk, causal[0:w, 0:w], ALU.mult)
                    last.then_inc(dready, 1)

            heads_loop(pool, 2, step0)

            pool.wait_ge(unit_done, U_IN1)
            pool.dma_start(lamv[:, :, :], a["diff_lambda"][0:1].broadcast_to([P, 4, DQK])).then_inc(lamv_in, 16)
            pool.wait_ge(z_ready, 2 * HEADS)
            pool.dma_start(gfin[:, :], a["final_gain"].rearrange("(o d) -> o d", o=1).broadcast_to([P, D])).then_inc(gfin_in, 16)

        @block.scalar
        def _(act):
            def copy(o, i, scale=1.0):
                return nc.scalar.activation(o, i, ACT.Copy, scale=scale)

            def split(u, k, layer):
                if isinstance(u, int) and u >= U_END:
                    return
                if k % 2 == 0:
                    missed = 16 * MISSED[layer][k // 2]
                    act.wait_ge(raw_in[k // 2], (u - k) * 4 + (16 - missed))
                wait(act, unit_done, u - RING + 1)
                copy(wh[:, k, :, :], raw[:, k // 2, :, P * (k % 2):P * (k % 2) + P]).then_inc(split_hi, 1)

            def split_unit(u, j, came):
                act.wait_ge(unit_in[j], came * 16)
                act.wait_ge(unit_done, u - 2)
                copy(wh[:, j, :, :], raw[:, j // 2, :, P * (j % 2):P * (j % 2) + P]).then_inc(split_hi, 1)

            def norm_prep(n, b, spans):
                t0 = spans[0][0]
                copy(yh[:, b, t0:T], h[:, b, t0:T], gains[:, 8 * n + b:8 * n + b + 1]).then_inc(yh_done, 1)
                wait(act, acc_done, 8 * n + b)
                nc.scalar.activation(abuf[:, t0:T], h[:, b, t0:T], ACT.Square).then_inc(sq_done, 1)

            def norm_factor(n, spans):
                act.wait_ge(sum_done, n + 1)
                src = ps[:, B_SUM:B_SUM + 2, 0:HALF] if len(spans) == 2 else ps[:, B_SUM, 0:X]
                nc.scalar.activation(tokens(rb[:, :], spans), src, ACT.Ln, bias=eps_d[:, 0:1], scale=1.0 / D).then_inc(ln_done, 1)
                act.wait_ge(ln_done, n + 1)
                nc.scalar.activation(tokens(rb[:, :], spans), tokens(rb[:, :], spans), ACT.Exp, scale=-0.5).then_inc(rb_ready, 1)

            def values_out(n, vt):
                act.wait_ge(v_t, n + 1)
                hd = n % HEADS
                copy(vt[:, 0:4, hd, :], ps[:, B_TR, :].rearrange("p (s e) -> p s e", e=P))
                copy(vt[0:16, 4, hd, :], ps[0:16, B_TR + 1, 0:P]).then_inc(vt_rd, 1)

            nc.scalar.preload_act_table_set("natural_log_exp_and_others")
            for u in range(AHEAD):
                split(u, u, 0)
            for c in range(CB):
                act.wait_ge(x_t, c + 1)
                copy(h[:, c, 0:NMETA], ps[:, 4 + c % 2, 0:NMETA]).then_inc(hm_rd, 1)
                if c == 0:
                    act.wait_ge(gain_rd, 1)
                act.wait_ge(hm_rd, c + 1)
                act.wait_ge(hx_rd, c + 1)
                norm_prep(0, c, ALL)
            norm_factor(0, ALL)
            fg = slice(FG_ROW, FG_ROW + HEADS)
            act.wait_ge(gate_dve, 4)
            nc.scalar.activation(gabs[fg, :], gx[fg, :], ACT.Abs).then_inc(gate_act, 1)
            act.wait_ge(gate_act, 1)
            nc.scalar.activation(gexp[fg, :], gabs[fg, :], ACT.Exp, scale=-1.0).then_inc(gate_act, 1)
            act.wait_ge(gate_act, 2)
            nc.scalar.activation(gln[fg, :], gexp[fg, :], ACT.Ln, bias=1.0).then_inc(gate_act, 1)

            for k in range(8):
                split(k + AHEAD, (k + AHEAD) % 4, 0)
            act.wait_ge(u_t, 1)
            copy(ucol[:, 0:4, :], ps[:, B_SUM, 0:32].rearrange("p (s g) -> p s g", s=4))
            copy(ucol[0:16, 4, :], ps[0:16, B_SUM, 32:40]).then_inc(ucol_rd, 1)
            for k in range(8):
                split(U_IN0 + 8 + k + AHEAD, (k + AHEAD) % 4, 0)
                if k >= 2:
                    values_out(k - 2, vt0)
            split(16 + AHEAD, AHEAD, 0)
            values_out(6, vt0)
            split(17 + AHEAD, AHEAD + 1, 0)
            values_out(7, vt0)
            for k in range(8):
                if k >= 2:
                    split(16 + k + AHEAD, (k + AHEAD) % 4, 0)
                act.wait_ge(evac, 16 + k + 1)
                nc.scalar.activation(osig[:, k, :], osig[:, k, :], ACT.Sigmoid).then_inc(sig_done, 1)
            for k in range(8):
                act.wait_ge(sig_done, k + 1)
                copy(osig[:, k, :], osig[:, k, :], gains[:, 32 + k:33 + k]).then_inc(og_done, 1)

            nc.scalar.preload_act_table_set("natural_log_exp_and_others")
            act.wait_ge(unit_done, U_OUT0)

            def step0(hd, par, pair):
                b0, b1 = 64 * par, 64 - 64 * par
                n2 = hd + 2
                if exists(n2):
                    wait(act, s_done, hd + 1)
                    q = qk[b0:b0 + 64, ds(pair + 1, 1), :].rearrange("p o t -> p (o t)")
                    k = qk[b0:b0 + 64, ds(pair + 5, 1), :].rearrange("p o t -> p (o t)")
                    copy(ks[par][b0:b0 + 64, :], k)
                    copy(qhs[par][b0:b0 + 64, :], q)
                    copy(qhs[par][b1:b1 + 64, :], q).then_inc(stack_hi, 1)
                if exists(hd + 1):
                    act.wait_ge(nrow_in[1 - par], pair * 16 + (32 if par else 16))
                    nc.scalar.activation(nmbc[1 - par][:, :], nmbc[1 - par][:, :], ACT.Exp, scale=2.0).then_inc(emn_done, 1)
                if exists(hd - 1):
                    act.wait_ge(t_rd, hd)
                    nc.scalar.activation(acc[:, :], acc[:, :], ACT.Ln).then_inc(hln_done, 1)
                    act.wait_ge(hln_done, hd)
                    nc.scalar.activation(acc[:, :], acc[:, :], ACT.Exp, scale=-0.5).then_inc(rs_rd, 1)
                if exists(n2):
                    act.wait_ge(dpre, hd + 3)
                    nc.scalar.activation(dmat[par][:, 0:D_FULL], dmat[par][:, 0:D_FULL], ACT.Exp, scale=-1.0)
                    nc.scalar.activation(dmat[par][0:16, D_FULL:DW], dmat[par][0:16, D_FULL:DW], ACT.Exp,
                                         scale=-1.0).then_inc(dexp, 1)
                if exists(hd - 1):
                    act.wait_ge(z_mul, hd)
                    copy(ah[:, ds(hd - 1, 1), :].rearrange("p o t -> p (o t)"), tbuf[:, :]).then_inc(zh_rd, 1)
                if exists(hd):
                    act.wait_ge(pv_done, hd + 1)
                    wait(act, zz_rd, hd)
                    wait(act, ssq_done, hd)
                    if isinstance(hd, int) and hd == 0:
                        act.wait_ge(evac, U_OUT0)
                    for b, t0, t1 in ((B_NUM, 0, QSPLIT), (B_NUM + 1, QSPLIT, T)):
                        copy(rb[:, t0:t1], ps[:, b, 0:t1 - t0])
                        last = nc.scalar.activation(abuf[:, t0:t1], ps[:, b, 0:t1 - t0], ACT.Square)
                    last.then_inc(num_rd, 1)
                    act.wait_ge(den_done, hd + 1)
                    nc.scalar.activation(acc[:, 0:QSPLIT], ps[:, B_DEN, 0:QSPLIT], ACT.Square)
                    nc.scalar.activation(acc[:, QSPLIT:T], ps[:, B_DEN + 1, 0:T - QSPLIT], ACT.Square).then_inc(den_sq, 1)

            heads_loop(act, 2, step0)

            def out_product(layer, base, n, spans):
                for k in range(8):
                    if layer == 0:
                        split(base + k + AHEAD, (k + AHEAD) % 4, layer)
                    elif k < 6:
                        split(base + k + 4, k % 4, layer)
                    act.wait_ge(h_ready, base_h(n) + k + 1)
                    norm_prep(n, k, spans)

            def base_h(n):
                return 8 * (n - 1)

            def up_units(layer, base, g_all, spans, factor=None):
                t0 = spans[0][0]
                for k in range(8):
                    split(base + (k + AHEAD), (k + AHEAD) % 4, layer)
                    if factor is not None and k == 0:
                        norm_factor(factor, spans)
                    act.wait_ge(relu_done, g_all * 8 + (k + 1))
                    nc.scalar.activation(abuf[:, t0:T], tbuf[:, t0:T], ACT.Square).then_inc(sqa_done, 1)
                    nc.scalar.activation(ah[:, k, t0:T], tbuf[:, t0:T], ACT.Square).then_inc(ah_done, 1)

            def mlp(layer, base, spans):
                g0 = 4 * layer
                up_units(layer, base, g0, spans, factor=2 * layer + 1)
                for k in range(8):
                    split(base + 8 + k + AHEAD, (k + AHEAD) % 4, layer)
                with act.Fori(1, GROUPS - 1) as g:
                    up_units(layer, g * 16 + base, g + g0, spans)
                    for k in range(8):
                        split(g * 16 + (base + 8 + k + AHEAD), (k + AHEAD) % 4, layer)
                last = base + 16 * (GROUPS - 1)
                up_units(layer, last, g0 + GROUPS - 1, spans)
                for k in range(8):
                    if layer == 0 and k >= 8 - AHEAD:
                        split_unit(U_IN1 + k + AHEAD - 8, k + AHEAD - 8, 1)
                    else:
                        split(last + 8 + k + AHEAD, (k + AHEAD) % 4, layer)
                    if layer == 0:
                        act.wait_ge(h_ready, base_h(2) + k + 1)
                        norm_prep(2, k, ALL)

            out_product(0, U_OUT0, 1, ALL)
            mlp(0, U_MLP0, ALL)

            norm_factor(2, ALL)
            act.wait_ge(lam_dve, 2)
            nc.scalar.activation(lam[:, 2:4], lam[:, 0:2], ACT.Exp).then_inc(lam_act, 1)

            def scores(n, i, c):
                act.wait_ge(max_done[c], n + 1)
                if c == 0:
                    wait(act, attn_rd, n - 1)
                w = NMETA + P * (i + 1)
                b = B_SC[c]
                src = ps[:, b, 0:w] if i < 3 else ps[:, b:b + 2, 0:HALF]
                e = es[c][i % 2]
                dst = e[:, 0:w] if i < 3 else halves(e[:, :])
                nc.scalar.activation(dst, src, ACT.Exp, bias=stat[:, i % 2, c:c + 1],
                                     accum_out=stat[:, i % 2, 2 + c:3 + c]).then_inc(exp_done[c], 1)

            def turned(hd, n, i):
                act.wait_ge(at_t, n + 1)
                if i == 0:
                    wait(act, pv_done1, hd)
                copy(att[:, 0:i + 1, P * i:P * (i + 1)],
                     ps[:, B_TR1, 0:P * (i + 1)].rearrange("p (s t) -> p s t", t=P)).then_inc(at_rd, 1)

            def keys_hi(par, c):
                k = kf1[64 * c:64 * c + 64, :]
                copy(khs[1 - par][c][0:64, :], k)
                copy(khs[1 - par][c][64:128, :], k).then_inc(khi_done, 1)

            def step1(hd, par, pair):
                n1 = hd + 1
                if exists(hd - 1):
                    turned(hd - 1, hd * 4 - 1, 3)
                if exists(hd):
                    scores(hd * 4, 0, 0)
                    scores(hd * 4, 0, 1)
                if exists(n1):
                    split_unit(n1 * 3 + (U_IN1 + 2), 2, hd + 2)
                elif exists(hd):
                    act.wait_ge(unit_done, U_OUT1)
                    split(U_OUT1 + 2, 2, 1)
                if exists(hd):
                    act.wait_ge(v_t1, hd + 1)
                    copy(vth1[par][:, 0:4, :], ps[:, B_TR1, :].rearrange("p (s e) -> p s e", e=P))
                    copy(vth1[par][0:16, 4, :], ps[0:16, B_TR1 + 1, 0:P]).then_inc(vt_rd1, 1)
                if exists(hd - 1):
                    act.wait_ge(meta_t, hd)
                    copy(att_meta[:, :], ps[0:NMETA, B_TR1, :]).then_inc(meta_rd, 1)
                if exists(hd):
                    for c in range(2):
                        scores(hd * 4 + 1, 1, c)
                if exists(hd - 1):
                    act.wait_ge(pv_done1, hd)
                    wait(act, z_ready, hd + (HEADS - 1))
                    copy(zf[:, :], ps[:, B_PV1, :], gains[:, ds(hd + 39, 1)])
                    nc.scalar.activation(abuf[:, NMETA:T], ps[:, B_PV1, :], ACT.Square).then_inc(pv_rd1, 1)
                if exists(hd):
                    turned(hd, hd * 4, 0)
                if exists(n1):
                    act.wait_ge(evac, n1 * 3 + (U_IN1 + 1))
                    wait(act, sc_done[1], hd * 4)
                    for c in range(2):
                        b0 = 64 * c
                        last = copy(qst[1 - par][c][b0:b0 + 64, :], qf1[b0:b0 + 64, NMETA:T], SCORE_SCALE)
                    last.then_inc(qhi_done, 1)
                    split_unit(n1 * 3 + (U_IN1 + 3), 0, hd + 3)
                elif exists(hd):
                    split(U_OUT1 + 3, 3, 1)
                if exists(hd):
                    for c in range(2):
                        scores(hd * 4 + 2, 2, c)
                    turned(hd, hd * 4 + 1, 1)
                if exists(n1):
                    act.wait_ge(evac, n1 * 3 + (U_IN1 + 2))
                    keys_hi(par, 0)
                if exists(hd):
                    for c in range(2):
                        scores(hd * 4 + 3, 3, c)
                if exists(n1):
                    keys_hi(par, 1)
                if exists(hd):
                    turned(hd, hd * 4 + 2, 2)
                if exists(hd - 1):
                    act.wait_ge(ssq_done1, hd)
                    nc.scalar.activation(acc[:, NMETA:T], ps[:, B_PV1, :], ACT.Ln, bias=eps_s[:, 0:1]).then_inc(hln_done1, 1)
                    act.wait_ge(hln_done1, hd)
                    nc.scalar.activation(acc[:, NMETA:T], acc[:, NMETA:T], ACT.Exp, scale=-0.5).then_inc(rs_rd1, 1)
                if exists(n1):
                    split_unit(n1 * 3 + (U_IN1 + 4), 1, hd + 3)
                if exists(hd - 1):
                    act.wait_ge(z_mul1, hd)
                    copy(ah[:, ds(hd - 1, 1), NMETA:T].rearrange("p o t -> p (o t)"), zf[:, :]).then_inc(zh_rd1, 1)

            heads_loop(act, 1, step1)
            out_product(1, U_OUT1, 3, SEQ)
            mlp(1, U_MLP1, SEQ)

            for i in range(4):
                act.wait_ge(out_t, i + 1)
                nc.scalar.activation(sqf[:, :].rearrange("p (b n) -> p b n", b=2), ps[:, 2 * i:2 * i + 2, :], ACT.Square,
                                     accum_out=lam[:, i:i + 1]).then_inc(fsq, 1)
                act.wait_ge(fsq, i + 1)
                nc.scalar.activation(lam[:, i:i + 1], lam[:, i:i + 1], ACT.Ln, bias=eps_d[:, 0:1], scale=1.0 / D).then_inc(fln, 1)
                act.wait_ge(fln, i + 1)
                nc.scalar.activation(lam[:, i:i + 1], lam[:, i:i + 1], ACT.Exp, scale=-0.5).then_inc(frs, 1)

        @block.vector
        def _(dve):
            V = nc.vector

            def split(u, k):
                if isinstance(u, int) and u >= U_END:
                    return
                dve.wait_ge(split_hi, u + 1)
                V.tensor_tensor(wl[:, k, :, :], raw[:, k // 2, :, P * (k % 2):P * (k % 2) + P],
                                wh[:, k, :, :].bitcast(F32), ALU.subtract).then_inc(split_lo, 1)

            def norm_prep(n, b, spans):
                t0 = spans[0][0]
                dve.wait_ge(yh_done, 8 * n + b + 1)
                V.scalar_tensor_tensor(yl[:, b, t0:T], h[:, b, t0:T], gains[:, 8 * n + b:8 * n + b + 1],
                                       yh[:, b, t0:T].bitcast(F32), ALU.mult, ALU.subtract).then_inc(y_ready, 1)
                dve.wait_ge(sq_done, 8 * n + b + 1)
                if b == 0:
                    V.tensor_copy(acc[:, t0:T], abuf[:, t0:T]).then_inc(acc_done, 1)
                else:
                    dve.wait_ge(acc_done, 8 * n + b)
                    V.tensor_tensor(acc[:, t0:T], acc[:, t0:T], abuf[:, t0:T], ALU.add).then_inc(acc_done, 1)

            def scaled(u, k, spans, dest, src=None):
                dve.wait_ge(unit_done, u + 1)
                V.tensor_tensor(tokens(dest, spans), src or banks(k, spans), tokens(rb[:, :], spans), ALU.mult).then_inc(evac, 1)

            dve.wait_ge(gain_t, 1)
            V.tensor_copy(gains[:, :], ps[:, 7, 0:48]).then_inc(gain_rd, 1)
            dve.wait_ge(small_in, 6 * 16)
            dve.wait_ge(gw_zero, 2)
            V.tensor_copy(gwh[:, :, 0:HEADS], graw[:, :, 0:HEADS])
            V.tensor_copy(gwh[:, :, FG_ROW:FG_ROW + HEADS], graw[:, :, HEADS:2 * HEADS]).then_inc(gwh_done, 1)
            dve.wait_ge(gwh_done, 1)
            V.tensor_tensor(gwl[:, :, 0:HEADS], graw[:, :, 0:HEADS], gwh[:, :, 0:HEADS].bitcast(F32), ALU.subtract)
            V.tensor_tensor(gwl[:, :, FG_ROW:FG_ROW + HEADS], graw[:, :, HEADS:2 * HEADS],
                            gwh[:, :, FG_ROW:FG_ROW + HEADS].bitcast(F32), ALU.subtract).then_inc(gw_ready, 1)
            for u in range(AHEAD):
                split(u, u)
            for c in range(CB):
                dve.wait_ge(x_t, c + 1)
                V.tensor_copy(h[:, c, NMETA:T], ps[:, c % 4, :]).then_inc(hx_rd, 1)
                dve.wait_ge(hx_rd, c + 1)
                norm_prep(0, c, ALL)

            ig, fg = slice(0, HEADS), slice(FG_ROW, FG_ROW + HEADS)
            dve.wait_ge(rb_ready, 1)
            dve.wait_ge(gate_mm, 1)
            V.tensor_tensor(halves(gi[:, :]), ps[ig, 4:6, 0:HALF], halves(rb[ig, :]), ALU.mult).then_inc(gate_dve, 1)
            V.tensor_tensor(halves(gx[fg, :]), ps[fg, 4:6, 0:HALF], halves(rb[fg, :]), ALU.mult).then_inc(gate_dve, 1)
            dve.wait_ge(gate_dve, 1)
            V.tensor_scalar(gi[:, :], gi[:, :], bias_i[:, 0:1], None, ALU.add).then_inc(gate_dve, 1)
            dve.wait_ge(gate_dve, 2)
            V.tensor_scalar(gx[fg, :], gx[fg, :], bias_f[fg, 0:1], None, ALU.add).then_inc(gate_dve, 1)
            dve.wait_ge(gate_act, 3)
            V.scalar_tensor_tensor(glf[ig, :], gx[fg, :], 0.0, gln[fg, :], ALU.min, ALU.subtract).then_inc(gate_dve, 1)
            dve.wait_ge(gate_dve, 5)
            V.tensor_tensor_scan(gb[:, :], gone[ig, :], glf[ig, :], 0.0, ALU.mult, ALU.add).then_inc(gate_dve, 1)
            dve.wait_ge(gate_dve, 6)
            V.tensor_tensor(gu[:, :], gi[:, :], gb[:, :], ALU.subtract).then_inc(gate_dve, 1)
            dve.wait_ge(gate_dve, 7)
            V.tensor_tensor_scan(gm[:, :], gu[:, :], gu[:, :], 0.0, ALU.max, ALU.max).then_inc(gate_dve, 1)
            dve.wait_ge(gate_dve, 8)
            V.tensor_tensor(gnm[:, :], gb[:, :], gm[:, :], ALU.add).then_inc(gate_dve, 1)
            dve.wait_ge(gate_dve, 9)
            V.tensor_scalar(gnm[:, :], gnm[:, :], -1.0, NM_MAX, ALU.mult, ALU.min).then_inc(gate_dve, 1)

            def blk(t, j):
                return t[:, ds(j, 1), :].rearrange("p o t -> p (o t)")

            with dve.Fori(0, 2) as i:
                for k in range(4):
                    split(i * 4 + (k + AHEAD), (k + AHEAD) % 4)
                    scaled(i * 4 + k, k, ALL, blk(qk, i * 4 + k))
            for k in range(8):
                split(8 + k + AHEAD, (k + AHEAD) % 4)
                wait(dve, v_t, k - 1)
                scaled(8 + k, k, ALL, vf0[:, k % 2, :])
            with dve.Fori(4, 6) as i:
                for k in range(4):
                    split(i * 4 + (k + AHEAD), (k + AHEAD) % 4)
                    scaled(i * 4 + k, k, ALL, blk(osig, i * 4 + (k - 16)))

            def step0(hd, par, pair):
                b0, b1 = 64 * par, 64 - 64 * par
                n1, n2 = hd + 1, hd + 2
                if exists(n1):
                    dve.wait_ge(s_done, hd + 2)
                    dve.wait_ge(dready, hd + 2)
                    dm = dmat[1 - par]
                    for b, w, c0 in P_BANKS:
                        V.scalar_tensor_tensor(dm[:, c0:c0 + w], ps[:, b, 0:w], SCORE_SCALE, dm[:, c0:c0 + w],
                                               ALU.mult, ALU.mult)
                    V.scalar_tensor_tensor(dm[0:16, D_FULL:DW], ps[0:16, 3, 272:288], SCORE_SCALE, dm[0:16, D_FULL:DW],
                                           ALU.mult, ALU.mult).then_inc(p_ready, 1)
                if exists(hd - 1):
                    dve.wait_ge(ssq_done, hd)
                    dve.wait_ge(x_rd, hd)
                    V.scalar_tensor_tensor(acc[:, 0:QSPLIT], acc[:, 0:QSPLIT], EPS, ps[:, B_DEN, 0:QSPLIT],
                                           ALU.mult, ALU.add)
                    V.scalar_tensor_tensor(acc[:, QSPLIT:T], acc[:, QSPLIT:T], EPS, ps[:, B_DEN + 1, 0:T - QSPLIT],
                                           ALU.mult, ALU.add).then_inc(t_rd, 1)
                if exists(n2):
                    dve.wait_ge(stack_hi, hd + 3)
                    q, k = blk(qk, pair + 1)[b0:b0 + 64], blk(qk, pair + 5)[b0:b0 + 64]
                    V.tensor_tensor(ks[par][b1:b1 + 64, :], k, ks[par][b0:b0 + 64, :].bitcast(F32), ALU.subtract)
                    V.tensor_tensor(qls[par][b0:b0 + 64, :], q, qhs[par][b0:b0 + 64, :].bitcast(F32), ALU.subtract)
                    V.tensor_tensor(qls[par][b1:b1 + 64, :], q, qhs[par][b0:b0 + 64, :].bitcast(F32),
                                    ALU.subtract).then_inc(stack_lo, 1)
                    if isinstance(n2, int) and n2 < 2:
                        dve.wait_ge(ucol_rd, 1)
                    wait(dve, den_done, hd + 1)
                    dve.wait_ge(mrow_in[par], pair * 16 + 32)
                    for n, (j, t0, t1, _, _) in enumerate(PIECES):
                        rows = TILES0[j][1]
                        last = V.tensor_scalar(dmat[par][0:rows, DCOL[n]:DCOL[n + 1]], mbc[par][0:rows, t0:t1],
                                               ucol[0:rows, j, ds(n2, 1)], 0.0, ALU.subtract, ALU.max)
                    last.then_inc(dpre, 1)
                if exists(hd - 1):
                    dve.wait_ge(zz_rd, hd)
                    dve.wait_ge(rs_rd, hd)
                    V.tensor_tensor(tbuf[:, :], tbuf[:, :], acc[:, :], ALU.mult).then_inc(z_mul, 1)
                    dve.wait_ge(zh_rd, hd)
                    V.tensor_tensor(blk(al, hd - 1), tbuf[:, :], blk(ah, hd - 1).bitcast(F32), ALU.subtract).then_inc(z_ready, 1)
                if exists(hd):
                    dve.wait_ge(den_sq, hd + 1)
                    dve.wait_ge(emn_done, hd + 1)
                    V.tensor_tensor(acc[:, :], acc[:, :], nmbc[par][:, :], ALU.max).then_inc(x_rd, 1)

            heads_loop(dve, 2, step0)

            def residual(u, k, b, spans, ready=None):
                dve.wait_ge(unit_done, u + 1)
                ins = V.tensor_tensor(tokens(h[:, b, :], spans), banks(k, spans), tokens(h[:, b, :], spans), ALU.add)
                ins.then_inc(evac, 1)
                if ready is not None:
                    dve.wait_ge(evac, u + 1)
                    V.nop().then_inc(h_ready, 1)

            def out_product(base, n, spans):
                for k in range(8):
                    if n == 1:
                        split(base + k + AHEAD, (k + AHEAD) % 4)
                    residual(base + k, k, k, spans, ready=n)
                    if n == 3 and k < 6:
                        split(base + k + 4, k % 4)
                    norm_prep(n, k, spans)

            def up_units(base, spans, g_all, factor=None):
                t0 = spans[0][0]
                for k in range(8):
                    split(base + (k + AHEAD), (k + AHEAD) % 4)
                    if factor is not None and k == 0:
                        dve.wait_ge(rb_ready, factor + 1)
                    dve.wait_ge(unit_done, base + (k + 1))
                    V.scalar_tensor_tensor(tokens(tbuf[:, :], spans), banks(k, spans), 0.0, tokens(rb[:, :], spans),
                                           ALU.max, ALU.mult).then_inc(evac, 1)
                    dve.wait_ge(evac, base + (k + 1))
                    V.nop().then_inc(relu_done, 1)
                    dve.wait_ge(ah_done, g_all * 8 + (k + 1))
                    V.tensor_tensor(al[:, k, t0:T], abuf[:, t0:T], ah[:, k, t0:T].bitcast(F32), ALU.subtract).then_inc(a_ready, 1)

            def down_units(base, spans):
                for k in range(8):
                    split(base + (k + AHEAD), (k + AHEAD) % 4)
                    residual(base + k, k, k, spans)

            def mlp(layer, base, spans):
                g0 = 4 * layer
                up_units(base, spans, g0, factor=2 * layer + 1)
                down_units(base + 8, spans)
                with dve.Fori(1, GROUPS - 1) as g:
                    up_units(g * 16 + base, spans, g + g0)
                    down_units(g * 16 + (base + 8), spans)
                last = base + 16 * (GROUPS - 1)
                up_units(last, spans, g0 + GROUPS - 1)
                for k in range(8):
                    split(last + 8 + k + AHEAD, (k + AHEAD) % 4)
                    residual(last + 8 + k, k, k, spans, ready=layer)
                    if layer == 0:
                        norm_prep(2, k, ALL)

            out_product(U_OUT0, 1, ALL)
            mlp(0, U_MLP0, ALL)

            dve.wait_ge(rb_ready, 3)
            dve.wait_ge(lamv_in, 16)
            V.tensor_tensor(lamv[:, 0, :], lamv[:, 0, :], lamv[:, 1, :], ALU.mult)
            V.tensor_tensor(lamv[:, 2, :], lamv[:, 2, :], lamv[:, 3, :], ALU.mult).then_inc(lam_dve, 1)
            dve.wait_ge(lam_dve, 1)
            V.tensor_reduce(lam[:, 0:2], lamv[:, :, :].rearrange("p (a b) d -> p a b d", b=2)[:, :, 0, :], AX.X, ALU.add).then_inc(lam_dve, 1)
            dve.wait_ge(lam_act, 1)
            V.scalar_tensor_tensor(lam[:, 4:5], lam[:, 3:4], -LAMBDA_INIT, lam[:, 2:3], ALU.add, ALU.subtract).then_inc(lam_dve, 1)
            V.tensor_scalar(gains[:, 40:48], gains[:, 40:48], 1.0 - LAMBDA_INIT, None, ALU.mult).then_inc(lam_dve, 1)
            dve.wait_ge(lam_dve, 4)

            def maxima(n, i):
                for c in range(2):
                    dve.wait_ge(sc_done[c], n + 1)
                    w = NMETA + P * (i + 1)
                    if i < 3:
                        V.tensor_reduce(stat[:, i % 2, c:c + 1], ps[:, B_SC[c], 0:w], AX.X, ALU.max,
                                        negate=True).then_inc(max_done[c], 1)
                    else:
                        V.tensor_reduce(stat[:, i % 2, c:c + 1], ps[:, B_SC[c]:B_SC[c] + 2, 0:HALF], AX.XY, ALU.max,
                                        negate=True).then_inc(max_done[c], 1)

            def weights(hd, n, i):
                w = NMETA + P * (i + 1)
                dve.wait_ge(exp_done[0], n + 1)
                dve.wait_ge(exp_done[1], n + 1)
                V.reciprocal(stat[:, i % 2, 4:6], stat[:, i % 2, 2:4]).then_inc(rden_rd, 1)
                dve.wait_ge(rden_rd, n + 1)
                V.tensor_scalar(stat[:, i % 2, 6:7], stat[:, i % 2, 5:6], lam[:, 4:5], None, ALU.mult).then_inc(nlam_rd, 1)
                dve.wait_ge(nlam_rd, n + 1)
                e = es[0][i % 2], es[1][i % 2]
                V.tensor_scalar(e[1][:, 0:w], e[1][:, 0:w], stat[:, i % 2, 6:7], None, ALU.mult).then_inc(e1_rd, 1)
                dve.wait_ge(e1_rd, n + 1)
                wait(dve, at_t, n - 3)
                if i == 0:
                    wait(dve, meta_t, hd)
                V.scalar_tensor_tensor(attn[:, i, 0:w], e[0][:, 0:w], stat[:, i % 2, 4:5], e[1][:, 0:w],
                                       ALU.mult, ALU.add).then_inc(attn_rd, 1)

            def keys_lo(n1, par, c):
                dve.wait_ge(khi_done, n1 * 2 + (c + 1))
                for b in (0, 64):
                    last = V.tensor_tensor(kls[1 - par][c][b:b + 64, :], kf1[64 * c:64 * c + 64, :],
                                           khs[1 - par][c][0:64, :].bitcast(F32), ALU.subtract)
                last.then_inc(klo_done, 1)

            def step1(hd, par, pair):
                n1 = hd + 1
                if exists(hd):
                    maxima(hd * 4, 0)
                    weights(hd, hd * 4, 0)
                if exists(n1):
                    split(n1 * 3 + (U_IN1 + 2), 2)
                elif exists(hd):
                    split(U_OUT1 + 2, 2)
                if exists(hd):
                    maxima(hd * 4 + 1, 1)
                    weights(hd, hd * 4 + 1, 1)
                if exists(n1):
                    scaled(n1 * 3 + U_IN1, 0, SEQ, qf1[:, :], ps[:, B_Q1, :])
                    split(n1 * 3 + (U_IN1 + 3), 0)
                    dve.wait_ge(qhi_done, n1 + 1)
                    for c in range(2):
                        b0, b1 = 64 * c, 64 - 64 * c
                        last = V.scalar_tensor_tensor(qst[1 - par][c][b1:b1 + 64, :], qf1[b0:b0 + 64, NMETA:T], SCORE_SCALE,
                                                      qst[1 - par][c][b0:b0 + 64, :].bitcast(F32), ALU.mult, ALU.subtract)
                    last.then_inc(qlo_done, 1)
                elif exists(hd):
                    split(U_OUT1 + 3, 3)
                if exists(hd):
                    maxima(hd * 4 + 2, 2)
                    weights(hd, hd * 4 + 2, 2)
                if exists(n1):
                    scaled(n1 * 3 + (U_IN1 + 1), 0, ALL, kf1[:, :])
                if exists(hd):
                    maxima(hd * 4 + 3, 3)
                if exists(n1):
                    keys_lo(n1, par, 0)
                if exists(hd):
                    weights(hd, hd * 4 + 3, 3)
                if exists(n1):
                    keys_lo(n1, par, 1)
                if exists(hd - 1):
                    dve.wait_ge(rs_rd1, hd)
                    V.tensor_tensor(zf[:, :], zf[:, :], acc[:, NMETA:T], ALU.mult).then_inc(z_mul1, 1)
                if exists(n1):
                    wait(dve, v_t1, n1)
                    scaled(n1 * 3 + (U_IN1 + 2), 0, ALL, vf1[:, :])
                    split(n1 * 3 + (U_IN1 + 4), 1)
                if exists(hd - 1):
                    dve.wait_ge(zh_rd1, hd)
                    V.tensor_tensor(blk(al, hd - 1)[:, NMETA:T], zf[:, :], blk(ah, hd - 1)[:, NMETA:T].bitcast(F32),
                                    ALU.subtract).then_inc(z_ready, 1)

            heads_loop(dve, 1, step1)
            out_product(U_OUT1, 3, SEQ)
            mlp(1, U_MLP1, SEQ)

            dve.wait_ge(gfin_in, 16)
            for i in range(4):
                dve.wait_ge(frs, i + 1)
                V.scalar_tensor_tensor(fin[:, i, :].rearrange("p (b n) -> p b n", b=2), ps[:, 2 * i:2 * i + 2, :],
                                       lam[:, i:i + 1], gfin[:, :].rearrange("p (b n) -> p b n", b=2),
                                       ALU.mult, ALU.mult).then_inc(fmul, 1)

        @block.tensor
        def _(pe):
            mm = nc.tensor.matmul

            def blocks(u, slot, mh, ml, spans, bank, free, kb0=0, kb1=CB, block_wait=None):
                if kb0 == 0:
                    pe.wait_ge(split_lo, u + 1)
                    wait(pe, evac, free)
                for kb in range(kb0, kb1):
                    if block_wait is not None:
                        block_wait(kb)
                    for n, (w, m) in enumerate(((wh, mh), (wh, ml), (wl, mh))):
                        for s, (t0, w_) in enumerate(spans):
                            last = mm(ps[:, bank + s, 0:w_], w[:, slot, kb, :], m[:, kb, t0:t0 + w_],
                                      start=(kb == 0 and n == 0), stop=(kb == CB - 1 and n == 2))
                if kb1 == CB:
                    last.then_inc(unit_done, 1)

            def unit(u, k, mh, ml, spans, block_wait=None):
                if len(spans) == 2:
                    blocks(u, k % 4, mh, ml, spans, 2 * (k % 2), u - 1, block_wait=block_wait)
                else:
                    blocks(u, k % 4, mh, ml, spans, k % 4, u - 3, block_wait=block_wait)

            def mean_squares(n, spans):
                pe.wait_ge(acc_done, 8 * n + 8)
                for s, (t0, w) in enumerate(spans):
                    last = mm(ps[:, B_SUM + s, 0:w], ones[:, :], acc[:, t0:t0 + w], start=True, stop=True)
                last.then_inc(sum_done, 1)

            def turn_values(n, u, vf, tiles):
                pe.wait_ge(evac, u + 1)
                wait(pe, vt_rd, n)
                for s, (t0, w) in enumerate(tiles):
                    o = ps[:, B_TR, P * s:P * (s + 1)] if w == P else ps[0:w, B_TR + 1, 0:P]
                    last = nc.tensor.transpose(o, vf[:, n % 2, t0:t0 + w], ident[:, :])
                last.then_inc(v_t, 1)

            def y_block(n):
                return lambda kb: pe.wait_ge(y_ready, 8 * n + kb + 1)

            pe.wait_ge(ident_made, 1)
            pe.wait_ge(small_in, 6 * 16)
            nc.tensor.transpose(ps[:, 7, 0:48], gain_rows[:, :], ident[0:48, 0:48]).then_inc(gain_t, 1)
            pe.wait_ge(x_in, 2 * 16)
            for c in range(CB):
                wait(pe, hx_rd, c - 3)
                wait(pe, hm_rd, c - 1)
                for i in range(4):
                    nc.tensor.transpose(ps[:, c % 4, P * i:P * (i + 1)], xin[:, i, P * c:P * (c + 1)], ident[:, :])
                nc.tensor.transpose(ps[:, 4 + c % 2, 0:NMETA], meta_in[:, P * c:P * (c + 1)],
                                    ident[0:NMETA, 0:NMETA]).then_inc(x_t, 1)
            pe.wait_ge(gw_ready, 1)
            pe.wait_ge(hm_rd, CB)
            for kb in range(CB):
                pe.wait_ge(y_ready, kb + 1)
                for n, (w, m) in enumerate(((gwh, yh), (gwh, yl), (gwl, yh))):
                    for s, (t0, w_) in enumerate(ALL):
                        last = mm(ps[0:40, 4 + s, 0:w_], w[:, kb, :], m[:, kb, t0:t0 + w_],
                                  start=(kb == 0 and n == 0), stop=(kb == CB - 1 and n == 2))
            last.then_inc(gate_mm, 1)
            pe.wait_ge(gain_rd, 1)
            mean_squares(0, ALL)

            pe.wait_ge(hx_rd, CB)
            for k in range(4):
                unit(k, k, yh, yl, ALL)
            for k in range(4, 8):
                unit(k, k, yh, yl, ALL)
            pe.wait_ge(gate_dve, 7)
            pe.wait_ge(rb_ready, 1)
            for s, (t0, w) in enumerate(TILES0):
                last = nc.tensor.transpose(ps[0:w, B_SUM, 8 * s:8 * s + 8], gu[:, t0:t0 + w], ident[0:HEADS, 0:HEADS])
            last.then_inc(u_t, 1)
            for k in range(8):
                unit(8 + k, k, yh, yl, ALL)
                if k >= 1:
                    turn_values(k - 1, 8 + k - 1, vf0, TILES0)
            unit(16, 0, yh, yl, ALL)
            turn_values(7, 15, vf0, TILES0)
            for k in range(1, 4):
                unit(16 + k, k, yh, yl, ALL)
            with pe.Fori(5, 6) as i:
                for k in range(4):
                    unit(i * 4 + k, k, yh, yl, ALL)

            def step0(hd, par, pair):
                if exists(hd + 1):
                    pe.wait_ge(stack_lo, hd + 2)
                    wait(pe, p_ready, hd + 1)
                    if isinstance(hd, int) and hd < 0:
                        pe.wait_ge(evac, U_OUT0)
                    o = 1 - par
                    for n, (j, t0, t1, b, c) in enumerate(PIECES):
                        s0, rows = TILES0[j]
                        for m, q in enumerate((qhs[o], qls[o])):
                            last = mm(ps[0:rows, b, c:c + t1 - t0], ks[o][:, s0:s0 + rows], q[:, t0:t1],
                                      start=(m == 0), stop=(m == 1))
                    last.then_inc(s_done, 1)
                if exists(hd - 1):
                    pe.wait_ge(num_rd, hd)
                    pe.wait_ge(den_sq, hd)
                    mm(ps[:, B_DEN, 0:QSPLIT], head_mean[:, :], abuf[:, 0:QSPLIT], start=True, stop=True)
                    mm(ps[:, B_DEN + 1, 0:T - QSPLIT], head_mean[:, :], abuf[:, QSPLIT:T],
                       start=True, stop=True).then_inc(ssq_done, 1)
                if exists(hd):
                    pe.wait_ge(p_ready, hd + 1)
                    pe.wait_ge(vth_rd, hd + 1)
                    wait(pe, num_rd, hd)
                    for what, bank, done in ((vth0[par], B_NUM, pv_done), (None, B_DEN, den_done)):
                        if what is None:
                            wait(pe, t_rd, hd)
                        seen = set()
                        for n, (j, t0, t1, _, _) in enumerate(PIECES):
                            rows = TILES0[j][1]
                            b, c = (bank, t0) if t1 <= QSPLIT else (bank + 1, t0 - QSPLIT)
                            lhs = ones[0:rows, :] if what is None else what[0:rows, j, :]
                            last = mm(ps[:, b, c:c + t1 - t0], lhs, dmat[par][0:rows, DCOL[n]:DCOL[n + 1]],
                                      start=(b not in seen), stop=(n in (1, len(PIECES) - 1)))
                            seen.add(b)
                        last.then_inc(done, 1)

            heads_loop(pe, 2, step0)

            def z_block(layer):
                return lambda kb: pe.wait_ge(z_ready, HEADS * layer + kb + 1)

            def mlp(layer, base, spans):
                g0 = 4 * layer

                def group(u0, g, first=False):
                    for k in range(8):
                        unit(u0 + k, k, yh, yl, spans, y_block(2 * layer + 1) if first and k == 0 else None)
                        if first and k == 0:
                            mean_squares(2 * layer + 1, spans)
                    for k in range(8):
                        unit(u0 + (8 + k), k, ah, al, spans,
                             (lambda kb: pe.wait_ge(a_ready, g * 8 + (kb + 1))) if k == 0 else None)

                group(base, g0, True)
                with pe.Fori(1, GROUPS) as g:
                    group(g * 16 + base, g + g0)

            def out_product(base, layer, spans):
                for k in range(8):
                    unit(base + k, k, ah, al, spans, z_block(layer) if k == 0 else None)

            out_product(U_OUT0, 0, ALL)
            mlp(0, U_MLP0, ALL)

            def part(n1, j, kb0, kb1, block_wait=None):
                free = n1 * 3 + (U_IN1 + (-2, 0, 2)[j])
                if isinstance(n1, int):
                    free = max(free, U_IN1)
                blocks(n1 * 3 + (U_IN1 + j), j, yh, yl, SEQ if j == 0 else ALL, B_Q1 if j == 0 else 0,
                       free, kb0, kb1, block_wait)

            def scores(n, i, par):
                w = NMETA + P * (i + 1)
                cuts = [(0, w)] if i < 3 else ALL
                for c in range(2):
                    wait(pe, exp_done[c], n)
                    q = qst[par][c][:, P * i:P * (i + 1)]
                    for s, (t0, w_) in enumerate(cuts):
                        o = ps[:, B_SC[c] + s, 0:w_]
                        masked = s == len(cuts) - 1
                        mm(o, q, khs[par][c][:, t0:t0 + w_], start=True, stop=False)
                        last = mm(o, q, kls[par][c][:, t0:t0 + w_], start=False, stop=not masked)
                        if masked:
                            last = mm(o[:, w_ - 64:w_], neg_row[:, :], one_row[:, :], start=False, stop=True)
                    last.then_inc(sc_done[c], 1)

            def turn(n, i):
                pe.wait_ge(attn_rd, n + 1)
                wait(pe, at_rd, n)
                for s in range(i + 1):
                    last = nc.tensor.transpose(ps[:, B_TR1, P * s:P * (s + 1)],
                                               attn[:, i, NMETA + P * s:NMETA + P * (s + 1)], ident[:, :])
                last.then_inc(at_t, 1)

            def output(n, par):
                pe.wait_ge(meta_rd, n + 1)
                mm(ps[:, B_PV1, :], vth1[par][0:NMETA, 4, :], att_meta[:, :], start=True, stop=False)
                for s in range(4):
                    last = mm(ps[:, B_PV1, P * s:X], vth1[par][:, s, :], att[:, s, P * s:X], start=False, stop=(s == 3))
                last.then_inc(pv_done1, 1)

            def turn_meta(n):
                pe.wait_ge(vt_rd1, min(n + 2, HEADS) if isinstance(n, int) else n + 2)
                pe.wait_ge(at_rd, n * 4 + 4)
                for i in range(4):
                    last = nc.tensor.transpose(ps[0:NMETA, B_TR1, P * i:P * (i + 1)], attn[:, i, 0:NMETA], ident[:, :])
                last.then_inc(meta_t, 1)

            def squares(n):
                pe.wait_ge(pv_rd1, n + 1)
                mm(ps[:, B_PV1, :], head_mean[:, :], abuf[:, NMETA:T], start=True, stop=True).then_inc(ssq_done1, 1)

            def out_part(k, kb0, kb1):
                if kb0 == 0 and k == 2:
                    pe.wait_ge(exp_done[0], 4 * HEADS)
                blocks(U_OUT1 + k, k, ah, al, SEQ, k, U_OUT1, kb0, kb1, z_block(1))

            def step1(hd, par, pair):
                n1, nxt = hd + 1, exists(hd + 1)
                last_head = isinstance(hd, int) and hd == HEADS - 1
                if exists(hd):
                    pe.wait_ge(qlo_done, n1)
                    pe.wait_ge(klo_done, n1 * 2)
                    scores(hd * 4, 0, par)
                if not exists(hd) and exists(hd - 1):
                    out_part(2, 0, 6)
                if exists(hd - 1):
                    turn(hd * 4 - 1, 3)
                if nxt:
                    if isinstance(hd, int) and hd < 0:
                        part(n1, 0, 0, CB, y_block(2))
                        mean_squares(2, ALL)
                    else:
                        part(n1, 0, 0, 2)
                elif last_head:
                    out_part(0, 0, 3)
                if exists(hd):
                    pe.wait_ge(evac, hd * 3 + (U_IN1 + 3))
                    wait(pe, at_rd, hd * 4)
                    wait(pe, hln_done1, hd - 1)
                    for s, (t0, w) in enumerate(TILES1):
                        o = ps[:, B_TR1, P * s:P * (s + 1)] if w == P else ps[0:w, B_PV1, 0:P]
                        last = nc.tensor.transpose(o, vf1[:, t0:t0 + w], ident[:, :])
                    last.then_inc(v_t1, 1)
                    if nxt:
                        part(n1, 0, 2, 5)
                    elif last_head:
                        out_part(0, 3, 5)
                if exists(hd - 1):
                    turn_meta(hd - 1)
                    if not exists(hd):
                        out_part(3, 0, 3)
                if exists(hd):
                    if nxt:
                        part(n1, 0, 5, 6)
                    scores(hd * 4 + 1, 1, par)
                if exists(hd - 1):
                    output(hd - 1, 1 - par)
                if exists(hd):
                    if nxt:
                        part(n1, 0, 6, CB)
                    elif last_head:
                        out_part(0, 5, 6)
                        out_part(1, 0, 1)
                    wait(pe, meta_rd, hd)
                    wait(pe, vt_rd1, hd + 1)
                    turn(hd * 4, 0)
                if nxt:
                    part(n1, 1, 0, 3)
                elif last_head:
                    out_part(1, 1, 3)
                if exists(hd):
                    scores(hd * 4 + 2, 2, par)
                    turn(hd * 4 + 1, 1)
                if nxt:
                    part(n1, 1, 3, CB)
                elif last_head:
                    out_part(1, 3, 5)
                if exists(hd - 1):
                    if not exists(hd):
                        out_part(3, 3, 6)
                    squares(hd - 1)
                if exists(hd):
                    if nxt:
                        pe.wait_ge(evac, n1 * 3 + (U_IN1 + 1))
                    scores(hd * 4 + 3, 3, par)
                    turn(hd * 4 + 2, 2)
                if nxt:
                    part(n1, 2, 0, CB)
                elif last_head:
                    out_part(1, 5, 6)

            heads_loop(pe, 1, step1)
            for k in range(2):
                out_part(k, 6, 7)
            for k in range(4):
                out_part(k, 7 if k < 2 else 6, CB)
            for k in range(4, 8):
                unit(U_OUT1 + k, k, ah, al, SEQ)
            mlp(1, U_MLP1, SEQ)

            pe.wait_ge(evac, U_END)
            for i in range(4):
                for c in range(CB):
                    last = nc.tensor.transpose(ps[:, 2 * i + c // 4, P * (c % 4):P * (c % 4 + 1)],
                                               h[:, c, NMETA + P * i:NMETA + P * (i + 1)], ident[:, :])
                last.then_inc(out_t, 1)


_INS = ["x", "meta_tokens", "norm_gains", "mlstm_w_in", "mlstm_b_gate", "mlstm_head_gain", "mlstm_w_out",
        "diff_w_in", "diff_lambda", "diff_head_gain", "diff_w_out", "mlp_w_up", "mlp_w_down", "final_gain"]
_OUTS = [((1, X, D), "float32")]


def kernel(**inputs):
    import numpy as _np
    import concourse.bacc as _bacc
    from concourse import mybir as _mybir
    from concourse.bass_utils import run_bass_kernel_spmd as _run

    nc = _bacc.Bacc("TRN2", target_bir_lowering=False, num_devices=1)
    arrays, args = {}, {}
    for name in _INS:
        arr = _np.ascontiguousarray(inputs[name])
        arrays[f"in_{name}_dram"] = arr
        args[name] = nc.dram_tensor(f"in_{name}_dram", arr.shape, _mybir.dt.from_np(arr.dtype), kind="ExternalInput").ap()
    shape, dtype = _OUTS[0]
    out = nc.dram_tensor("out_0_dram", shape, _mybir.dt.from_np(_np.dtype(dtype)), kind="ExternalOutput").ap()
    program(nc, args, out)
    r = _run(nc, [arrays], core_ids=[0])
    return r.results[0]["out_0_dram"]
```

```python
from contextlib import ExitStack
import math

import concourse.bass as bass
from concourse import mybir

ALU = mybir.AluOpType
ACT = mybir.ActivationFunctionType
AX = mybir.AxisListType
F32 = mybir.dt.float32
F32R = mybir.dt.float32r
BF16 = mybir.dt.bfloat16
ds = bass.ds

P = 128
D = 1024
NMETA = 16
X = 512
T = NMETA + X
HALF = T // 2
CB = D // P
FF = 4096
GROUPS = FF // D
HEADS = 8
DQK = 64
GATE_COL = 3072
FG_ROW = 32
EPS = 1e-6
SUBLN_EPS = 1e-5
LAMBDA_INIT = 0.8 - 0.6 * math.exp(-0.3)
NEG = -1e30
SCORE_SCALE = DQK ** -0.5
NM_MAX = 28.0

RING = 4
RAW = 2
AHEAD = 2
MISSED = [(7, 6), (14, 12)]
CAME = [(0, 0, 0), (9, 9, 8)]

U_IN0, U_OUT0, U_MLP0 = 0, 24, 32
U_IN1, U_OUT1, U_MLP1 = 96, 120, 128
U_END = 192

ALL = [(0, HALF), (HALF, HALF)]
SEQ = [(NMETA, X)]

B_SUM = 6
B_S0, B_ND = 2, 6

QSPLIT = 256
PIECES = [(0, 0, 256, B_S0, 0), (1, 128, 256, B_S0, 256),
          (0, 256, 528, B_S0 + 1, 0), (3, 384, 528, B_S0 + 1, 272),
          (1, 256, 528, B_S0 + 2, 0),
          (2, 256, 528, B_S0 + 3, 0), (4, 512, 528, B_S0 + 3, 272)]
DCOL = [sum(q[2] - q[1] for q in PIECES[:n]) for n in range(len(PIECES) + 1)]
DW = DCOL[-1]
D_FULL = DCOL[-2]
P_BANKS = [(B_S0, 384, 0), (B_S0 + 1, 416, 384), (B_S0 + 2, 272, 800), (B_S0 + 3, 272, 1072)]
DIAG = [(DCOL[0], 128), (DCOL[1], 128), (DCOL[5], 128), (DCOL[3], 128), (DCOL[6], 16)]

B_SC, B_TR1, B_PV1 = (2, 4), 6, 7
B_Q1 = 3
TILES0 = [(0, 128), (128, 128), (256, 128), (384, 128), (512, 16)]
TILES1 = [(16, 128), (144, 128), (272, 128), (400, 128), (0, 16)]


def wait(eng, sem, value):
    if not isinstance(value, int) or value > 0:
        eng.wait_ge(sem, value)


def heads_loop(eng, lead, step, tail=1):
    pairs = (HEADS - 1 - lead) // 2
    for h in range(-lead, 1):
        step(h, h % 2, h // 2)
    with eng.Fori(0, pairs) as i:
        step(i * 2 + 1, 1, i)
        step(i * 2 + 2, 0, i + 1)
    for h in range(2 * pairs + 1, HEADS + tail):
        step(h, h % 2, h // 2)


def exists(h):
    return not isinstance(h, int) or 0 <= h < HEADS


def program(nc, a, out):
    with ExitStack() as ctx:
        cursor = [(nc.sbuf_base + 63) // 64 * 64]
        limit = nc.sbuf_usable_end

        def place(name, shape, dt, where, end):
            size = 2 if dt == BF16 else 4
            for n in shape[1:]:
                size *= n
            size = (size + 31) // 32 * 32
            assert where[0] + size <= end, (name, where[0] + size - end)
            t = nc.alloc_sbuf_tensor_at(name, shape, dt, offset=where[0])
            where[0] += size
            return t

        def new(name, shape, dt=F32):
            return place(name, shape, dt, cursor, limit)

        h = new("h", [P, CB, T])
        y_at = cursor[0]
        yh = new("yh", [P, CB, T], F32R)
        yl = new("yl", [P, CB, T], F32R)
        y_end = a_at = cursor[0]
        ah = new("ah", [P, CB, T], F32R)
        al = new("al", [P, CB, T], F32R)
        a_end = cursor[0]
        wh = new("wh", [P, RING, CB, P], F32R)
        wl = new("wl", [P, RING, CB, P], F32R)
        raw = new("raw", [P, RAW, CB, 2 * P])
        tbuf = new("tbuf", [P, T])
        abuf = new("abuf", [P, T])
        acc = new("acc", [P, T])
        rb = new("rb", [P, T])
        ident = new("ident", [P, P])
        ones = new("ones", [P, P])
        causal = new("causal", [P, P])
        head_mean = new("head_mean", [P, P])
        gains = new("gains", [P, 48])
        gain_rows = new("gain_rows", [48, P])
        eps_d = new("eps_d", [P, 1])
        eps_s = new("eps_s", [P, 1])
        bias_i = new("bias_i", [HEADS, 1])
        bias_f = new("bias_f", [64, 1])
        stat = new("stat", [P, 2, 8])
        lam = new("lam", [P, 8])
        ucol = new("ucol", [P, 5, HEADS])
        neg_row = new("neg_row", [1, P], BF16)
        one_row = new("one_row", [1, 64], BF16)
        lamv = new("lamv", [P, 4, DQK])
        arena = cursor[0]

        w0 = [arena]
        xin = place("xin", [P, 4, D], F32, w0, limit)
        meta_in = place("meta_in", [NMETA, D], F32, w0, limit)
        w0 = [arena]
        qkf, vf0, nf = (place(n, [P, T], F32, w0, limit) for n in ("qkf", "vf0", "nf"))
        ks, qhs, qls, vth0, of, mbc, nmbc, dmat = (
            [place(f"{name}{par}", shape, dt, w0, limit) for par in range(2)]
            for name, shape, dt in (("ks", [P, T], F32R), ("qhs", [P, T], F32R), ("qls", [P, T], F32R),
                                    ("vth0_", [P, 5, P], F32), ("of", [P, T], F32), ("mbc", [P, T], F32),
                                    ("nmbc", [P, T], F32), ("dmat", [P, DW], F32)))
        w0 = [a_at]
        gx, gabs, gexp, gln, glf, gone = (place(n, [64, T], F32, w0, a_end)
                                          for n in ("gx", "gabs", "gexp", "gln", "glf", "gone"))
        gi, gb, gu, gm, gnm = (place(n, [HEADS, T], F32, w0, a_end) for n in ("gi", "gb", "gu", "gm", "gnm"))
        graw = place("graw", [P, CB, 16], F32, w0, a_end)
        gwh = place("gwh", [P, CB, 40], F32R, w0, a_end)
        gwl = place("gwl", [P, CB, 40], F32R, w0, a_end)
        w0 = [arena]
        qf1 = place("qf1", [P, T], F32, w0, limit)
        kf1 = place("kf1", [P, T], F32, w0, limit)
        vf1 = place("vf1", [P, T], F32, w0, limit)
        qst = [[place(f"qst{par}{c}", [P, X], F32R, w0, limit) for c in range(2)] for par in range(2)]
        khs = [[place(f"khs{par}{c}", [P, T], F32R, w0, limit) for c in range(2)] for par in range(2)]
        kls = [[place(f"kls{par}{c}", [P, T], F32R, w0, limit) for c in range(2)] for par in range(2)]
        vth1 = [place(f"vth1{par}", [P, 5, P], F32, w0, limit) for par in range(2)]
        att = place("att", [P, 4, X], F32, w0, limit)
        att_meta = place("att_meta", [NMETA, X], F32, w0, limit)
        attn = place("attn", [P, 4, T], F32, w0, limit)
        es = [[place("e00", [P, T], F32, w0, limit), place("e01", [P, T], F32, w0, limit)],
              [tbuf, place("e11", [P, T], F32, w0, limit)]]
        zf = place("zf", [P, X], F32, w0, limit)
        w0 = [arena]
        fin = place("fin", [P, 4, D], F32, w0, limit)
        gfin = place("gfin", [P, D], F32, w0, limit)
        sqf = place("sqf", [P, D], F32, w0, limit)

        ps = ctx.enter_context(nc.psum_tensor("ps", [P, 8, 512], F32))
        gate_rows = nc.dram_tensor("gate_rows", [2 * HEADS, T], F32).ap()

        def sem(name):
            return ctx.enter_context(nc.semaphore(name))

        def sems(names):
            return [sem(n) for n in names.split()]

        raw_in = [sem(f"raw_in{i}") for i in range(RAW)]
        mrow_in = [sem(f"mrow_in{i}") for i in range(2)]
        nrow_in = [sem(f"nrow_in{i}") for i in range(2)]
        small_in, gains_in, meta_come, lamv_in, gfin_in, gate_sent, out_sent = sems("small_in gains_in meta_come lamv_in gfin_in gate_sent out_sent")
        ones_made, consts, ident_made, gain_t, gain_rd, gw_zero, gwh_done, gw_ready = sems(
            "ones_made consts ident_made gain_t gain_rd gw_zero gwh_done gw_ready")
        x_t, hx_rd, meta_t0, hm_rd = sems("x_t hx_rd meta_t0 hm_rd")
        split_hi, split_lo, unit_done, evac = sems("split_hi split_lo unit_done evac")
        h_ready, yh_done, y_ready, sq_done, acc_done, sum_done, ln_done, rb_ready = sems(
            "h_ready yh_done y_ready sq_done acc_done sum_done ln_done rb_ready")
        relu_done, sqa_done, ah_done, a_ready = sems("relu_done sqa_done ah_done a_ready")
        gate_mm, gate_dve, gate_act, u_t, ucol_rd = sems("gate_mm gate_dve gate_act u_t ucol_rd")
        stack_hi, stack_lo, v_t, vth_rd, dpre, dexp, dready, emn_done = sems(
            "stack_hi stack_lo v_t vth_rd dpre dexp dready emn_done")
        s_done, p_ready, pv_done, den_done, num_rd, den_sq, x_rd, ssq_done, t_rd = sems(
            "s_done p_ready pv_done den_done num_rd den_sq x_rd ssq_done t_rd")
        lsig, w_done, hln_done, e_done, rs_rd, z_mul, zh_rd, z_ready = sems(
            "lsig w_done hln_done e_done rs_rd z_mul zh_rd z_ready")
        x_in = [sem(f"x_in{i}") for i in range(4)]
        unit_in = [sem(f"unit_in{i}") for i in range(3)]
        half_in = sem("half_in")
        qhi_done, qlo_done, khi_done, klo_done, v_t1, vt_rd1, meta_t, meta_rd = sems(
            "qhi_done qlo_done khi_done klo_done v_t1 vt_rd1 meta_t meta_rd")
        pv_done1, pv_rd1, ssq_done1, hln_done1, rs_rd1, z_mul1, zh_rd1 = sems(
            "pv_done1 pv_rd1 ssq_done1 hln_done1 rs_rd1 z_mul1 zh_rd1")
        sc_done = [sem(f"sc_done{c}") for c in range(2)]
        max_done = [sem(f"max_done{c}") for c in range(2)]
        exp_done = [sem(f"exp_done{c}") for c in range(2)]
        rden_rd, nlam_rd, e1_rd, attn_rd, at_t, at_rd = sems("rden_rd nlam_rd e1_rd attn_rd at_t at_rd")
        lam_dve, lam_act = sems("lam_dve lam_act")
        out_t, fsq, fln, frs, fmul = sems("out_t fsq fln frs fmul")

        w_in0, w_in1 = a["mlstm_w_in"][0], a["diff_w_in"][0]
        w_out0, w_out1 = a["mlstm_w_out"][0], a["diff_w_out"][0]

        def columns(w, c0, n):
            return w.rearrange("(k p) m -> p k m", p=P)[:, :, ds(c0, n)]

        def halves(t):
            return t.rearrange("p (s n) -> p s n", s=2)

        def banks(u, spans):
            b = 2 * (u % 2)
            return ps[:, b:b + 2, 0:HALF] if len(spans) == 2 else ps[:, u % 4, 0:X]

        def tokens(t, spans):
            return halves(t) if len(spans) == 2 else t[:, NMETA:T]

        block = ctx.enter_context(nc.Block())

        @block.sync
        def _(sp):
            def load_x(j):
                sp.dma_start(xin[:, :, 256 * j:256 * j + 256],
                             a["x"][0].rearrange("(i p) d -> p i d", p=P)[:, :, 256 * j:256 * j + 256]).then_inc(x_in[j], 16)

            load_x(0)
            sp.dma_start(graw[:, :, :], columns(w_in0, GATE_COL, 16)).then_inc(small_in, 16)
            bg = a["mlstm_b_gate"].rearrange("l (g o) -> (l g) o", o=1)
            sp.dma_start(bias_i[:, :], bg[0:HEADS, :]).then_inc(small_in, 16)
            sp.dma_start(bias_f[FG_ROW:FG_ROW + HEADS, :], bg[HEADS:2 * HEADS, :]).then_inc(small_in, 16)
            load_x(1)

            def load(slot, src, split=None):
                if split is not None:
                    sp.wait_ge(split_lo, split)
                sp.dma_start(raw[:, slot, :, :], src).then_inc(raw_in[slot], 16)

            def load_unit(slot, src, split):
                sp.wait_ge(split_lo, split)
                sp.dma_start(raw[:, slot // 2, :, P * (slot % 2):P * (slot % 2) + P], src).then_inc(unit_in[slot], 16)

            def load_halves(w, c0, c1):
                sp.dma_start(raw[:, 0, :, 0:DQK], columns(w, c0, DQK)).then_inc(unit_in[0], 16)
                sp.dma_start(raw[:, 0, :, DQK:P], columns(w, c1, DQK)).then_inc(half_in, 16)

            def head0(h, split):
                for j in range(3):
                    if split is not None:
                        sp.wait_ge(split_lo, split + j)
                    elif j > 0:
                        load_x(j + 1)
                    if j == 0:
                        load_halves(w_in0, h * DQK, h * DQK + D // 2)
                    else:
                        sp.dma_start(raw[:, j // 2, :, P * (j % 2):P * (j % 2) + P],
                                     columns(w_in0, h * P + D * j, P)).then_inc(unit_in[j], 16)

            def out_weights(w, base):
                if base == U_OUT0:
                    sp.wait_ge(split_lo, base - 2)
                    load_halves(w, 0, DQK)
                else:
                    load_unit(0, columns(w, 0, P), base - 2)
                load_unit(1, columns(w, P, P), base - 1)
                load(1, columns(w, 256, 256), base)
                for j in range(2):
                    load(j, columns(w, 512 + 256 * j, 256), base + 4 + 2 * j - 2)

            def mlp(layer, base):
                up = a["mlp_w_up"][layer]
                down = a["mlp_w_down"][layer].rearrange("(g k p) m -> g p k m", k=CB, p=P)
                with sp.Fori(0, GROUPS) as g:
                    for j in range(4):
                        load(j % 2, columns(up, g * D + 256 * j, 256), g * 16 + (base + 2 * j - 2))
                    for j in range(4):
                        src = down[ds(g, 1), :, :, 256 * j:256 * j + 256].rearrange("g p k m -> p (g k) m")
                        load(j % 2, src, g * 16 + (base + 8 + 2 * j - 2))

            head0(0, None)
            with sp.Fori(1, HEADS) as i:
                head0(i, i * 3 - 2)
            out_weights(w_out0, U_OUT0)
            mlp(0, U_MLP0)
            with sp.Fori(0, HEADS) as i:
                for j in range(3):
                    load_unit(j, columns(w_in1, i * P + D * j, P), i * 3 + (U_IN1 + j - 2))
            out_weights(w_out1, U_OUT1)
            mlp(1, U_MLP1)

            for i in range(4):
                sp.wait_ge(fmul, i + 1)
                sp.dma_start(out[0, P * i:P * (i + 1), :], fin[:, i, :]).then_inc(out_sent, 16)
            sp.wait_ge(out_sent, 4 * 16)

        @block.gpsimd
        def _(pool):
            nc.gpsimd.memset(ones[:, :], 1.0).then_inc(ones_made, 1)
            pool.wait_ge(ones_made, 1)
            nc.gpsimd.affine_select(out=ident[:, :], in_=ones[:, :], compare_op=ALU.is_equal, fill=0.0, base=0,
                                    pattern=[[-1, P]], channel_multiplier=1).then_inc(ident_made, 1)
            nc.gpsimd.memset(gwh[:, :, :].bitcast(F32), 0.0).then_inc(gw_zero, 1)
            nc.gpsimd.memset(gwl[:, :, :].bitcast(F32), 0.0).then_inc(gw_zero, 1)
            nc.gpsimd.memset(eps_d[:, :], EPS).then_inc(consts, 1)
            nc.gpsimd.memset(eps_s[:, :], SUBLN_EPS).then_inc(consts, 1)
            nc.gpsimd.memset(head_mean[:, :], 1.0 / P).then_inc(consts, 1)
            nc.gpsimd.memset(one_row[:, :], 1.0).then_inc(consts, 1)
            nc.gpsimd.memset(neg_row[:, 0:64], NEG).then_inc(consts, 1)
            nc.gpsimd.memset(neg_row[:, 64:P], 0.0).then_inc(consts, 1)
            nc.gpsimd.affine_select(out=causal[:, :], in_=ones[:, :], compare_op=ALU.is_ge, fill=0.0, base=0,
                                    pattern=[[1, P]], channel_multiplier=-1).then_inc(consts, 1)
            for c in range(1, CB):
                pool.wait_ge(sq_done, c + 1)
                wait(pool, acc_done, c if c > 1 else 0)
                nc.gpsimd.tensor_tensor(acc[:, :], abuf[:, :] if c == 1 else acc[:, :], (abuf, tbuf)[c % 2][:, :],
                                        ALU.add).then_inc(acc_done, 2 if c == 1 else 1)
            nc.gpsimd.memset(gone[:, :], 1.0).then_inc(consts, 1)
            pool.dma_start(lamv[:, :, :], a["diff_lambda"][0:1].broadcast_to([P, 4, DQK])).then_inc(lamv_in, 16)
            pool.wait_ge(consts, 8)

            pool.wait_ge(gate_dve, 10)
            pool.dma_start(gate_rows[0:HEADS, :], gm[:, :]).then_inc(gate_sent, 16)
            pool.dma_start(gate_rows[HEADS:2 * HEADS, :], gnm[:, :]).then_inc(gate_sent, 16)
            pool.wait_ge(gate_sent, 32)

            def step0(hd, par, pair):
                n1 = hd + 1
                if not exists(n1):
                    return
                wait(pool, dpre, hd)
                pool.dma_start(mbc[1 - par][:, :], gate_rows[ds(n1, 1), :].broadcast_to([P, T])).then_inc(mrow_in[1 - par], 16)
                wait(pool, x_rd, hd)
                pool.dma_start(nmbc[1 - par][:, :],
                               gate_rows[ds(n1 + HEADS, 1), :].broadcast_to([P, T])).then_inc(nrow_in[1 - par], 16)
                pool.wait_ge(dexp, n1 + 1)
                for c0, w in DIAG:
                    blk = dmat[1 - par][0:w, c0:c0 + w]
                    last = nc.gpsimd.tensor_tensor(blk, blk, causal[0:w, 0:w], ALU.mult)
                last.then_inc(dready, 1)

            heads_loop(pool, 1, step0, tail=0)

            pool.wait_ge(z_ready, 2 * HEADS)
            pool.dma_start(gfin[:, :], a["final_gain"].rearrange("(o d) -> o d", o=1).broadcast_to([P, D])).then_inc(gfin_in, 16)

        @block.scalar
        def _(act):
            def copy(o, i, scale=1.0):
                return nc.scalar.activation(o, i, ACT.Copy, scale=scale)

            def split(u, k, layer):
                if isinstance(u, int) and u >= U_END:
                    return
                if k % 2 == 0:
                    missed = 16 * MISSED[layer][k // 2]
                    act.wait_ge(raw_in[k // 2], (u - k) * 4 + (16 - missed))
                wait(act, unit_done, u - RING + 1)
                copy(wh[:, k, :, :], raw[:, k // 2, :, P * (k % 2):P * (k % 2) + P]).then_inc(split_hi, 1)

            def split_unit(u, j, layer, head):
                act.wait_ge(unit_in[j], head * 16 + (CAME[layer][j] + 1) * 16)
                if layer == 0 and j == 0:
                    act.wait_ge(half_in, head * 16 + 16)
                wait(act, unit_done, u - 2)
                copy(wh[:, j, :, :], raw[:, j // 2, :, P * (j % 2):P * (j % 2) + P]).then_inc(split_hi, 1)

            def norm_prep(n, b, spans):
                t0 = spans[0][0]
                copy(yh[:, b, t0:T], h[:, b, t0:T], gains[:, 8 * n + b:8 * n + b + 1]).then_inc(yh_done, 1)
                wait(act, acc_done, 8 * n + b if n > 0 else b - 1)
                sq = tbuf if n == 0 and b % 2 else abuf
                nc.scalar.activation(sq[:, t0:T], h[:, b, t0:T], ACT.Square).then_inc(sq_done, 1)

            def norm_factor(n, spans, bank=B_SUM):
                act.wait_ge(sum_done, n + 1)
                src = ps[:, bank:bank + 2, 0:HALF] if len(spans) == 2 else ps[:, bank, 0:X]
                nc.scalar.activation(tokens(rb[:, :], spans), src, ACT.Ln, bias=eps_d[:, 0:1], scale=1.0 / D).then_inc(ln_done, 1)
                act.wait_ge(ln_done, n + 1)
                nc.scalar.activation(tokens(rb[:, :], spans), tokens(rb[:, :], spans), ACT.Exp, scale=-0.5).then_inc(rb_ready, 1)

            nc.scalar.preload_act_table_set("natural_log_exp_and_others")
            act.dma_start(gain_rows[0:32, :], a["norm_gains"].rearrange("l n (c p) -> (l n c) p", p=P)).then_inc(gains_in, 16)
            act.dma_start(gain_rows[32:40, :], a["mlstm_head_gain"].rearrange("l (c p) -> (l c) p", p=P)).then_inc(gains_in, 16)
            act.dma_start(gain_rows[40:48, :], a["diff_head_gain"].rearrange("l (c p) -> (l c) p", p=P)).then_inc(gains_in, 16)
            act.dma_start(meta_in[:, :], a["meta_tokens"]).then_inc(meta_come, 16)
            act.wait_ge(meta_t0, 1)
            copy(h[:, :, 0:NMETA], ps[:, 7, 0:P].rearrange("p (c t) -> p c t", t=NMETA)).then_inc(hm_rd, 1)
            act.wait_ge(hm_rd, 1)
            act.wait_ge(gain_rd, 1)
            for c in range(CB):
                act.wait_ge(hx_rd, c + 1)
                norm_prep(0, c, ALL)
                if c in (0, 2):
                    split_unit(c // 2, c // 2, 0, 0)
            norm_factor(0, ALL, 4)
            split_unit(2, 2, 0, 0)
            fg = slice(FG_ROW, FG_ROW + HEADS)
            act.wait_ge(gate_dve, 4)
            nc.scalar.activation(gabs[fg, :], gx[fg, :], ACT.Abs).then_inc(gate_act, 1)
            act.wait_ge(gate_act, 1)
            nc.scalar.activation(gexp[fg, :], gabs[fg, :], ACT.Exp, scale=-1.0).then_inc(gate_act, 1)
            act.wait_ge(gate_act, 2)
            nc.scalar.activation(gln[fg, :], gexp[fg, :], ACT.Ln, bias=1.0).then_inc(gate_act, 1)

            def decays(n1, par):
                act.wait_ge(dpre, n1 + 1)
                d = dmat[1 - par]
                nc.scalar.activation(d[:, 0:D_FULL], d[:, 0:D_FULL], ACT.Exp, scale=-1.0)
                nc.scalar.activation(d[0:16, D_FULL:DW], d[0:16, D_FULL:DW], ACT.Exp, scale=-1.0).then_inc(dexp, 1)

            def step0(hd, par, pair):
                n1, nxt = hd + 1, exists(hd + 1)
                first = isinstance(hd, int) and hd < 0
                if exists(hd):
                    act.wait_ge(evac, hd * 3 + 3)
                    wait(act, w_done, hd)
                    nc.scalar.activation(tbuf[:, :], of[par][:, :], ACT.Abs).then_inc(lsig, 1)
                    act.wait_ge(lsig, hd * 3 + 1)
                    nc.scalar.activation(tbuf[:, :], tbuf[:, :], ACT.Exp, scale=-1.0).then_inc(lsig, 1)
                    act.wait_ge(lsig, hd * 3 + 2)
                    nc.scalar.activation(tbuf[:, :], tbuf[:, :], ACT.Ln, bias=1.0).then_inc(lsig, 1)
                if nxt:
                    if not first:
                        decays(n1, par)
                        split_unit(n1 * 3 + 2, 2, 0, n1)
                    act.wait_ge(evac, n1 * 3 + 1)
                    wait(act, s_done, hd)
                    copy(ks[1 - par][0:64, :], qkf[64:128, :])
                    copy(qhs[1 - par][0:64, :], qkf[0:64, :])
                    copy(qhs[1 - par][64:128, :], qkf[0:64, :]).then_inc(stack_hi, 1)
                    split_unit(n1 * 3 + 3, 0, 0, n1 + 1)
                elif exists(hd):
                    act.wait_ge(unit_done, U_OUT0)
                    split(U_OUT0 + 2, 2, 0)
                    split(U_OUT0 + 3, 3, 0)
                if exists(hd):
                    act.wait_ge(pv_done, hd + 1)
                    wait(act, z_ready, hd)
                    wait(act, ssq_done, hd)
                    for b, t0, t1 in ((B_ND, 0, QSPLIT), (B_ND + 1, QSPLIT, T)):
                        copy(nf[:, t0:t1], ps[:, b, 0:t1 - t0], gains[:, ds(hd + 32, 1)])
                        last = nc.scalar.activation(abuf[:, t0:t1], ps[:, b, 0:t1 - t0], ACT.Square)
                    last.then_inc(num_rd, 1)
                if nxt:
                    act.wait_ge(nrow_in[1 - par], pair * 16 + 16 * (par + 1))
                    nc.scalar.activation(nmbc[1 - par][:, :], nmbc[1 - par][:, :], ACT.Exp, scale=2.0).then_inc(emn_done, 1)
                    split_unit(n1 * 3 + 4, 1, 0, n1 + 1)
                if exists(hd):
                    act.wait_ge(den_done, hd + 1)
                    nc.scalar.activation(acc[:, 0:QSPLIT], ps[:, B_ND, 0:QSPLIT], ACT.Square)
                    nc.scalar.activation(acc[:, QSPLIT:T], ps[:, B_ND + 1, 0:T - QSPLIT], ACT.Square).then_inc(den_sq, 1)
                    act.wait_ge(t_rd, hd + 1)
                    nc.scalar.activation(acc[:, :], acc[:, :], ACT.Ln).then_inc(hln_done, 1)
                    act.wait_ge(e_done, hd + 1)
                    nc.scalar.activation(acc[:, :], acc[:, :], ACT.Exp).then_inc(rs_rd, 1)
                if first:
                    act.wait_ge(u_t, 1)
                    copy(ucol[:, 0:4, :], ps[:, B_SUM, 0:32].rearrange("p (s g) -> p s g", s=4))
                    copy(ucol[0:16, 4, :], ps[0:16, B_SUM, 32:40]).then_inc(ucol_rd, 1)
                    decays(0, 1)
                if nxt:
                    act.wait_ge(v_t, n1 + 1)
                    wait(act, pv_done, hd)
                    copy(vth0[1 - par][:, 0:4, :], ps[:, B_ND, :].rearrange("p (s e) -> p s e", e=P))
                    copy(vth0[1 - par][0:16, 4, :], ps[0:16, B_ND + 1, 0:P]).then_inc(vth_rd, 1)
                if exists(hd):
                    act.wait_ge(z_mul, hd + 1)
                    copy(ah[:, ds(hd, 1), :].rearrange("p o t -> p (o t)"), nf[:, :]).then_inc(zh_rd, 1)

            heads_loop(act, 1, step0, tail=0)

            def out_product(layer, base, n, spans):
                for k in range(8):
                    if k < 6:
                        split(base + k + 4, k % 4, layer)
                    act.wait_ge(h_ready, base_h(n) + k + 1)
                    norm_prep(n, k, spans)

            def base_h(n):
                return 8 * (n - 1)

            def up_units(layer, base, g_all, spans, factor=None):
                t0 = spans[0][0]
                for k in range(8):
                    split(base + (k + AHEAD), (k + AHEAD) % 4, layer)
                    if factor is not None and k == 0:
                        norm_factor(factor, spans)
                    act.wait_ge(relu_done, g_all * 8 + (k + 1))
                    nc.scalar.activation(abuf[:, t0:T], tbuf[:, t0:T], ACT.Square).then_inc(sqa_done, 1)
                    nc.scalar.activation(ah[:, k, t0:T], tbuf[:, t0:T], ACT.Square).then_inc(ah_done, 1)

            def mlp(layer, base, spans):
                g0 = 4 * layer
                up_units(layer, base, g0, spans, factor=2 * layer + 1)
                for k in range(8):
                    split(base + 8 + k + AHEAD, (k + AHEAD) % 4, layer)
                with act.Fori(1, GROUPS - 1) as g:
                    up_units(layer, g * 16 + base, g + g0, spans)
                    for k in range(8):
                        split(g * 16 + (base + 8 + k + AHEAD), (k + AHEAD) % 4, layer)
                last = base + 16 * (GROUPS - 1)
                up_units(layer, last, g0 + GROUPS - 1, spans)
                for k in range(8):
                    if layer == 0 and k >= 8 - AHEAD:
                        split_unit(U_IN1 + k + AHEAD - 8, k + AHEAD - 8, 1, 0)
                    else:
                        split(last + 8 + k + AHEAD, (k + AHEAD) % 4, layer)
                    if layer == 0:
                        act.wait_ge(h_ready, base_h(2) + k + 1)
                        norm_prep(2, k, ALL)

            out_product(0, U_OUT0, 1, ALL)
            act.wait_ge(lam_dve, 2)
            nc.scalar.activation(lam[:, 2:4], lam[:, 0:2], ACT.Exp).then_inc(lam_act, 1)
            mlp(0, U_MLP0, ALL)

            split_unit(U_IN1 + 2, 2, 1, 0)
            norm_factor(2, ALL)

            def scores(n, i, c):
                act.wait_ge(max_done[c], n + 1)
                if c == 0:
                    wait(act, attn_rd, n - 1)
                w = NMETA + P * (i + 1)
                b = B_SC[c]
                src = ps[:, b, 0:w] if i < 3 else ps[:, b:b + 2, 0:HALF]
                e = es[c][i % 2]
                dst = e[:, 0:w] if i < 3 else halves(e[:, :])
                nc.scalar.activation(dst, src, ACT.Exp, bias=stat[:, i % 2, c:c + 1],
                                     accum_out=stat[:, i % 2, 2 + c:3 + c]).then_inc(exp_done[c], 1)

            def turned(hd, n, i):
                act.wait_ge(at_t, n + 1)
                if i == 0:
                    wait(act, pv_done1, hd)
                copy(att[:, 0:i + 1, P * i:P * (i + 1)],
                     ps[:, B_TR1, 0:P * (i + 1)].rearrange("p (s t) -> p s t", t=P)).then_inc(at_rd, 1)

            def keys_hi(par, c):
                k = kf1[64 * c:64 * c + 64, :]
                copy(khs[1 - par][c][0:64, :], k)
                copy(khs[1 - par][c][64:128, :], k).then_inc(khi_done, 1)

            def step1(hd, par, pair):
                n1 = hd + 1
                if exists(hd - 1):
                    turned(hd - 1, hd * 4 - 1, 3)
                if exists(hd):
                    scores(hd * 4, 0, 0)
                    scores(hd * 4, 0, 1)
                if exists(hd):
                    act.wait_ge(v_t1, hd + 1)
                    copy(vth1[par][:, 0:4, :], ps[:, B_TR1, :].rearrange("p (s e) -> p s e", e=P))
                    copy(vth1[par][0:16, 4, :], ps[0:16, B_TR1 + 1, 0:P]).then_inc(vt_rd1, 1)
                    if exists(n1):
                        split_unit(n1 * 3 + (U_IN1 + 2), 2, 1, n1)
                    else:
                        act.wait_ge(unit_done, U_OUT1)
                        split(U_OUT1 + 2, 2, 1)
                if exists(hd - 1):
                    act.wait_ge(meta_t, hd)
                    copy(att_meta[:, :], ps[0:NMETA, B_TR1, :]).then_inc(meta_rd, 1)
                if exists(hd):
                    for c in range(2):
                        scores(hd * 4 + 1, 1, c)
                if exists(hd - 1):
                    act.wait_ge(pv_done1, hd)
                    wait(act, z_ready, hd + (HEADS - 1))
                    copy(zf[:, :], ps[:, B_PV1, :], gains[:, ds(hd + 39, 1)])
                    nc.scalar.activation(abuf[:, NMETA:T], ps[:, B_PV1, :], ACT.Square).then_inc(pv_rd1, 1)
                if exists(hd):
                    turned(hd, hd * 4, 0)
                if exists(n1):
                    act.wait_ge(evac, n1 * 3 + (U_IN1 + 1))
                    wait(act, sc_done[1], hd * 4)
                    for c in range(2):
                        b0 = 64 * c
                        last = copy(qst[1 - par][c][b0:b0 + 64, :], qf1[b0:b0 + 64, NMETA:T], SCORE_SCALE)
                    last.then_inc(qhi_done, 1)
                    split_unit(n1 * 3 + (U_IN1 + 3), 0, 1, n1 + 1)
                elif exists(hd):
                    split(U_OUT1 + 3, 3, 1)
                if exists(hd):
                    for c in range(2):
                        scores(hd * 4 + 2, 2, c)
                    turned(hd, hd * 4 + 1, 1)
                if exists(n1):
                    act.wait_ge(evac, n1 * 3 + (U_IN1 + 2))
                    keys_hi(par, 0)
                if exists(hd):
                    for c in range(2):
                        scores(hd * 4 + 3, 3, c)
                if exists(n1):
                    keys_hi(par, 1)
                if exists(hd):
                    turned(hd, hd * 4 + 2, 2)
                if exists(hd - 1):
                    act.wait_ge(ssq_done1, hd)
                    nc.scalar.activation(acc[:, NMETA:T], ps[:, B_PV1, :], ACT.Ln, bias=eps_s[:, 0:1]).then_inc(hln_done1, 1)
                    act.wait_ge(hln_done1, hd)
                    nc.scalar.activation(acc[:, NMETA:T], acc[:, NMETA:T], ACT.Exp, scale=-0.5).then_inc(rs_rd1, 1)
                if exists(n1):
                    split_unit(n1 * 3 + (U_IN1 + 4), 1, 1, n1 + 1)
                if exists(hd - 1):
                    act.wait_ge(z_mul1, hd)
                    copy(ah[:, ds(hd - 1, 1), NMETA:T].rearrange("p o t -> p (o t)"), zf[:, :]).then_inc(zh_rd1, 1)

            heads_loop(act, 1, step1)
            out_product(1, U_OUT1, 3, SEQ)
            mlp(1, U_MLP1, SEQ)

            for i in range(4):
                act.wait_ge(out_t, i + 1)
                nc.scalar.activation(sqf[:, :].rearrange("p (b n) -> p b n", b=2), ps[:, 2 * i:2 * i + 2, :], ACT.Square,
                                     accum_out=lam[:, i:i + 1]).then_inc(fsq, 1)
                act.wait_ge(fsq, i + 1)
                nc.scalar.activation(lam[:, i:i + 1], lam[:, i:i + 1], ACT.Ln, bias=eps_d[:, 0:1], scale=1.0 / D).then_inc(fln, 1)
                act.wait_ge(fln, i + 1)
                nc.scalar.activation(lam[:, i:i + 1], lam[:, i:i + 1], ACT.Exp, scale=-0.5).then_inc(frs, 1)

        @block.vector
        def _(dve):
            V = nc.vector

            def split(u, k):
                if isinstance(u, int) and u >= U_END:
                    return
                dve.wait_ge(split_hi, u + 1)
                V.tensor_tensor(wl[:, k, :, :], raw[:, k // 2, :, P * (k % 2):P * (k % 2) + P],
                                wh[:, k, :, :].bitcast(F32), ALU.subtract).then_inc(split_lo, 1)

            def norm_prep(n, b, spans):
                t0 = spans[0][0]
                dve.wait_ge(yh_done, 8 * n + b + 1)
                V.scalar_tensor_tensor(yl[:, b, t0:T], h[:, b, t0:T], gains[:, 8 * n + b:8 * n + b + 1],
                                       yh[:, b, t0:T].bitcast(F32), ALU.mult, ALU.subtract).then_inc(y_ready, 1)
                dve.wait_ge(sq_done, 8 * n + b + 1)
                if b == 0:
                    V.tensor_copy(acc[:, t0:T], abuf[:, t0:T]).then_inc(acc_done, 1)
                else:
                    dve.wait_ge(acc_done, 8 * n + b)
                    V.tensor_tensor(acc[:, t0:T], acc[:, t0:T], abuf[:, t0:T], ALU.add).then_inc(acc_done, 1)

            def scaled(u, k, spans, dest, src=None):
                dve.wait_ge(unit_done, u + 1)
                V.tensor_tensor(tokens(dest, spans), src or banks(k, spans), tokens(rb[:, :], spans), ALU.mult).then_inc(evac, 1)

            dve.wait_ge(gain_t, 1)
            V.tensor_copy(gains[:, :], ps[:, 6, 0:48]).then_inc(gain_rd, 1)

            def x_out(c):
                dve.wait_ge(x_t, c + 1)
                V.tensor_copy(h[:, c, NMETA:T], ps[:, 4 + c % 2, :]).then_inc(hx_rd, 1)

            x_out(0)
            x_out(1)
            dve.wait_ge(small_in, 3 * 16)
            dve.wait_ge(gw_zero, 2)
            V.tensor_copy(gwh[:, :, 0:HEADS], graw[:, :, 0:HEADS])
            V.tensor_copy(gwh[:, :, FG_ROW:FG_ROW + HEADS], graw[:, :, HEADS:2 * HEADS]).then_inc(gwh_done, 1)
            dve.wait_ge(gwh_done, 1)
            V.tensor_tensor(gwl[:, :, 0:HEADS], graw[:, :, 0:HEADS], gwh[:, :, 0:HEADS].bitcast(F32), ALU.subtract)
            V.tensor_tensor(gwl[:, :, FG_ROW:FG_ROW + HEADS], graw[:, :, HEADS:2 * HEADS],
                            gwh[:, :, FG_ROW:FG_ROW + HEADS].bitcast(F32), ALU.subtract).then_inc(gw_ready, 1)
            for c in range(CB):
                dve.wait_ge(yh_done, c + 1)
                V.scalar_tensor_tensor(yl[:, c, :], h[:, c, :], gains[:, c:c + 1], yh[:, c, :].bitcast(F32),
                                       ALU.mult, ALU.subtract).then_inc(y_ready, 1)
                if c in (1, 3):
                    split(c // 2, c // 2)
                if c + 2 < CB:
                    x_out(c + 2)

            ig, fg = slice(0, HEADS), slice(FG_ROW, FG_ROW + HEADS)
            split(2, 2)
            dve.wait_ge(rb_ready, 1)
            dve.wait_ge(gate_mm, 1)
            V.tensor_tensor(halves(gi[:, :]), ps[ig, 6:8, 0:HALF], halves(rb[ig, :]), ALU.mult).then_inc(gate_dve, 1)
            V.tensor_tensor(halves(gx[fg, :]), ps[fg, 6:8, 0:HALF], halves(rb[fg, :]), ALU.mult).then_inc(gate_dve, 1)
            dve.wait_ge(gate_dve, 1)
            V.tensor_scalar(gi[:, :], gi[:, :], bias_i[:, 0:1], None, ALU.add).then_inc(gate_dve, 1)
            dve.wait_ge(gate_dve, 2)
            V.tensor_scalar(gx[fg, :], gx[fg, :], bias_f[fg, 0:1], None, ALU.add).then_inc(gate_dve, 1)
            dve.wait_ge(gate_act, 3)
            V.scalar_tensor_tensor(glf[ig, :], gx[fg, :], 0.0, gln[fg, :], ALU.min, ALU.subtract).then_inc(gate_dve, 1)
            dve.wait_ge(gate_dve, 5)
            dve.wait_ge(consts, 8)
            V.tensor_tensor_scan(gb[:, :], gone[ig, :], glf[ig, :], 0.0, ALU.mult, ALU.add).then_inc(gate_dve, 1)
            dve.wait_ge(gate_dve, 6)
            V.tensor_tensor(gu[:, :], gi[:, :], gb[:, :], ALU.subtract).then_inc(gate_dve, 1)
            dve.wait_ge(gate_dve, 7)
            V.tensor_tensor_scan(gm[:, :], gu[:, :], gu[:, :], 0.0, ALU.max, ALU.max).then_inc(gate_dve, 1)
            dve.wait_ge(gate_dve, 8)
            V.tensor_tensor(gnm[:, :], gb[:, :], gm[:, :], ALU.add).then_inc(gate_dve, 1)
            dve.wait_ge(gate_dve, 9)
            V.tensor_scalar(gnm[:, :], gnm[:, :], -1.0, NM_MAX, ALU.mult, ALU.min).then_inc(gate_dve, 1)

            def blk(t, j):
                return t[:, ds(j, 1), :].rearrange("p o t -> p (o t)")

            def exponents(n1, par, pair):
                wait(dve, den_done, n1 - 1)
                dve.wait_ge(mrow_in[1 - par], pair * 16 + 16 * (par + 1))
                for n, (j, t0, t1, _, _) in enumerate(PIECES):
                    rows = TILES0[j][1]
                    last = V.tensor_scalar(dmat[1 - par][0:rows, DCOL[n]:DCOL[n + 1]], mbc[1 - par][0:rows, t0:t1],
                                           ucol[0:rows, j, ds(n1, 1)], 0.0, ALU.subtract, ALU.max)
                last.then_inc(dpre, 1)

            def step0(hd, par, pair):
                n1, nxt = hd + 1, exists(hd + 1)
                first = isinstance(hd, int) and hd < 0
                if exists(hd):
                    if nxt:
                        exponents(n1, par, pair)
                    dve.wait_ge(s_done, hd + 1)
                    dve.wait_ge(dready, hd + 1)
                    dm = dmat[par]
                    for b, w, c0 in P_BANKS:
                        V.scalar_tensor_tensor(dm[:, c0:c0 + w], ps[:, b, 0:w], SCORE_SCALE, dm[:, c0:c0 + w],
                                               ALU.mult, ALU.mult)
                    V.scalar_tensor_tensor(dm[0:16, D_FULL:DW], ps[0:16, B_S0 + 3, 272:288], SCORE_SCALE,
                                           dm[0:16, D_FULL:DW], ALU.mult, ALU.mult).then_inc(p_ready, 1)
                    dve.wait_ge(lsig, hd * 3 + 3)
                    V.scalar_tensor_tensor(of[par][:, :], of[par][:, :], 0.0, tbuf[:, :], ALU.min, ALU.subtract).then_inc(w_done, 1)
                if nxt:
                    if not first:
                        split(n1 * 3 + 2, 2)
                    scaled(n1 * 3, 0, ALL, qkf[:, :])
                    split(n1 * 3 + 3, 0)
                    dve.wait_ge(stack_hi, n1 + 1)
                    q, k = qkf[0:64, :], qkf[64:128, :]
                    V.tensor_tensor(ks[1 - par][64:128, :], k, ks[1 - par][0:64, :].bitcast(F32), ALU.subtract)
                    V.tensor_tensor(qls[1 - par][0:64, :], q, qhs[1 - par][0:64, :].bitcast(F32), ALU.subtract)
                    V.tensor_tensor(qls[1 - par][64:128, :], q, qhs[1 - par][0:64, :].bitcast(F32),
                                    ALU.subtract).then_inc(stack_lo, 1)
                    wait(dve, v_t, n1)
                    scaled(n1 * 3 + 1, 1 if first else 0, ALL, vf0[:, :])
                    split(n1 * 3 + 4, 1)
                elif exists(hd):
                    split(U_OUT0 + 2, 2)
                    split(U_OUT0 + 3, 3)
                if exists(hd):
                    dve.wait_ge(den_sq, hd + 1)
                    dve.wait_ge(emn_done, hd + 1)
                    V.tensor_tensor(acc[:, :], acc[:, :], nmbc[par][:, :], ALU.max).then_inc(x_rd, 1)
                    dve.wait_ge(ssq_done, hd + 1)
                    dve.wait_ge(x_rd, hd + 1)
                    V.scalar_tensor_tensor(acc[:, 0:QSPLIT], acc[:, 0:QSPLIT], EPS, ps[:, B_ND, 0:QSPLIT],
                                           ALU.mult, ALU.add)
                    V.scalar_tensor_tensor(acc[:, QSPLIT:T], acc[:, QSPLIT:T], EPS, ps[:, B_ND + 1, 0:T - QSPLIT],
                                           ALU.mult, ALU.add).then_inc(t_rd, 1)
                    dve.wait_ge(hln_done, hd + 1)
                    dve.wait_ge(w_done, hd + 1)
                    V.scalar_tensor_tensor(acc[:, :], acc[:, :], -0.5, of[par][:, :], ALU.mult, ALU.add).then_inc(e_done, 1)
                if nxt:
                    scaled(n1 * 3 + 2, 0, ALL, of[1 - par][:, :], ps[:, 4:6, 0:HALF] if first else None)
                if first:
                    dve.wait_ge(ucol_rd, 1)
                    exponents(0, 1, -1)
                if exists(hd):
                    dve.wait_ge(rs_rd, hd + 1)
                    V.tensor_tensor(nf[:, :], nf[:, :], acc[:, :], ALU.mult).then_inc(z_mul, 1)
                    dve.wait_ge(zh_rd, hd + 1)
                    V.tensor_tensor(blk(al, hd), nf[:, :], blk(ah, hd).bitcast(F32), ALU.subtract).then_inc(z_ready, 1)

            heads_loop(dve, 1, step0, tail=0)

            def residual(u, k, b, spans, ready=None, src=None):
                dve.wait_ge(unit_done, u + 1)
                ins = V.tensor_tensor(tokens(h[:, b, :], spans), src or banks(k, spans), tokens(h[:, b, :], spans), ALU.add)
                ins.then_inc(evac, 1)
                if ready is not None:
                    dve.wait_ge(evac, u + 1)
                    V.nop().then_inc(h_ready, 1)

            def out_product(base, n, spans):
                for k in range(8):
                    residual(base + k, k, k, spans, ready=n, src=ps[:, 2 * (k % 4):2 * (k % 4) + 2, 0:HALF] if n == 1 else None)
                    if k < 6:
                        split(base + k + 4, k % 4)
                    norm_prep(n, k, spans)

            def up_units(base, spans, g_all, factor=None):
                t0 = spans[0][0]
                for k in range(8):
                    split(base + (k + AHEAD), (k + AHEAD) % 4)
                    if factor is not None and k == 0:
                        dve.wait_ge(rb_ready, factor + 1)
                    dve.wait_ge(unit_done, base + (k + 1))
                    V.scalar_tensor_tensor(tokens(tbuf[:, :], spans), banks(k, spans), 0.0, tokens(rb[:, :], spans),
                                           ALU.max, ALU.mult).then_inc(evac, 1)
                    dve.wait_ge(evac, base + (k + 1))
                    V.nop().then_inc(relu_done, 1)
                    dve.wait_ge(ah_done, g_all * 8 + (k + 1))
                    V.tensor_tensor(al[:, k, t0:T], abuf[:, t0:T], ah[:, k, t0:T].bitcast(F32), ALU.subtract).then_inc(a_ready, 1)

            def down_units(base, spans):
                for k in range(8):
                    split(base + (k + AHEAD), (k + AHEAD) % 4)
                    residual(base + k, k, k, spans)

            def mlp(layer, base, spans):
                g0 = 4 * layer
                up_units(base, spans, g0, factor=2 * layer + 1)
                down_units(base + 8, spans)
                with dve.Fori(1, GROUPS - 1) as g:
                    up_units(g * 16 + base, spans, g + g0)
                    down_units(g * 16 + (base + 8), spans)
                last = base + 16 * (GROUPS - 1)
                up_units(last, spans, g0 + GROUPS - 1)
                for k in range(8):
                    split(last + 8 + k + AHEAD, (k + AHEAD) % 4)
                    residual(last + 8 + k, k, k, spans, ready=layer)
                    if layer == 0:
                        norm_prep(2, k, ALL)

            out_product(U_OUT0, 1, ALL)
            dve.wait_ge(lamv_in, 16)
            V.tensor_tensor(lamv[:, 0, :], lamv[:, 0, :], lamv[:, 1, :], ALU.mult)
            V.tensor_tensor(lamv[:, 2, :], lamv[:, 2, :], lamv[:, 3, :], ALU.mult).then_inc(lam_dve, 1)
            dve.wait_ge(lam_dve, 1)
            V.tensor_reduce(lam[:, 0:2], lamv[:, :, :].rearrange("p (a b) d -> p a b d", b=2)[:, :, 0, :], AX.X, ALU.add).then_inc(lam_dve, 1)
            dve.wait_ge(lam_act, 1)
            V.scalar_tensor_tensor(lam[:, 4:5], lam[:, 3:4], -LAMBDA_INIT, lam[:, 2:3], ALU.add, ALU.subtract).then_inc(lam_dve, 1)
            V.tensor_scalar(gains[:, 40:48], gains[:, 40:48], 1.0 - LAMBDA_INIT, None, ALU.mult).then_inc(lam_dve, 1)
            dve.wait_ge(lam_dve, 4)

            mlp(0, U_MLP0, ALL)

            split(U_IN1 + 2, 2)
            dve.wait_ge(rb_ready, 3)
            def maxima(n, i):
                for c in range(2):
                    dve.wait_ge(sc_done[c], n + 1)
                    w = NMETA + P * (i + 1)
                    if i < 3:
                        V.tensor_reduce(stat[:, i % 2, c:c + 1], ps[:, B_SC[c], 0:w], AX.X, ALU.max,
                                        negate=True).then_inc(max_done[c], 1)
                    else:
                        V.tensor_reduce(stat[:, i % 2, c:c + 1], ps[:, B_SC[c]:B_SC[c] + 2, 0:HALF], AX.XY, ALU.max,
                                        negate=True).then_inc(max_done[c], 1)

            def weights(hd, n, i):
                w = NMETA + P * (i + 1)
                dve.wait_ge(exp_done[0], n + 1)
                dve.wait_ge(exp_done[1], n + 1)
                V.reciprocal(stat[:, i % 2, 4:6], stat[:, i % 2, 2:4]).then_inc(rden_rd, 1)
                dve.wait_ge(rden_rd, n + 1)
                V.tensor_scalar(stat[:, i % 2, 6:7], stat[:, i % 2, 5:6], lam[:, 4:5], None, ALU.mult).then_inc(nlam_rd, 1)
                dve.wait_ge(nlam_rd, n + 1)
                e = es[0][i % 2], es[1][i % 2]
                V.tensor_scalar(e[1][:, 0:w], e[1][:, 0:w], stat[:, i % 2, 6:7], None, ALU.mult).then_inc(e1_rd, 1)
                dve.wait_ge(e1_rd, n + 1)
                wait(dve, at_t, n - 3)
                if i == 0:
                    wait(dve, meta_t, hd)
                V.scalar_tensor_tensor(attn[:, i, 0:w], e[0][:, 0:w], stat[:, i % 2, 4:5], e[1][:, 0:w],
                                       ALU.mult, ALU.add).then_inc(attn_rd, 1)

            def keys_lo(n1, par, c):
                dve.wait_ge(khi_done, n1 * 2 + (c + 1))
                for b in (0, 64):
                    last = V.tensor_tensor(kls[1 - par][c][b:b + 64, :], kf1[64 * c:64 * c + 64, :],
                                           khs[1 - par][c][0:64, :].bitcast(F32), ALU.subtract)
                last.then_inc(klo_done, 1)

            def step1(hd, par, pair):
                n1 = hd + 1
                if exists(hd):
                    maxima(hd * 4, 0)
                    weights(hd, hd * 4, 0)
                if exists(n1) and exists(hd):
                    split(n1 * 3 + (U_IN1 + 2), 2)
                elif exists(hd):
                    split(U_OUT1 + 2, 2)
                if exists(hd):
                    maxima(hd * 4 + 1, 1)
                    weights(hd, hd * 4 + 1, 1)
                if exists(n1):
                    scaled(n1 * 3 + U_IN1, 0, SEQ, qf1[:, :], ps[:, B_Q1, :])
                    split(n1 * 3 + (U_IN1 + 3), 0)
                    dve.wait_ge(qhi_done, n1 + 1)
                    for c in range(2):
                        b0, b1 = 64 * c, 64 - 64 * c
                        last = V.scalar_tensor_tensor(qst[1 - par][c][b1:b1 + 64, :], qf1[b0:b0 + 64, NMETA:T], SCORE_SCALE,
                                                      qst[1 - par][c][b0:b0 + 64, :].bitcast(F32), ALU.mult, ALU.subtract)
                    last.then_inc(qlo_done, 1)
                elif exists(hd):
                    split(U_OUT1 + 3, 3)
                if exists(hd):
                    maxima(hd * 4 + 2, 2)
                    weights(hd, hd * 4 + 2, 2)
                if exists(n1):
                    scaled(n1 * 3 + (U_IN1 + 1), 0, ALL, kf1[:, :])
                if exists(hd):
                    maxima(hd * 4 + 3, 3)
                if exists(n1):
                    keys_lo(n1, par, 0)
                if exists(hd):
                    weights(hd, hd * 4 + 3, 3)
                if exists(n1):
                    keys_lo(n1, par, 1)
                if exists(hd - 1):
                    dve.wait_ge(rs_rd1, hd)
                    V.tensor_tensor(zf[:, :], zf[:, :], acc[:, NMETA:T], ALU.mult).then_inc(z_mul1, 1)
                if exists(n1):
                    wait(dve, v_t1, n1)
                    scaled(n1 * 3 + (U_IN1 + 2), 0, ALL, vf1[:, :],
                           ps[:, 4:6, 0:HALF] if isinstance(hd, int) and hd < 0 else None)
                    split(n1 * 3 + (U_IN1 + 4), 1)
                if exists(hd - 1):
                    dve.wait_ge(zh_rd1, hd)
                    V.tensor_tensor(blk(al, hd - 1)[:, NMETA:T], zf[:, :], blk(ah, hd - 1)[:, NMETA:T].bitcast(F32),
                                    ALU.subtract).then_inc(z_ready, 1)

            heads_loop(dve, 1, step1)
            out_product(U_OUT1, 3, SEQ)
            mlp(1, U_MLP1, SEQ)

            dve.wait_ge(gfin_in, 16)
            for i in range(4):
                dve.wait_ge(frs, i + 1)
                V.scalar_tensor_tensor(fin[:, i, :].rearrange("p (b n) -> p b n", b=2), ps[:, 2 * i:2 * i + 2, :],
                                       lam[:, i:i + 1], gfin[:, :].rearrange("p (b n) -> p b n", b=2),
                                       ALU.mult, ALU.mult).then_inc(fmul, 1)

        @block.tensor
        def _(pe):
            mm = nc.tensor.matmul

            def blocks(u, slot, mh, ml, spans, bank, free, kb0=0, kb1=CB, block_wait=None):
                if kb0 == 0:
                    pe.wait_ge(split_lo, u + 1)
                    wait(pe, evac, free)
                for kb in range(kb0, kb1):
                    if block_wait is not None:
                        block_wait(kb)
                    for n, (w, m) in enumerate(((wh, mh), (wh, ml), (wl, mh))):
                        for s, (t0, w_) in enumerate(spans):
                            last = mm(ps[:, bank + s, 0:w_], w[:, slot, kb, :], m[:, kb, t0:t0 + w_],
                                      start=(kb == 0 and n == 0), stop=(kb == CB - 1 and n == 2))
                if kb1 == CB:
                    last.then_inc(unit_done, 1)

            def unit(u, k, mh, ml, spans, block_wait=None):
                if len(spans) == 2:
                    blocks(u, k % 4, mh, ml, spans, 2 * (k % 2), u - 1, block_wait=block_wait)
                else:
                    blocks(u, k % 4, mh, ml, spans, k % 4, u - 3, block_wait=block_wait)

            def mean_squares(n, spans, bank=B_SUM):
                pe.wait_ge(acc_done, 8 * n + 8)
                for s, (t0, w) in enumerate(spans):
                    last = mm(ps[:, bank + s, 0:w], ones[:, :], acc[:, t0:t0 + w], start=True, stop=True)
                last.then_inc(sum_done, 1)

            def y_block(n):
                return lambda kb: pe.wait_ge(y_ready, 8 * n + kb + 1)

            def z_block(layer):
                return lambda kb: pe.wait_ge(z_ready, HEADS * layer + kb + 1)

            def part0(n1, j, kb0, kb1):
                first = isinstance(n1, int) and n1 == 0
                if first and j == 2:
                    pe.wait_ge(ln_done, 1)
                blocks(n1 * 3 + j, j, yh, yl, ALL, 2 * j if first else 0, 0 if first else n1 * 3 + j, kb0, kb1)

            def out_part0(k, kb0, kb1):
                if kb0 == 0 and k > 0:
                    pe.wait_ge(p_ready, HEADS)
                blocks(U_OUT0 + k, k, ah, al, ALL, 2 * k, U_OUT0, kb0, kb1, z_block(0))

            def weighted(par, values, done):
                seen = set()
                for n, (j, t0, t1, _, _) in enumerate(PIECES):
                    rows = TILES0[j][1]
                    b, c = (B_ND, t0) if t1 <= QSPLIT else (B_ND + 1, t0 - QSPLIT)
                    lhs = ones[0:rows, :] if values is None else values[0:rows, j, :]
                    last = mm(ps[:, b, c:c + t1 - t0], lhs, dmat[par][0:rows, DCOL[n]:DCOL[n + 1]],
                              start=(b not in seen), stop=(n in (1, len(PIECES) - 1)))
                    seen.add(b)
                last.then_inc(done, 1)

            def step0(hd, par, pair):
                n1, nxt = hd + 1, exists(hd + 1)
                first = isinstance(hd, int) and hd < 0
                if exists(hd):
                    pe.wait_ge(stack_lo, hd + 1)
                    wait(pe, p_ready, hd)
                    if isinstance(hd, int) and hd == 0:
                        pe.wait_ge(evac, 3)
                    for j, t0, t1, b, c in PIECES:
                        s0, rows = TILES0[j]
                        for m, q in enumerate((qhs[par], qls[par])):
                            last = mm(ps[0:rows, b, c:c + t1 - t0], ks[par][:, s0:s0 + rows], q[:, t0:t1],
                                      start=(m == 0), stop=(m == 1))
                    last.then_inc(s_done, 1)
                if nxt and not first:
                    part0(n1, 0, 0, CB)
                elif not nxt:
                    out_part0(0, 0, 4)
                if exists(hd):
                    pe.wait_ge(p_ready, hd + 1)
                    pe.wait_ge(vth_rd, hd + 1)
                    weighted(par, vth0[par], pv_done)
                if nxt and not first:
                    part0(n1, 1, 0, CB)
                elif not nxt:
                    out_part0(0, 4, 6)
                    out_part0(1, 0, 3)
                if exists(hd):
                    pe.wait_ge(num_rd, hd + 1)
                    weighted(par, None, den_done)
                if nxt:
                    part0(n1, 2, 0, 4)
                else:
                    out_part0(1, 3, 6)
                if exists(hd):
                    pe.wait_ge(den_sq, hd + 1)
                    mm(ps[:, B_ND, 0:QSPLIT], head_mean[:, :], abuf[:, 0:QSPLIT], start=True, stop=True)
                    mm(ps[:, B_ND + 1, 0:T - QSPLIT], head_mean[:, :], abuf[:, QSPLIT:T],
                       start=True, stop=True).then_inc(ssq_done, 1)
                if nxt:
                    part0(n1, 2, 4, CB)
                if first:
                    pe.wait_ge(gate_dve, 7)
                    pe.wait_ge(rb_ready, 1)
                    for s, (t0, w) in enumerate(TILES0):
                        last = nc.tensor.transpose(ps[0:w, B_SUM, 8 * s:8 * s + 8], gu[:, t0:t0 + w],
                                                   ident[0:HEADS, 0:HEADS])
                    last.then_inc(u_t, 1)
                    pe.wait_ge(ucol_rd, 1)
                if nxt:
                    pe.wait_ge(evac, n1 * 3 + 2)
                    wait(pe, t_rd, n1)
                    for s, (t0, w) in enumerate(TILES0):
                        o = ps[:, B_ND, P * s:P * (s + 1)] if w == P else ps[0:w, B_ND + 1, 0:P]
                        last = nc.tensor.transpose(o, vf0[:, t0:t0 + w], ident[:, :])
                    last.then_inc(v_t, 1)

            def turn_x(c):
                pe.wait_ge(x_in[c // 2], 16)
                wait(pe, hx_rd, c - 1)
                for i in range(4):
                    last = nc.tensor.transpose(ps[:, 4 + c % 2, P * i:P * (i + 1)], xin[:, i, P * c:P * (c + 1)], ident[:, :])
                last.then_inc(x_t, 1)

            pe.wait_ge(ident_made, 1)
            pe.wait_ge(gains_in, 3 * 16)
            nc.tensor.transpose(ps[:, 6, 0:48], gain_rows[:, :], ident[0:48, 0:48]).then_inc(gain_t, 1)
            pe.wait_ge(meta_come, 16)
            for c in range(CB):
                last = nc.tensor.transpose(ps[:, 7, NMETA * c:NMETA * (c + 1)], meta_in[:, P * c:P * (c + 1)],
                                           ident[0:NMETA, 0:NMETA])
            last.then_inc(meta_t0, 1)
            turn_x(0)
            turn_x(1)
            pe.wait_ge(gw_ready, 1)
            pe.wait_ge(gain_rd, 1)
            pe.wait_ge(hm_rd, 1)
            for kb in range(CB):
                if kb + 2 < CB:
                    turn_x(kb + 2)
                pe.wait_ge(y_ready, kb + 1)
                for n, (w, m) in enumerate(((gwh, yh), (gwh, yl), (gwl, yh))):
                    for s, (t0, w_) in enumerate(ALL):
                        last = mm(ps[0:40, 6 + s, 0:w_], w[:, kb, :], m[:, kb, t0:t0 + w_],
                                  start=(kb == 0 and n == 0), stop=(kb == CB - 1 and n == 2))
                if kb == CB - 1:
                    last.then_inc(gate_mm, 1)
                if kb >= 1:
                    part0(0, 0, kb - 1, kb)
                if kb >= 4:
                    part0(0, 1, kb - 4, kb - 3)
            part0(0, 0, 7, CB)
            mean_squares(0, ALL, 4)
            part0(0, 1, 4, CB)
            heads_loop(pe, 1, step0, tail=0)
            for k in range(2):
                out_part0(k, 6, 7)
            out_part0(2, 0, 7)
            for k in range(3):
                out_part0(k, 7, CB)
            pe.wait_ge(t_rd, HEADS)
            for k in range(3, 8):
                blocks(U_OUT0 + k, k % 4, ah, al, ALL, 2 * (k % 4), U_OUT0 + k - 3)

            def mlp(layer, base, spans):
                g0 = 4 * layer

                def group(u0, g, first=False):
                    for k in range(8):
                        unit(u0 + k, k, yh, yl, spans, y_block(2 * layer + 1) if first and k == 0 else None)
                        if first and k == 0:
                            mean_squares(2 * layer + 1, spans)
                    for k in range(8):
                        unit(u0 + (8 + k), k, ah, al, spans,
                             (lambda kb: pe.wait_ge(a_ready, g * 8 + (kb + 1))) if k == 0 else None)

                group(base, g0, True)
                with pe.Fori(1, GROUPS) as g:
                    group(g * 16 + base, g + g0)

            mlp(0, U_MLP0, ALL)

            def part(n1, j, kb0, kb1, block_wait=None):
                free = n1 * 3 + (U_IN1 + (-2, 0, 2)[j])
                first = isinstance(n1, int) and n1 == 0
                if first:
                    free = U_IN1
                blocks(n1 * 3 + (U_IN1 + j), j, yh, yl, SEQ if j == 0 else ALL,
                       B_Q1 if j == 0 else 4 if first and j == 2 else 0, free, kb0, kb1, block_wait)

            def scores(n, i, par):
                w = NMETA + P * (i + 1)
                cuts = [(0, w)] if i < 3 else ALL
                for c in range(2):
                    wait(pe, exp_done[c], n)
                    q = qst[par][c][:, P * i:P * (i + 1)]
                    for s, (t0, w_) in enumerate(cuts):
                        o = ps[:, B_SC[c] + s, 0:w_]
                        masked = s == len(cuts) - 1
                        mm(o, q, khs[par][c][:, t0:t0 + w_], start=True, stop=False)
                        last = mm(o, q, kls[par][c][:, t0:t0 + w_], start=False, stop=not masked)
                        if masked:
                            last = mm(o[:, w_ - 64:w_], neg_row[:, :], one_row[:, :], start=False, stop=True)
                    last.then_inc(sc_done[c], 1)

            def turn(n, i):
                pe.wait_ge(attn_rd, n + 1)
                wait(pe, at_rd, n)
                for s in range(i + 1):
                    last = nc.tensor.transpose(ps[:, B_TR1, P * s:P * (s + 1)],
                                               attn[:, i, NMETA + P * s:NMETA + P * (s + 1)], ident[:, :])
                last.then_inc(at_t, 1)

            def output(n, par):
                pe.wait_ge(meta_rd, n + 1)
                mm(ps[:, B_PV1, :], vth1[par][0:NMETA, 4, :], att_meta[:, :], start=True, stop=False)
                for s in range(4):
                    last = mm(ps[:, B_PV1, P * s:X], vth1[par][:, s, :], att[:, s, P * s:X], start=False, stop=(s == 3))
                last.then_inc(pv_done1, 1)

            def turn_meta(n):
                pe.wait_ge(vt_rd1, min(n + 2, HEADS) if isinstance(n, int) else n + 2)
                pe.wait_ge(at_rd, n * 4 + 4)
                for i in range(4):
                    last = nc.tensor.transpose(ps[0:NMETA, B_TR1, P * i:P * (i + 1)], attn[:, i, 0:NMETA], ident[:, :])
                last.then_inc(meta_t, 1)

            def squares(n):
                pe.wait_ge(pv_rd1, n + 1)
                mm(ps[:, B_PV1, :], head_mean[:, :], abuf[:, NMETA:T], start=True, stop=True).then_inc(ssq_done1, 1)

            def out_part(k, kb0, kb1):
                if kb0 == 0 and k == 2:
                    pe.wait_ge(exp_done[0], 4 * HEADS)
                blocks(U_OUT1 + k, k, ah, al, SEQ, k, U_OUT1, kb0, kb1, z_block(1))

            def step1(hd, par, pair):
                n1, nxt = hd + 1, exists(hd + 1)
                last_head = isinstance(hd, int) and hd == HEADS - 1
                if exists(hd):
                    pe.wait_ge(qlo_done, n1)
                    pe.wait_ge(klo_done, n1 * 2)
                    if isinstance(hd, int) and hd == 0:
                        pe.wait_ge(evac, U_IN1 + 3)
                    scores(hd * 4, 0, par)
                if not exists(hd) and exists(hd - 1):
                    out_part(2, 0, 6)
                if exists(hd - 1):
                    turn(hd * 4 - 1, 3)
                if nxt:
                    if isinstance(hd, int) and hd < 0:
                        part(n1, 0, 0, CB, y_block(2))
                        mean_squares(2, ALL)
                    else:
                        part(n1, 0, 0, 2)
                elif last_head:
                    out_part(0, 0, 3)
                if exists(hd):
                    pe.wait_ge(evac, hd * 3 + (U_IN1 + 3))
                    wait(pe, at_rd, hd * 4)
                    wait(pe, hln_done1, hd - 1)
                    for s, (t0, w) in enumerate(TILES1):
                        o = ps[:, B_TR1, P * s:P * (s + 1)] if w == P else ps[0:w, B_PV1, 0:P]
                        last = nc.tensor.transpose(o, vf1[:, t0:t0 + w], ident[:, :])
                    last.then_inc(v_t1, 1)
                    if nxt:
                        part(n1, 0, 2, 5)
                    elif last_head:
                        out_part(0, 3, 5)
                if exists(hd - 1):
                    turn_meta(hd - 1)
                    if not exists(hd):
                        out_part(3, 0, 3)
                if exists(hd):
                    if nxt:
                        part(n1, 0, 5, 6)
                    scores(hd * 4 + 1, 1, par)
                if exists(hd - 1):
                    output(hd - 1, 1 - par)
                if exists(hd):
                    if nxt:
                        part(n1, 0, 6, CB)
                    elif last_head:
                        out_part(0, 5, 6)
                        out_part(1, 0, 1)
                    wait(pe, meta_rd, hd)
                    wait(pe, vt_rd1, hd + 1)
                    turn(hd * 4, 0)
                if nxt:
                    part(n1, 1, 0, 2)
                elif last_head:
                    out_part(1, 1, 3)
                if exists(hd):
                    scores(hd * 4 + 2, 2, par)
                    turn(hd * 4 + 1, 1)
                if nxt:
                    part(n1, 1, 2, CB)
                elif last_head:
                    out_part(1, 3, 5)
                if exists(hd - 1):
                    if not exists(hd):
                        out_part(3, 3, 6)
                if exists(hd):
                    if nxt:
                        pe.wait_ge(evac, n1 * 3 + (U_IN1 + 1))
                    scores(hd * 4 + 3, 3, par)
                if exists(hd - 1):
                    squares(hd - 1)
                if exists(hd):
                    turn(hd * 4 + 2, 2)
                if nxt:
                    part(n1, 2, 0, CB)
                elif last_head:
                    out_part(1, 5, 6)

            heads_loop(pe, 1, step1)
            for k in range(2):
                out_part(k, 6, 7)
            for k in range(4):
                out_part(k, 7 if k < 2 else 6, CB)
            for k in range(4, 8):
                unit(U_OUT1 + k, k, ah, al, SEQ)
            mlp(1, U_MLP1, SEQ)

            pe.wait_ge(evac, U_END)
            for i in range(4):
                for c in range(CB):
                    last = nc.tensor.transpose(ps[:, 2 * i + c // 4, P * (c % 4):P * (c % 4 + 1)],
                                               h[:, c, NMETA + P * i:NMETA + P * (i + 1)], ident[:, :])
                last.then_inc(out_t, 1)


_INS = ["x", "meta_tokens", "norm_gains", "mlstm_w_in", "mlstm_b_gate", "mlstm_head_gain", "mlstm_w_out",
        "diff_w_in", "diff_lambda", "diff_head_gain", "diff_w_out", "mlp_w_up", "mlp_w_down", "final_gain"]
_OUTS = [((1, X, D), "float32")]


def kernel(**inputs):
    import numpy as _np
    import concourse.bacc as _bacc
    from concourse import mybir as _mybir
    from concourse.bass_utils import run_bass_kernel_spmd as _run

    nc = _bacc.Bacc("TRN2", target_bir_lowering=False, num_devices=1)
    arrays, args = {}, {}
    for name in _INS:
        arr = _np.ascontiguousarray(inputs[name])
        arrays[f"in_{name}_dram"] = arr
        args[name] = nc.dram_tensor(f"in_{name}_dram", arr.shape, _mybir.dt.from_np(arr.dtype), kind="ExternalInput").ap()
    shape, dtype = _OUTS[0]
    out = nc.dram_tensor("out_0_dram", shape, _mybir.dt.from_np(_np.dtype(dtype)), kind="ExternalOutput").ap()
    program(nc, args, out)
    r = _run(nc, [arrays], core_ids=[0])
    return r.results[0]["out_0_dram"]
```

```python
from contextlib import ExitStack
import math

import concourse.bass as bass
from concourse import mybir

ALU = mybir.AluOpType
ACT = mybir.ActivationFunctionType
AX = mybir.AxisListType
F32 = mybir.dt.float32
F32R = mybir.dt.float32r
BF16 = mybir.dt.bfloat16
ds = bass.ds

P = 128
D = 1024
NMETA = 16
X = 512
T = NMETA + X
HALF = T // 2
CB = D // P
FF = 4096
GROUPS = FF // D
HEADS = 8
DQK = 64
GATE_COL = 3072
FG_ROW = 32
EPS = 1e-6
SUBLN_EPS = 1e-5
LAMBDA_INIT = 0.8 - 0.6 * math.exp(-0.3)
NEG = -1e30
SCORE_SCALE = DQK ** -0.5
NM_MAX = 28.0

RING = 4
RAW = 2
AHEAD = 2
MISSED = [(7, 6), (14, 12)]
CAME = [(0, 0, 0), (9, 9, 8)]

U_IN0, U_OUT0, U_MLP0 = 0, 24, 32
U_IN1, U_OUT1, U_MLP1 = 96, 120, 128
U_END = 192

ALL = [(0, HALF), (HALF, HALF)]
SEQ = [(NMETA, X)]

B_SUM = 6
B_S0, B_ND = 2, 6

QSPLIT = 256
PIECES = [(0, 0, 256, B_S0, 0), (1, 128, 256, B_S0, 256),
          (0, 256, 528, B_S0 + 1, 0), (3, 384, 528, B_S0 + 1, 272),
          (1, 256, 528, B_S0 + 2, 0),
          (2, 256, 528, B_S0 + 3, 0), (4, 512, 528, B_S0 + 3, 272)]
DCOL = [sum(q[2] - q[1] for q in PIECES[:n]) for n in range(len(PIECES) + 1)]
DW = DCOL[-1]
D_FULL = DCOL[-2]
P_BANKS = [(B_S0, 384, 0), (B_S0 + 1, 416, 384), (B_S0 + 2, 272, 800), (B_S0 + 3, 272, 1072)]
P_CUTS = [(0, DCOL[4]), (DCOL[4], D_FULL), (D_FULL, DW)]
DIAG = [(DCOL[0], 128), (DCOL[1], 128), (DCOL[5], 128), (DCOL[3], 128), (DCOL[6], 16)]

B_SC, B_TR1, B_PV1 = (2, 4), 6, 7
LAST_BANKS = [0, 1, 2, 3, 0, 1, 0, 1]
OUT_BANKS = [(4, 5), (6, 7), (2, 3), (1, 0)]
B_Q1 = 3
TILES0 = [(0, 128), (128, 128), (256, 128), (384, 128), (512, 16)]
TILES1 = [(16, 128), (144, 128), (272, 128), (400, 128), (0, 16)]


def wait(eng, sem, value):
    if not isinstance(value, int) or value > 0:
        eng.wait_ge(sem, value)


def heads_loop(eng, lead, step, tail=1):
    pairs = (HEADS - 1 - lead) // 2
    for h in range(-lead, 1):
        step(h, h % 2, h // 2)
    with eng.Fori(0, pairs) as i:
        step(i * 2 + 1, 1, i)
        step(i * 2 + 2, 0, i + 1)
    for h in range(2 * pairs + 1, HEADS + tail):
        step(h, h % 2, h // 2)


def exists(h):
    return not isinstance(h, int) or 0 <= h < HEADS


def program(nc, a, out):
    with ExitStack() as ctx:
        cursor = [(nc.sbuf_base + 63) // 64 * 64]
        limit = nc.sbuf_usable_end

        def place(name, shape, dt, where, end):
            size = 2 if dt == BF16 else 4
            for n in shape[1:]:
                size *= n
            size = (size + 31) // 32 * 32
            assert where[0] + size <= end, (name, where[0] + size - end)
            t = nc.alloc_sbuf_tensor_at(name, shape, dt, offset=where[0])
            where[0] += size
            return t

        def new(name, shape, dt=F32):
            return place(name, shape, dt, cursor, limit)

        h = new("h", [P, CB, T])
        y_at = cursor[0]
        yh = new("yh", [P, CB, T], F32R)
        yl = new("yl", [P, CB, T], F32R)
        y_end = a_at = cursor[0]
        ah = new("ah", [P, CB, T], F32R)
        al = new("al", [P, CB, T], F32R)
        a_end = cursor[0]
        wh = new("wh", [P, RING, CB, P], F32R)
        wl = new("wl", [P, RING, CB, P], F32R)
        raw = new("raw", [P, RAW, CB, 2 * P])
        tbuf = new("tbuf", [P, T])
        abuf = new("abuf", [P, T])
        acc = new("acc", [P, T])
        rb = new("rb", [P, T])
        ident = new("ident", [P, P])
        ones_r = new("ones_r", [P, P], F32R)
        ones = ones_r[:, :].bitcast(F32)
        causal = new("causal", [P, P])
        head_mean = new("head_mean", [P, P], F32R)
        gains = new("gains", [P, 56])
        eps_d = new("eps_d", [P, 1])
        eps_s = new("eps_s", [P, 1])
        bias_i = new("bias_i", [HEADS, 1])
        bias_f = new("bias_f", [64, 1])
        stat = new("stat", [P, 2, 8])
        lam = new("lam", [P, 8])
        ucol = new("ucol", [P, 5, HEADS])
        neg_row = new("neg_row", [1, P], BF16)
        one_row = new("one_row", [1, 64], BF16)
        arena = cursor[0]

        w0 = [arena]
        xin = place("xin", [P, 4, D], F32, w0, limit)
        meta_in = place("meta_in", [NMETA, D], F32, w0, limit)
        gain_rows = place("gain_rows", [32, P], F32, w0, limit)
        more_rows = place("more_rows", [24, P], F32, w0, limit)
        w0 = [arena]
        qkf, vf0, nf = (place(n, [P, T], F32, w0, limit) for n in ("qkf", "vf0", "nf"))
        sqh, sql = (place(n, [P, T], F32R, w0, limit) for n in ("sqh", "sql"))
        dmat = place("dmat", [P, DW], F32, w0, limit)
        phi, plo = (place(n, [P, DW], F32R, w0, limit) for n in ("phi", "plo"))
        ks, qhs, qls, vh, vl, of, mbc, nmbc = (
            [place(f"{name}{par}", shape, dt, w0, limit) for par in range(2)]
            for name, shape, dt in (("ks", [P, T], F32R), ("qhs", [P, T], F32R), ("qls", [P, T], F32R),
                                    ("vh", [P, 5, P], F32R), ("vl", [P, 5, P], F32R), ("of", [P, T], F32), ("mbc", [P, T], F32),
                                    ("nmbc", [P, T], F32)))
        w0 = [a_at]
        gx, gabs, gexp, gln, glf, gone = (place(n, [64, T], F32, w0, a_end)
                                          for n in ("gx", "gabs", "gexp", "gln", "glf", "gone"))
        gi, gb, gu, gm, gnm = (place(n, [HEADS, T], F32, w0, a_end) for n in ("gi", "gb", "gu", "gm", "gnm"))
        graw = place("graw", [P, CB, 16], F32, w0, a_end)
        gwh = place("gwh", [P, CB, 40], F32R, w0, a_end)
        gwl = place("gwl", [P, CB, 40], F32R, w0, a_end)
        lamv = place("lamv", [P, 4, DQK], F32, [arena], limit)
        w0 = [arena]
        qf1 = place("qf1", [P, T], F32, w0, limit)
        kf1 = place("kf1", [P, T], F32, w0, limit)
        vf1 = place("vf1", [P, T], F32, w0, limit)
        qst = [[place(f"qst{par}{c}", [P, X], F32R, w0, limit) for c in range(2)] for par in range(2)]
        khs = [[place(f"khs{par}{c}", [P, T], F32R, w0, limit) for c in range(2)] for par in range(2)]
        kls = [[place(f"kls{par}{c}", [P, T], F32R, w0, limit) for c in range(2)] for par in range(2)]
        vth1 = [place(f"vth1{par}", [P, 5, P], F32, w0, limit) for par in range(2)]
        att = place("att", [P, 4, X], F32, w0, limit)
        att_meta = place("att_meta", [NMETA, X], F32, w0, limit)
        attn = place("attn", [P, 4, T], F32, w0, limit)
        es = [[place("e00", [P, T], F32, w0, limit), place("e01", [P, T], F32, w0, limit)],
              [tbuf, place("e11", [P, T], F32, w0, limit)]]
        zf = place("zf", [P, X], F32, w0, limit)
        sqh1, sql1 = (place(n, [P, X], F32R, w0, limit) for n in ("sqh1", "sql1"))
        hg = place("hg", [P, CB, X], F32, [y_at], y_end)
        fin = place("fin", [P, 4, D], F32, [arena], limit)

        ps = ctx.enter_context(nc.psum_tensor("ps", [P, 8, 512], F32))
        gate_rows = nc.dram_tensor("gate_rows", [2 * HEADS, T], F32).ap()

        def sem(name):
            return ctx.enter_context(nc.semaphore(name))

        def sems(names):
            return [sem(n) for n in names.split()]

        raw_in = [sem(f"raw_in{i}") for i in range(RAW)]
        mrow_in = [sem(f"mrow_in{i}") for i in range(2)]
        nrow_in = [sem(f"nrow_in{i}") for i in range(2)]
        small_in, gains_in, more_in, meta_come, lamv_in, m_sent, nm_sent, out_sent = sems("small_in gains_in more_in meta_come lamv_in m_sent nm_sent out_sent")
        ones_made, consts, ident_made, gain_t, gain_rd, gw_zero, gwh_done, gw_ready = sems(
            "ones_made consts ident_made gain_t gain_rd gw_zero gwh_done gw_ready")
        x_t, hx_rd, meta_t0, hm_rd = sems("x_t hx_rd meta_t0 hm_rd")
        split_hi, split_lo, unit_done, evac = sems("split_hi split_lo unit_done evac")
        h_ready, yh_done, y_ready, sq_done, acc_done, sum_done, ln_done, rb_ready = sems(
            "h_ready yh_done y_ready sq_done acc_done sum_done ln_done rb_ready")
        relu_done, sqa_done, ah_done, a_ready = sems("relu_done sqa_done ah_done a_ready")
        gate_mm, gate_dve, gate_act, u_t, ucol_rd = sems("gate_mm gate_dve gate_act u_t ucol_rd")
        sq_hi, sq_lo, sq_hi1, sq_lo1 = sems("sq_hi sq_lo sq_hi1 sq_lo1")
        p_done, ph_done, vh_done, vl_done = sems("p_done ph_done vh_done vl_done")
        stack_hi, stack_lo, v_t, dpre, dexp, dready, emn_done = sems(
            "stack_hi stack_lo v_t dpre dexp dready emn_done")
        s_done, p_ready, pv_done, den_done, num_rd, den_sq, x_rd, ssq_done, t_rd = sems(
            "s_done p_ready pv_done den_done num_rd den_sq x_rd ssq_done t_rd")
        lsig, w_done, hln_done, e_done, rs_rd, z_mul, zh_rd, z_ready = sems(
            "lsig w_done hln_done e_done rs_rd z_mul zh_rd z_ready")
        x_in = [sem(f"x_in{i}") for i in range(4)]
        unit_in = [sem(f"unit_in{i}") for i in range(3)]
        half_in = sem("half_in")
        qhi_done, qlo_done, khi_done, klo_done, v_t1, vt_rd1, meta_t, meta_rd = sems(
            "qhi_done qlo_done khi_done klo_done v_t1 vt_rd1 meta_t meta_rd")
        pv_done1, pv_rd1, ssq_done1, hln_done1, rs_rd1, z_mul1, zh_rd1 = sems(
            "pv_done1 pv_rd1 ssq_done1 hln_done1 rs_rd1 z_mul1 zh_rd1")
        sc_done = [sem(f"sc_done{c}") for c in range(2)]
        max_done = [sem(f"max_done{c}") for c in range(2)]
        exp_done = [sem(f"exp_done{c}") for c in range(2)]
        rden_rd, e1_rd, attn_rd, at_t, at_rd = sems("rden_rd e1_rd attn_rd at_t at_rd")
        lam_dve, lam_act = sems("lam_dve lam_act")
        hg_done, fsum, fln, frs, fmul_act, fmul_dve = sems("hg_done fsum fln frs fmul_act fmul_dve")
        out_t = [sem(f"out_t{i}") for i in range(2)]

        w_in0, w_in1 = a["mlstm_w_in"][0], a["diff_w_in"][0]
        w_out0, w_out1 = a["mlstm_w_out"][0], a["diff_w_out"][0]

        def columns(w, c0, n):
            return w.rearrange("(k p) m -> p k m", p=P)[:, :, ds(c0, n)]

        def halves(t):
            return t.rearrange("p (s n) -> p s n", s=2)

        def banks(u, spans):
            b = 2 * (u % 2)
            return ps[:, b:b + 2, 0:HALF] if len(spans) == 2 else ps[:, u % 4, 0:X]

        def tokens(t, spans):
            return halves(t) if len(spans) == 2 else t[:, NMETA:T]

        block = ctx.enter_context(nc.Block())

        @block.sync
        def _(sp):
            def load_x(j):
                sp.dma_start(xin[:, :, 256 * j:256 * j + 256],
                             a["x"][0].rearrange("(i p) d -> p i d", p=P)[:, :, 256 * j:256 * j + 256]).then_inc(x_in[j], 16)

            load_x(0)
            sp.dma_start(graw[:, :, :], columns(w_in0, GATE_COL, 16)).then_inc(small_in, 16)
            bg = a["mlstm_b_gate"].rearrange("l (g o) -> (l g) o", o=1)
            sp.dma_start(bias_i[:, :], bg[0:HEADS, :]).then_inc(small_in, 16)
            sp.dma_start(bias_f[FG_ROW:FG_ROW + HEADS, :], bg[HEADS:2 * HEADS, :]).then_inc(small_in, 16)
            load_x(1)

            def load(slot, src, split=None):
                if split is not None:
                    sp.wait_ge(split_lo, split)
                sp.dma_start(raw[:, slot, :, :], src).then_inc(raw_in[slot], 16)

            def load_unit(slot, src, split):
                sp.wait_ge(split_lo, split)
                sp.dma_start(raw[:, slot // 2, :, P * (slot % 2):P * (slot % 2) + P], src).then_inc(unit_in[slot], 16)

            def load_halves(w, c0, c1):
                sp.dma_start(raw[:, 0, :, 0:DQK], columns(w, c0, DQK)).then_inc(unit_in[0], 16)
                sp.dma_start(raw[:, 0, :, DQK:P], columns(w, c1, DQK)).then_inc(half_in, 16)

            def head0(h, split):
                for j in range(3):
                    if split is not None:
                        sp.wait_ge(split_lo, split + j)
                    elif j > 0:
                        load_x(j + 1)
                    if j == 0:
                        load_halves(w_in0, h * DQK, h * DQK + D // 2)
                    else:
                        sp.dma_start(raw[:, j // 2, :, P * (j % 2):P * (j % 2) + P],
                                     columns(w_in0, h * P + D * j, P)).then_inc(unit_in[j], 16)

            def out_weights(w, base):
                if base == U_OUT0:
                    sp.wait_ge(split_lo, base - 2)
                    load_halves(w, 0, DQK)
                else:
                    load_unit(0, columns(w, 0, P), base - 2)
                load_unit(1, columns(w, P, P), base - 1)
                load(1, columns(w, 256, 256), base)
                for j in range(2):
                    load(j, columns(w, 512 + 256 * j, 256), base + 4 + 2 * j - 2)

            def mlp(layer, base):
                up = a["mlp_w_up"][layer]
                down = a["mlp_w_down"][layer].rearrange("(g k p) m -> g p k m", k=CB, p=P)
                with sp.Fori(0, GROUPS) as g:
                    for j in range(4):
                        load(j % 2, columns(up, g * D + 256 * j, 256), g * 16 + (base + 2 * j - 2))
                    for j in range(4):
                        src = down[ds(g, 1), :, :, 256 * j:256 * j + 256].rearrange("g p k m -> p (g k) m")
                        load(j % 2, src, g * 16 + (base + 8 + 2 * j - 2))

            head0(0, None)
            with sp.Fori(1, HEADS) as i:
                head0(i, i * 3 - 2)
            out_weights(w_out0, U_OUT0)
            mlp(0, U_MLP0)
            with sp.Fori(0, HEADS) as i:
                for j in range(3):
                    load_unit(j, columns(w_in1, i * P + D * j, P), i * 3 + (U_IN1 + j - 2))
            out_weights(w_out1, U_OUT1)
            mlp(1, U_MLP1)

            for i in range(4):
                sp.wait_ge(fmul_act, i + 1)
                sp.wait_ge(fmul_dve, i + 1)
                sp.dma_start(out[0, P * i:P * (i + 1), :], fin[:, i, :]).then_inc(out_sent, 16)
            sp.wait_ge(out_sent, 4 * 16)

        @block.gpsimd
        def _(pool):
            nc.gpsimd.memset(ones, 1.0).then_inc(ones_made, 1)
            pool.wait_ge(ones_made, 1)
            nc.gpsimd.affine_select(out=ident[:, :], in_=ones, compare_op=ALU.is_equal, fill=0.0, base=0,
                                    pattern=[[-1, P]], channel_multiplier=1).then_inc(ident_made, 1)
            nc.gpsimd.memset(gwh[:, :, :].bitcast(F32), 0.0).then_inc(gw_zero, 1)
            nc.gpsimd.memset(gwl[:, :, :].bitcast(F32), 0.0).then_inc(gw_zero, 1)
            nc.gpsimd.memset(eps_d[:, :], EPS).then_inc(consts, 1)
            nc.gpsimd.memset(eps_s[:, :], SUBLN_EPS).then_inc(consts, 1)
            nc.gpsimd.memset(head_mean[:, :].bitcast(F32), 1.0 / P).then_inc(consts, 1)
            nc.gpsimd.memset(one_row[:, :], 1.0).then_inc(consts, 1)
            nc.gpsimd.memset(neg_row[:, 0:64], NEG).then_inc(consts, 1)
            nc.gpsimd.memset(neg_row[:, 64:P], 0.0).then_inc(consts, 1)
            nc.gpsimd.affine_select(out=causal[:, :], in_=ones, compare_op=ALU.is_ge, fill=0.0, base=0,
                                    pattern=[[1, P]], channel_multiplier=-1).then_inc(consts, 1)
            for c in range(1, CB):
                pool.wait_ge(sq_done, c + 1)
                wait(pool, acc_done, c if c > 1 else 0)
                nc.gpsimd.tensor_tensor(acc[:, :], abuf[:, :] if c == 1 else acc[:, :], (abuf, tbuf)[c % 2][:, :],
                                        ALU.add).then_inc(acc_done, 2 if c == 1 else 1)
            nc.gpsimd.memset(gone[:, :], 1.0).then_inc(consts, 1)
            pool.wait_ge(consts, 8)

            pool.wait_ge(gate_dve, 8)
            pool.dma_start(gate_rows[0:HEADS, :], gm[:, :]).then_inc(m_sent, 16)
            pool.wait_ge(gate_dve, 10)
            pool.dma_start(gate_rows[HEADS:2 * HEADS, :], gnm[:, :]).then_inc(nm_sent, 16)
            pool.wait_ge(m_sent, 16)
            def m_row(n, p):
                pool.dma_start(mbc[p][:, :], gate_rows[ds(n, 1), :].broadcast_to([P, T])).then_inc(mrow_in[p], 16)

            def nm_row(n, p):
                pool.dma_start(nmbc[p][:, :], gate_rows[ds(n + HEADS, 1), :].broadcast_to([P, T])).then_inc(nrow_in[p], 16)

            def step0(hd, par, pair):
                n1, n2 = hd + 1, hd + 2
                if exists(n2):
                    wait(pool, dpre, n1)
                    m_row(n2, par)
                if exists(n1):
                    pool.wait_ge(dexp, n1 + 1)
                    for c0, w in DIAG:
                        blk = dmat[0:w, c0:c0 + w]
                        last = nc.gpsimd.tensor_tensor(blk, blk, causal[0:w, 0:w], ALU.mult)
                    last.then_inc(dready, 1)
                if exists(n2):
                    if isinstance(hd, int) and n2 == 0:
                        pool.wait_ge(nm_sent, 16)
                    wait(pool, x_rd, n1)
                    nm_row(n2, par)

            heads_loop(pool, 2, step0, tail=0)

            pool.wait_ge(z_ready, HEADS)
            pool.dma_start(lamv[:, :, :], a["diff_lambda"][0:1].broadcast_to([P, 4, DQK])).then_inc(lamv_in, 16)
            with pool.Fori(0, HEADS) as i:
                pool.wait_ge(sq_hi1, i + 1)
                nc.gpsimd.tensor_tensor(sql1[:, :], abuf[:, NMETA:T], sqh1[:, :].bitcast(F32),
                                        ALU.subtract).then_inc(sq_lo1, 1)

        @block.scalar
        def _(act):
            def copy(o, i, scale=1.0):
                return nc.scalar.activation(o, i, ACT.Copy, scale=scale)

            def split(u, k, layer):
                if isinstance(u, int) and u >= U_END:
                    return
                if k % 2 == 0:
                    missed = 16 * MISSED[layer][k // 2]
                    act.wait_ge(raw_in[k // 2], (u - k) * 4 + (16 - missed))
                wait(act, unit_done, u - RING + 1)
                copy(wh[:, k, :, :], raw[:, k // 2, :, P * (k % 2):P * (k % 2) + P]).then_inc(split_hi, 1)

            def split_unit(u, j, layer, head):
                act.wait_ge(unit_in[j], head * 16 + (CAME[layer][j] + 1) * 16)
                if layer == 0 and j == 0:
                    act.wait_ge(half_in, head * 16 + 16)
                wait(act, unit_done, u - 2)
                copy(wh[:, j, :, :], raw[:, j // 2, :, P * (j % 2):P * (j % 2) + P]).then_inc(split_hi, 1)

            def norm_prep(n, b, spans):
                t0 = spans[0][0]
                copy(yh[:, b, t0:T], h[:, b, t0:T], gains[:, 8 * n + b:8 * n + b + 1]).then_inc(yh_done, 1)
                wait(act, acc_done, 8 * n + b if n > 0 else b - 1)
                sq = tbuf if n == 0 and b % 2 else abuf
                nc.scalar.activation(sq[:, t0:T], h[:, b, t0:T], ACT.Square).then_inc(sq_done, 1)

            def norm_factor(n, spans, bank=B_SUM):
                act.wait_ge(sum_done, n + 1)
                src = ps[:, bank:bank + 2, 0:HALF] if len(spans) == 2 else ps[:, bank, 0:X]
                nc.scalar.activation(tokens(rb[:, :], spans), src, ACT.Ln, bias=eps_d[:, 0:1], scale=1.0 / D).then_inc(ln_done, 1)
                act.wait_ge(ln_done, n + 1)
                nc.scalar.activation(tokens(rb[:, :], spans), tokens(rb[:, :], spans), ACT.Exp, scale=-0.5).then_inc(rb_ready, 1)

            nc.scalar.preload_act_table_set("natural_log_exp_and_others")
            act.dma_start(gain_rows[:, :], a["norm_gains"].rearrange("l n (c p) -> (l n c) p", p=P)).then_inc(gains_in, 16)
            act.dma_start(meta_in[:, :], a["meta_tokens"]).then_inc(meta_come, 16)
            for n, (name, first) in enumerate((("mlstm_head_gain", "l"), ("diff_head_gain", "l"), ("final_gain", ""))):
                src = a[name].rearrange("l (c p) -> (l c) p" if first else "(c p) -> c p", p=P)
                act.dma_start(more_rows[8 * n:8 * n + 8, :], src).then_inc(more_in, 16)
            act.wait_ge(meta_t0, 1)
            copy(h[:, :, 0:NMETA], ps[:, 7, 0:P].rearrange("p (c t) -> p c t", t=NMETA)).then_inc(hm_rd, 1)
            act.wait_ge(hm_rd, 1)
            act.wait_ge(gain_rd, 1)
            for c in range(CB):
                act.wait_ge(hx_rd, c + 1)
                norm_prep(0, c, ALL)
                if c in (0, 2):
                    split_unit(c // 2, c // 2, 0, 0)
            split_unit(2, 2, 0, 0)
            norm_factor(0, ALL, 4)
            fg = slice(FG_ROW, FG_ROW + HEADS)
            act.wait_ge(gate_dve, 2)
            nc.scalar.activation(gabs[fg, :], gx[fg, :], ACT.Abs).then_inc(gate_act, 1)
            act.wait_ge(gate_act, 1)
            nc.scalar.activation(gexp[fg, :], gabs[fg, :], ACT.Exp, scale=-1.0).then_inc(gate_act, 1)
            act.wait_ge(gate_act, 2)
            nc.scalar.activation(gln[fg, :], gexp[fg, :], ACT.Ln, bias=1.0).then_inc(gate_act, 1)

            def decays(n1, par):
                act.wait_ge(dpre, n1 + 1)
                d = dmat
                nc.scalar.activation(d[:, 0:D_FULL], d[:, 0:D_FULL], ACT.Exp, scale=-1.0)
                nc.scalar.activation(d[0:16, D_FULL:DW], d[0:16, D_FULL:DW], ACT.Exp, scale=-1.0).then_inc(dexp, 1)

            def row(par, pair):
                act.wait_ge(nrow_in[1 - par], pair * 16 + 16 * (par + 1))
                nc.scalar.activation(nmbc[1 - par][:, :], nmbc[1 - par][:, :], ACT.Exp, scale=2.0).then_inc(emn_done, 1)

            def step0(hd, par, pair):
                n1, nxt = hd + 1, exists(hd + 1)
                first = isinstance(hd, int) and hd < 0
                if exists(hd):
                    wait(act, den_done, hd)
                    for n, (c0, c1) in enumerate(P_CUTS):
                        act.wait_ge(p_done, hd * len(P_CUTS) + (n + 1))
                        rows = 16 if c0 == D_FULL else P
                        copy(phi[0:rows, c0:c1], dmat[0:rows, c0:c1]).then_inc(ph_done, 1)
                if exists(hd):
                    act.wait_ge(evac, hd * 3 + 3)
                    wait(act, w_done, hd)
                    nc.scalar.activation(tbuf[:, :], of[par][:, :], ACT.Abs).then_inc(lsig, 1)
                    act.wait_ge(lsig, hd * 3 + 1)
                    nc.scalar.activation(tbuf[:, :], tbuf[:, :], ACT.Exp, scale=-1.0).then_inc(lsig, 1)
                    act.wait_ge(lsig, hd * 3 + 2)
                    nc.scalar.activation(tbuf[:, :], tbuf[:, :], ACT.Ln, bias=1.0).then_inc(lsig, 1)
                if nxt:
                    act.wait_ge(evac, n1 * 3 + 1)
                    wait(act, s_done, hd)
                    copy(ks[1 - par][0:64, :], qkf[64:128, :])
                    copy(qhs[1 - par][0:64, :], qkf[0:64, :])
                    copy(qhs[1 - par][64:128, :], qkf[0:64, :]).then_inc(stack_hi, 1)
                    if first:
                        act.wait_ge(u_t, 1)
                        copy(ucol[:, 0:4, :], ps[:, B_SUM, 0:32].rearrange("p (s g) -> p s g", s=4))
                        copy(ucol[0:16, 4, :], ps[0:16, B_SUM, 32:40])
                        copy(gains[:, 32:56], ps[:, B_SUM, 64:88]).then_inc(ucol_rd, 1)
                    else:
                        decays(n1, par)
                        split_unit(n1 * 3 + 2, 2, 0, n1)
                    split_unit(n1 * 3 + 3, 0, 0, n1 + 1)
                elif exists(hd):
                    act.wait_ge(unit_done, U_OUT0)
                    split(U_OUT0 + 2, 2, 0)
                    split(U_OUT0 + 3, 3, 0)
                if exists(hd):
                    act.wait_ge(pv_done, hd + 1)
                    wait(act, z_ready, hd)
                    wait(act, ssq_done, hd)
                    for b, t0, t1 in ((B_ND, 0, QSPLIT), (B_ND + 1, QSPLIT, T)):
                        copy(nf[:, t0:t1], ps[:, b, 0:t1 - t0], gains[:, ds(hd + 32, 1)])
                        last = nc.scalar.activation(abuf[:, t0:t1], ps[:, b, 0:t1 - t0], ACT.Square)
                    last.then_inc(num_rd, 1)
                    act.wait_ge(num_rd, hd + 1)
                    copy(sqh[:, :], abuf[:, :]).then_inc(sq_hi, 1)
                if nxt:
                    if not first:
                        row(par, pair)
                        split_unit(n1 * 3 + 4, 1, 0, n1 + 1)
                if exists(hd):
                    act.wait_ge(den_done, hd + 1)
                    nc.scalar.activation(acc[:, 0:QSPLIT], ps[:, B_ND, 0:QSPLIT], ACT.Square)
                    nc.scalar.activation(acc[:, QSPLIT:T], ps[:, B_ND + 1, 0:T - QSPLIT], ACT.Square).then_inc(den_sq, 1)
                    act.wait_ge(t_rd, hd + 1)
                    nc.scalar.activation(acc[:, :], acc[:, :], ACT.Ln).then_inc(hln_done, 1)
                    act.wait_ge(e_done, hd + 1)
                    nc.scalar.activation(acc[:, :], acc[:, :], ACT.Exp).then_inc(rs_rd, 1)
                if nxt:
                    act.wait_ge(v_t, n1 + 1)
                    wait(act, pv_done, hd)
                    copy(vh[1 - par][:, 0:4, :], ps[:, B_ND, :].rearrange("p (s e) -> p s e", e=P))
                    copy(vh[1 - par][0:16, 4, :], ps[0:16, B_ND + 1, 0:P]).then_inc(vh_done, 1)
                if first:
                    split_unit(4, 1, 0, 1)
                    decays(0, 1)
                    row(1, -1)
                if exists(hd):
                    act.wait_ge(z_mul, hd + 1)
                    copy(ah[:, ds(hd, 1), :].rearrange("p o t -> p (o t)"), nf[:, :]).then_inc(zh_rd, 1)

            heads_loop(act, 1, step0, tail=0)

            def out_product(layer, base, n, spans):
                for k in range(8):
                    if k < 6:
                        split(base + k + 4, k % 4, layer)
                    act.wait_ge(h_ready, base_h(n) + k + 1)
                    norm_prep(n, k, spans)

            def base_h(n):
                return 8 * (n - 1)

            def up_units(layer, base, g_all, spans, factor=None):
                t0 = spans[0][0]
                for k in range(8):
                    split(base + (k + AHEAD), (k + AHEAD) % 4, layer)
                    if factor is not None and k == 0:
                        norm_factor(factor, spans)
                    act.wait_ge(relu_done, g_all * 8 + (k + 1))
                    nc.scalar.activation(abuf[:, t0:T], tbuf[:, t0:T], ACT.Square).then_inc(sqa_done, 1)
                    nc.scalar.activation(ah[:, k, t0:T], tbuf[:, t0:T], ACT.Square).then_inc(ah_done, 1)

            def mlp(layer, base, spans):
                g0 = 4 * layer
                up_units(layer, base, g0, spans, factor=2 * layer + 1)
                for k in range(8):
                    split(base + 8 + k + AHEAD, (k + AHEAD) % 4, layer)
                with act.Fori(1, GROUPS - 1) as g:
                    up_units(layer, g * 16 + base, g + g0, spans)
                    for k in range(8):
                        split(g * 16 + (base + 8 + k + AHEAD), (k + AHEAD) % 4, layer)
                last = base + 16 * (GROUPS - 1)
                up_units(layer, last, g0 + GROUPS - 1, spans)
                for k in range(8):
                    if layer == 0 and k >= 8 - AHEAD:
                        split_unit(U_IN1 + k + AHEAD - 8, k + AHEAD - 8, 1, 0)
                    else:
                        split(last + 8 + k + AHEAD, (k + AHEAD) % 4, layer)
                    if layer == 0:
                        act.wait_ge(h_ready, base_h(2) + k + 1)
                        norm_prep(2, k, ALL)
                    else:
                        act.wait_ge(h_ready, base_h(4) + k + 1)
                        wait(act, acc_done, 32 + k)
                        nc.scalar.activation(abuf[:, NMETA:T], h[:, k, NMETA:T], ACT.Square).then_inc(sq_done, 1)
                        copy(hg[:, k, :], h[:, k, NMETA:T], gains[:, 48 + k:49 + k]).then_inc(hg_done, 1)

            out_product(0, U_OUT0, 1, ALL)
            act.wait_ge(lam_dve, 2)
            nc.scalar.activation(lam[:, 2:4], lam[:, 0:2], ACT.Exp).then_inc(lam_act, 1)
            mlp(0, U_MLP0, ALL)

            split_unit(U_IN1 + 2, 2, 1, 0)
            norm_factor(2, ALL)

            def scores(n, i, c):
                act.wait_ge(max_done[c], n + 1)
                if c == 0:
                    wait(act, attn_rd, n - 1)
                w = NMETA + P * (i + 1)
                b = B_SC[c]
                src = ps[:, b, 0:w] if i < 3 else ps[:, b:b + 2, 0:HALF]
                e = es[c][i % 2]
                dst = e[:, 0:w] if i < 3 else halves(e[:, :])
                nc.scalar.activation(dst, src, ACT.Exp, bias=stat[:, i % 2, c:c + 1],
                                     accum_out=stat[:, i % 2, 2 + c:3 + c]).then_inc(exp_done[c], 1)

            def turned(hd, n, i):
                act.wait_ge(at_t, n + 1)
                if i == 0:
                    wait(act, pv_done1, hd)
                copy(att[:, 0:i + 1, P * i:P * (i + 1)],
                     ps[:, B_TR1, 0:P * (i + 1)].rearrange("p (s t) -> p s t", t=P)).then_inc(at_rd, 1)

            def keys_hi(par, c):
                k = kf1[64 * c:64 * c + 64, :]
                copy(khs[1 - par][c][0:64, :], k)
                copy(khs[1 - par][c][64:128, :], k).then_inc(khi_done, 1)

            def step1(hd, par, pair):
                n1 = hd + 1
                if exists(hd - 1):
                    turned(hd - 1, hd * 4 - 1, 3)
                if exists(hd):
                    scores(hd * 4, 0, 0)
                    scores(hd * 4, 0, 1)
                if exists(hd):
                    act.wait_ge(v_t1, hd + 1)
                    copy(vth1[par][:, 0:4, :], ps[:, B_TR1, :].rearrange("p (s e) -> p s e", e=P))
                    copy(vth1[par][0:16, 4, :], ps[0:16, B_TR1 + 1, 0:P]).then_inc(vt_rd1, 1)
                    if exists(n1):
                        split_unit(n1 * 3 + (U_IN1 + 2), 2, 1, n1)
                    else:
                        act.wait_ge(unit_done, U_OUT1)
                        split(U_OUT1 + 2, 2, 1)
                if exists(hd - 1):
                    act.wait_ge(meta_t, hd)
                    copy(att_meta[:, :], ps[0:NMETA, B_TR1, :]).then_inc(meta_rd, 1)
                if exists(hd):
                    for c in range(2):
                        scores(hd * 4 + 1, 1, c)
                if exists(hd - 1):
                    act.wait_ge(pv_done1, hd)
                    wait(act, z_ready, hd + (HEADS - 1))
                    copy(zf[:, :], ps[:, B_PV1, :], gains[:, ds(hd + 39, 1)])
                    nc.scalar.activation(abuf[:, NMETA:T], ps[:, B_PV1, :], ACT.Square).then_inc(pv_rd1, 1)
                    act.wait_ge(pv_rd1, hd)
                    copy(sqh1[:, :], abuf[:, NMETA:T]).then_inc(sq_hi1, 1)
                if exists(hd):
                    turned(hd, hd * 4, 0)
                if exists(n1):
                    act.wait_ge(evac, n1 * 3 + (U_IN1 + 1))
                    wait(act, sc_done[1], hd * 4)
                    for c in range(2):
                        b0 = 64 * c
                        last = copy(qst[1 - par][c][b0:b0 + 64, :], qf1[b0:b0 + 64, NMETA:T], SCORE_SCALE)
                    last.then_inc(qhi_done, 1)
                    split_unit(n1 * 3 + (U_IN1 + 3), 0, 1, n1 + 1)
                elif exists(hd):
                    split(U_OUT1 + 3, 3, 1)
                if exists(hd):
                    for c in range(2):
                        scores(hd * 4 + 2, 2, c)
                    turned(hd, hd * 4 + 1, 1)
                if exists(n1):
                    act.wait_ge(evac, n1 * 3 + (U_IN1 + 2))
                    keys_hi(par, 0)
                if exists(hd):
                    for c in range(2):
                        scores(hd * 4 + 3, 3, c)
                if exists(n1):
                    keys_hi(par, 1)
                if exists(hd):
                    turned(hd, hd * 4 + 2, 2)
                if exists(hd - 1):
                    act.wait_ge(ssq_done1, hd)
                    nc.scalar.activation(acc[:, NMETA:T], ps[:, B_PV1, :], ACT.Ln, bias=eps_s[:, 0:1]).then_inc(hln_done1, 1)
                    act.wait_ge(hln_done1, hd)
                    nc.scalar.activation(acc[:, NMETA:T], acc[:, NMETA:T], ACT.Exp, scale=-0.5).then_inc(rs_rd1, 1)
                if exists(n1):
                    split_unit(n1 * 3 + (U_IN1 + 4), 1, 1, n1 + 1)
                if exists(hd - 1):
                    act.wait_ge(z_mul1, hd)
                    copy(ah[:, ds(hd - 1, 1), NMETA:T].rearrange("p o t -> p (o t)"), zf[:, :]).then_inc(zh_rd1, 1)

            heads_loop(act, 1, step1)
            out_product(1, U_OUT1, 3, SEQ)
            mlp(1, U_MLP1, SEQ)

            act.wait_ge(fsum, 1)
            nc.scalar.activation(lam[:, 0:4], ps[:, 0, 0:4], ACT.Ln, bias=eps_d[:, 0:1], scale=1.0 / D).then_inc(fln, 1)
            act.wait_ge(fln, 1)
            nc.scalar.activation(lam[:, 0:4], lam[:, 0:4], ACT.Exp, scale=-0.5).then_inc(frs, 1)
            act.wait_ge(frs, 1)
            for i in range(4):
                act.wait_ge(out_t[0], i + 1)
                copy(fin[:, i, 0:X], ps[:, OUT_BANKS[i][0], :], lam[:, i:i + 1]).then_inc(fmul_act, 1)

        @block.vector
        def _(dve):
            V = nc.vector

            def split(u, k):
                if isinstance(u, int) and u >= U_END:
                    return
                dve.wait_ge(split_hi, u + 1)
                V.tensor_tensor(wl[:, k, :, :], raw[:, k // 2, :, P * (k % 2):P * (k % 2) + P],
                                wh[:, k, :, :].bitcast(F32), ALU.subtract).then_inc(split_lo, 1)

            def norm_prep(n, b, spans):
                t0 = spans[0][0]
                dve.wait_ge(yh_done, 8 * n + b + 1)
                V.scalar_tensor_tensor(yl[:, b, t0:T], h[:, b, t0:T], gains[:, 8 * n + b:8 * n + b + 1],
                                       yh[:, b, t0:T].bitcast(F32), ALU.mult, ALU.subtract).then_inc(y_ready, 1)
                dve.wait_ge(sq_done, 8 * n + b + 1)
                if b == 0:
                    V.tensor_copy(acc[:, t0:T], abuf[:, t0:T]).then_inc(acc_done, 1)
                else:
                    dve.wait_ge(acc_done, 8 * n + b)
                    V.tensor_tensor(acc[:, t0:T], acc[:, t0:T], abuf[:, t0:T], ALU.add).then_inc(acc_done, 1)

            def scaled(u, k, spans, dest, src=None):
                dve.wait_ge(unit_done, u + 1)
                V.tensor_tensor(tokens(dest, spans), src or banks(k, spans), tokens(rb[:, :], spans), ALU.mult).then_inc(evac, 1)

            dve.wait_ge(gain_t, 1)
            V.tensor_copy(gains[:, 0:32], ps[:, 6, 0:32]).then_inc(gain_rd, 1)

            def x_out(c):
                dve.wait_ge(x_t, c + 1)
                V.tensor_copy(h[:, c, NMETA:T], ps[:, 4 + c % 2, :]).then_inc(hx_rd, 1)

            x_out(0)
            x_out(1)
            dve.wait_ge(small_in, 3 * 16)
            dve.wait_ge(gw_zero, 2)
            V.tensor_copy(gwh[:, :, 0:HEADS], graw[:, :, 0:HEADS])
            V.tensor_copy(gwh[:, :, FG_ROW:FG_ROW + HEADS], graw[:, :, HEADS:2 * HEADS]).then_inc(gwh_done, 1)
            dve.wait_ge(gwh_done, 1)
            V.tensor_tensor(gwl[:, :, 0:HEADS], graw[:, :, 0:HEADS], gwh[:, :, 0:HEADS].bitcast(F32), ALU.subtract)
            V.tensor_tensor(gwl[:, :, FG_ROW:FG_ROW + HEADS], graw[:, :, HEADS:2 * HEADS],
                            gwh[:, :, FG_ROW:FG_ROW + HEADS].bitcast(F32), ALU.subtract).then_inc(gw_ready, 1)
            for c in range(CB):
                dve.wait_ge(yh_done, c + 1)
                V.scalar_tensor_tensor(yl[:, c, :], h[:, c, :], gains[:, c:c + 1], yh[:, c, :].bitcast(F32),
                                       ALU.mult, ALU.subtract).then_inc(y_ready, 1)
                if c in (1, 3):
                    split(c // 2, c // 2)
                if c + 2 < CB:
                    x_out(c + 2)

            ig, fg = slice(0, HEADS), slice(FG_ROW, FG_ROW + HEADS)
            split(2, 2)
            dve.wait_ge(rb_ready, 1)
            dve.wait_ge(gate_mm, 1)
            V.tensor_tensor(halves(gx[fg, :]), ps[fg, 6:8, 0:HALF], halves(rb[fg, :]), ALU.mult).then_inc(gate_dve, 1)
            dve.wait_ge(gate_dve, 1)
            V.tensor_scalar(gx[fg, :], gx[fg, :], bias_f[fg, 0:1], None, ALU.add).then_inc(gate_dve, 1)
            V.tensor_tensor(halves(gi[:, :]), ps[ig, 6:8, 0:HALF], halves(rb[ig, :]), ALU.mult).then_inc(gate_dve, 1)
            dve.wait_ge(gate_dve, 3)
            V.tensor_scalar(gi[:, :], gi[:, :], bias_i[:, 0:1], None, ALU.add).then_inc(gate_dve, 1)
            dve.wait_ge(gate_act, 3)
            V.scalar_tensor_tensor(glf[ig, :], gx[fg, :], 0.0, gln[fg, :], ALU.min, ALU.subtract).then_inc(gate_dve, 1)
            dve.wait_ge(gate_dve, 5)
            dve.wait_ge(consts, 8)
            V.tensor_tensor_scan(gb[:, :], gone[ig, :], glf[ig, :], 0.0, ALU.mult, ALU.add).then_inc(gate_dve, 1)
            dve.wait_ge(gate_dve, 6)
            V.tensor_tensor(gu[:, :], gi[:, :], gb[:, :], ALU.subtract).then_inc(gate_dve, 1)
            dve.wait_ge(gate_dve, 7)
            V.tensor_tensor_scan(gm[:, :], gu[:, :], gu[:, :], 0.0, ALU.max, ALU.max).then_inc(gate_dve, 1)
            dve.wait_ge(gate_dve, 8)
            V.tensor_tensor(gnm[:, :], gb[:, :], gm[:, :], ALU.add).then_inc(gate_dve, 1)
            dve.wait_ge(gate_dve, 9)
            V.tensor_scalar(gnm[:, :], gnm[:, :], -1.0, NM_MAX, ALU.mult, ALU.min).then_inc(gate_dve, 1)

            def blk(t, j):
                return t[:, ds(j, 1), :].rearrange("p o t -> p (o t)")

            def exponents(n1, par, pair):
                wait(dve, p_ready, n1)
                dve.wait_ge(mrow_in[1 - par], pair * 16 + 16 * (par + 1))
                for n, (j, t0, t1, _, _) in enumerate(PIECES):
                    rows = TILES0[j][1]
                    last = V.tensor_scalar(dmat[0:rows, DCOL[n]:DCOL[n + 1]], mbc[1 - par][0:rows, t0:t1],
                                           ucol[0:rows, j, ds(n1, 1)], 0.0, ALU.subtract, ALU.max)
                last.then_inc(dpre, 1)

            def step0(hd, par, pair):
                n1, nxt = hd + 1, exists(hd + 1)
                first = isinstance(hd, int) and hd < 0
                if exists(hd):
                    dve.wait_ge(s_done, hd + 1)
                    dve.wait_ge(dready, hd + 1)
                    dm = dmat
                    for n, (b, w, c0) in enumerate(P_BANKS):
                        ins = V.scalar_tensor_tensor(dm[:, c0:c0 + w], ps[:, b, 0:w], SCORE_SCALE, dm[:, c0:c0 + w],
                                                     ALU.mult, ALU.mult)
                        if n in (1, 3):
                            ins.then_inc(p_done, 1)
                    V.scalar_tensor_tensor(dm[0:16, D_FULL:DW], ps[0:16, B_S0 + 3, 272:288], SCORE_SCALE,
                                           dm[0:16, D_FULL:DW], ALU.mult, ALU.mult).then_inc(p_done, 1)
                    wait(dve, den_done, hd)
                    for n, (c0, c1) in enumerate(P_CUTS):
                        rows = 16 if c0 == D_FULL else P
                        dve.wait_ge(ph_done, hd * len(P_CUTS) + (n + 1))
                        last = V.tensor_tensor(plo[0:rows, c0:c1], dm[0:rows, c0:c1],
                                               phi[0:rows, c0:c1].bitcast(F32), ALU.subtract)
                    last.then_inc(p_ready, 1)
                    if nxt:
                        scaled(n1 * 3, 0, ALL, qkf[:, :])
                    dve.wait_ge(lsig, hd * 3 + 3)
                    V.scalar_tensor_tensor(of[par][:, :], of[par][:, :], 0.0, tbuf[:, :], ALU.min, ALU.subtract).then_inc(w_done, 1)
                if nxt:
                    if not first:
                        exponents(n1, par, pair)
                    if first:
                        scaled(0, 0, ALL, qkf[:, :])
                        scaled(1, 1, ALL, vf0[:, :])
                        scaled(2, 0, ALL, of[0][:, :], ps[:, 4:6, 0:HALF])
                    dve.wait_ge(stack_hi, n1 + 1)
                    q, k = qkf[0:64, :], qkf[64:128, :]
                    V.tensor_tensor(ks[1 - par][64:128, :], k, ks[1 - par][0:64, :].bitcast(F32), ALU.subtract)
                    V.tensor_tensor(qls[1 - par][0:64, :], q, qhs[1 - par][0:64, :].bitcast(F32), ALU.subtract)
                    V.tensor_tensor(qls[1 - par][64:128, :], q, qhs[1 - par][0:64, :].bitcast(F32),
                                    ALU.subtract).then_inc(stack_lo, 1)
                    if not first:
                        split(n1 * 3 + 2, 2)
                    split(n1 * 3 + 3, 0)
                    if not first:
                        wait(dve, v_t, n1)
                        scaled(n1 * 3 + 1, 0, ALL, vf0[:, :])
                        split(n1 * 3 + 4, 1)
                elif exists(hd):
                    split(U_OUT0 + 2, 2)
                    split(U_OUT0 + 3, 3)
                if exists(hd):
                    dve.wait_ge(sq_hi, hd + 1)
                    V.tensor_tensor(sql[:, :], abuf[:, :], sqh[:, :].bitcast(F32), ALU.subtract).then_inc(sq_lo, 1)
                    dve.wait_ge(den_sq, hd + 1)
                    dve.wait_ge(emn_done, hd + 1)
                    V.tensor_tensor(acc[:, :], acc[:, :], nmbc[par][:, :], ALU.max).then_inc(x_rd, 1)
                    dve.wait_ge(ssq_done, hd + 1)
                    dve.wait_ge(x_rd, hd + 1)
                    V.scalar_tensor_tensor(acc[:, 0:QSPLIT], acc[:, 0:QSPLIT], EPS, ps[:, B_ND, 0:QSPLIT],
                                           ALU.mult, ALU.add)
                    V.scalar_tensor_tensor(acc[:, QSPLIT:T], acc[:, QSPLIT:T], EPS, ps[:, B_ND + 1, 0:T - QSPLIT],
                                           ALU.mult, ALU.add).then_inc(t_rd, 1)
                    dve.wait_ge(hln_done, hd + 1)
                    dve.wait_ge(w_done, hd + 1)
                    V.scalar_tensor_tensor(acc[:, :], acc[:, :], -0.5, of[par][:, :], ALU.mult, ALU.add).then_inc(e_done, 1)
                if nxt and not first:
                    scaled(n1 * 3 + 2, 0, ALL, of[1 - par][:, :])
                if first:
                    dve.wait_ge(ucol_rd, 1)
                    exponents(0, 1, -1)
                    split(4, 1)
                if exists(hd):
                    dve.wait_ge(rs_rd, hd + 1)
                    V.tensor_tensor(nf[:, :], nf[:, :], acc[:, :], ALU.mult).then_inc(z_mul, 1)
                if nxt:
                    dve.wait_ge(vh_done, n1 + 1)
                    V.tensor_tensor(vl[1 - par][:, 0:4, :], ps[:, B_ND, :].rearrange("p (s e) -> p s e", e=P),
                                    vh[1 - par][:, 0:4, :].bitcast(F32), ALU.subtract)
                    V.tensor_tensor(vl[1 - par][0:16, 4, :], ps[0:16, B_ND + 1, 0:P],
                                    vh[1 - par][0:16, 4, :].bitcast(F32), ALU.subtract).then_inc(vl_done, 1)
                if exists(hd):
                    dve.wait_ge(zh_rd, hd + 1)
                    V.tensor_tensor(blk(al, hd), nf[:, :], blk(ah, hd).bitcast(F32), ALU.subtract).then_inc(z_ready, 1)

            heads_loop(dve, 1, step0, tail=0)

            def residual(u, k, b, spans, ready=None, src=None):
                dve.wait_ge(unit_done, u + 1)
                ins = V.tensor_tensor(tokens(h[:, b, :], spans), src or banks(k, spans), tokens(h[:, b, :], spans), ALU.add)
                ins.then_inc(evac, 1)
                if ready is not None:
                    dve.wait_ge(evac, u + 1)
                    V.nop().then_inc(h_ready, 1)

            def out_product(base, n, spans):
                for k in range(8):
                    residual(base + k, k, k, spans, ready=n, src=ps[:, 2 * (k % 4):2 * (k % 4) + 2, 0:HALF] if n == 1 else None)
                    if k < 6:
                        split(base + k + 4, k % 4)
                    norm_prep(n, k, spans)

            def up_units(base, spans, g_all, factor=None):
                t0 = spans[0][0]
                for k in range(8):
                    split(base + (k + AHEAD), (k + AHEAD) % 4)
                    if factor is not None and k == 0:
                        dve.wait_ge(rb_ready, factor + 1)
                    dve.wait_ge(unit_done, base + (k + 1))
                    V.scalar_tensor_tensor(tokens(tbuf[:, :], spans), banks(k, spans), 0.0, tokens(rb[:, :], spans),
                                           ALU.max, ALU.mult).then_inc(evac, 1)
                    dve.wait_ge(evac, base + (k + 1))
                    V.nop().then_inc(relu_done, 1)
                    dve.wait_ge(ah_done, g_all * 8 + (k + 1))
                    V.tensor_tensor(al[:, k, t0:T], abuf[:, t0:T], ah[:, k, t0:T].bitcast(F32), ALU.subtract).then_inc(a_ready, 1)

            def down_units(base, spans):
                for k in range(8):
                    split(base + (k + AHEAD), (k + AHEAD) % 4)
                    residual(base + k, k, k, spans)

            def mlp(layer, base, spans):
                g0 = 4 * layer
                up_units(base, spans, g0, factor=2 * layer + 1)
                down_units(base + 8, spans)
                with dve.Fori(1, GROUPS - 1) as g:
                    up_units(g * 16 + base, spans, g + g0)
                    down_units(g * 16 + (base + 8), spans)
                last = base + 16 * (GROUPS - 1)
                up_units(last, spans, g0 + GROUPS - 1)
                for k in range(8):
                    split(last + 8 + k + AHEAD, (k + AHEAD) % 4)
                    residual(last + 8 + k, k, k, spans, ready=layer,
                             src=ps[:, LAST_BANKS[k], :] if layer == 1 else None)
                    if layer == 0:
                        norm_prep(2, k, ALL)
                    else:
                        dve.wait_ge(sq_done, 32 + k + 1)
                        if k == 0:
                            V.tensor_copy(acc[:, NMETA:T], abuf[:, NMETA:T]).then_inc(acc_done, 1)
                        else:
                            dve.wait_ge(acc_done, 32 + k)
                            V.tensor_tensor(acc[:, NMETA:T], acc[:, NMETA:T], abuf[:, NMETA:T], ALU.add).then_inc(acc_done, 1)

            out_product(U_OUT0, 1, ALL)
            dve.wait_ge(lamv_in, 16)
            V.tensor_tensor(lamv[:, 0, :], lamv[:, 0, :], lamv[:, 1, :], ALU.mult)
            V.tensor_tensor(lamv[:, 2, :], lamv[:, 2, :], lamv[:, 3, :], ALU.mult).then_inc(lam_dve, 1)
            dve.wait_ge(lam_dve, 1)
            V.tensor_reduce(lam[:, 0:2], lamv[:, :, :].rearrange("p (a b) d -> p a b d", b=2)[:, :, 0, :], AX.X, ALU.add).then_inc(lam_dve, 1)
            dve.wait_ge(lam_act, 1)
            V.scalar_tensor_tensor(lam[:, 4:5], lam[:, 3:4], -LAMBDA_INIT, lam[:, 2:3], ALU.add, ALU.subtract).then_inc(lam_dve, 1)
            V.tensor_scalar(gains[:, 40:48], gains[:, 40:48], 1.0 - LAMBDA_INIT, None, ALU.mult).then_inc(lam_dve, 1)
            dve.wait_ge(lam_dve, 4)

            mlp(0, U_MLP0, ALL)

            split(U_IN1 + 2, 2)
            dve.wait_ge(rb_ready, 3)
            def maxima(n, i):
                for c in range(2):
                    dve.wait_ge(sc_done[c], n + 1)
                    w = NMETA + P * (i + 1)
                    if i < 3:
                        V.tensor_reduce(stat[:, i % 2, c:c + 1], ps[:, B_SC[c], 0:w], AX.X, ALU.max,
                                        negate=True).then_inc(max_done[c], 1)
                    else:
                        V.tensor_reduce(stat[:, i % 2, c:c + 1], ps[:, B_SC[c]:B_SC[c] + 2, 0:HALF], AX.XY, ALU.max,
                                        negate=True).then_inc(max_done[c], 1)

            def weights(hd, n, i):
                w = NMETA + P * (i + 1)
                dve.wait_ge(exp_done[0], n + 1)
                dve.wait_ge(exp_done[1], n + 1)
                V.reciprocal(stat[:, i % 2, 4:6], stat[:, i % 2, 2:4]).then_inc(rden_rd, 1)
                dve.wait_ge(rden_rd, n + 1)
                e = es[0][i % 2], es[1][i % 2]
                V.tensor_scalar(e[1][:, 0:w], e[1][:, 0:w], stat[:, i % 2, 5:6], lam[:, 4:5], ALU.mult, ALU.mult).then_inc(e1_rd, 1)
                dve.wait_ge(e1_rd, n + 1)
                wait(dve, at_t, n - 3)
                if i == 0:
                    wait(dve, meta_t, hd)
                V.scalar_tensor_tensor(attn[:, i, 0:w], e[0][:, 0:w], stat[:, i % 2, 4:5], e[1][:, 0:w],
                                       ALU.mult, ALU.add).then_inc(attn_rd, 1)

            def keys_lo(n1, par, c):
                dve.wait_ge(khi_done, n1 * 2 + (c + 1))
                for b in (0, 64):
                    last = V.tensor_tensor(kls[1 - par][c][b:b + 64, :], kf1[64 * c:64 * c + 64, :],
                                           khs[1 - par][c][0:64, :].bitcast(F32), ALU.subtract)
                last.then_inc(klo_done, 1)

            def step1(hd, par, pair):
                n1 = hd + 1
                if exists(hd):
                    maxima(hd * 4, 0)
                    weights(hd, hd * 4, 0)
                if exists(n1) and exists(hd):
                    split(n1 * 3 + (U_IN1 + 2), 2)
                elif exists(hd):
                    split(U_OUT1 + 2, 2)
                if exists(hd):
                    maxima(hd * 4 + 1, 1)
                    weights(hd, hd * 4 + 1, 1)
                if exists(n1):
                    scaled(n1 * 3 + U_IN1, 0, SEQ, qf1[:, :],
                           ps[:, 4 if isinstance(hd, int) and hd < 0 else B_Q1, :])
                    split(n1 * 3 + (U_IN1 + 3), 0)
                    dve.wait_ge(qhi_done, n1 + 1)
                    for c in range(2):
                        b0, b1 = 64 * c, 64 - 64 * c
                        last = V.scalar_tensor_tensor(qst[1 - par][c][b1:b1 + 64, :], qf1[b0:b0 + 64, NMETA:T], SCORE_SCALE,
                                                      qst[1 - par][c][b0:b0 + 64, :].bitcast(F32), ALU.mult, ALU.subtract)
                    last.then_inc(qlo_done, 1)
                elif exists(hd):
                    split(U_OUT1 + 3, 3)
                if exists(hd):
                    maxima(hd * 4 + 2, 2)
                    weights(hd, hd * 4 + 2, 2)
                if exists(n1):
                    scaled(n1 * 3 + (U_IN1 + 1), 0, ALL, kf1[:, :])
                if exists(hd):
                    maxima(hd * 4 + 3, 3)
                if exists(n1):
                    keys_lo(n1, par, 0)
                if exists(hd):
                    weights(hd, hd * 4 + 3, 3)
                if exists(n1):
                    keys_lo(n1, par, 1)
                if exists(hd - 1):
                    dve.wait_ge(rs_rd1, hd)
                    V.tensor_tensor(zf[:, :], zf[:, :], acc[:, NMETA:T], ALU.mult).then_inc(z_mul1, 1)
                if exists(n1):
                    wait(dve, v_t1, n1)
                    scaled(n1 * 3 + (U_IN1 + 2), 0, ALL, vf1[:, :],
                           ps[:, 2:4, 0:HALF] if isinstance(hd, int) and hd < 0 else None)
                    split(n1 * 3 + (U_IN1 + 4), 1)
                if exists(hd - 1):
                    dve.wait_ge(zh_rd1, hd)
                    V.tensor_tensor(blk(al, hd - 1)[:, NMETA:T], zf[:, :], blk(ah, hd - 1)[:, NMETA:T].bitcast(F32),
                                    ALU.subtract).then_inc(z_ready, 1)

            heads_loop(dve, 1, step1)
            out_product(U_OUT1, 3, SEQ)
            mlp(1, U_MLP1, SEQ)

            dve.wait_ge(frs, 1)
            for i in range(4):
                dve.wait_ge(out_t[1], i + 1)
                V.tensor_scalar(fin[:, i, X:D], ps[:, OUT_BANKS[i][1], :], lam[:, i:i + 1], None, ALU.mult).then_inc(fmul_dve, 1)

        @block.tensor
        def _(pe):
            mm = nc.tensor.matmul

            def blocks(u, slot, mh, ml, spans, bank, free, kb0=0, kb1=CB, block_wait=None):
                if kb0 == 0:
                    pe.wait_ge(split_lo, u + 1)
                    wait(pe, evac, free)
                for kb in range(kb0, kb1):
                    if block_wait is not None:
                        block_wait(kb)
                    for n, (w, m) in enumerate(((wh, mh), (wh, ml), (wl, mh))):
                        for s, (t0, w_) in enumerate(spans):
                            last = mm(ps[:, bank + s, 0:w_], w[:, slot, kb, :], m[:, kb, t0:t0 + w_],
                                      start=(kb == 0 and n == 0), stop=(kb == CB - 1 and n == 2))
                if kb1 == CB:
                    last.then_inc(unit_done, 1)

            def unit(u, k, mh, ml, spans, block_wait=None):
                if len(spans) == 2:
                    blocks(u, k % 4, mh, ml, spans, 2 * (k % 2), u - 1, block_wait=block_wait)
                else:
                    blocks(u, k % 4, mh, ml, spans, k % 4, u - 3, block_wait=block_wait)

            def mean_squares(n, spans, bank=B_SUM):
                pe.wait_ge(acc_done, 8 * n + 8)
                for s, (t0, w) in enumerate(spans):
                    last = mm(ps[:, bank + s, 0:w], ones, acc[:, t0:t0 + w], start=True, stop=True)
                last.then_inc(sum_done, 1)

            def y_block(n):
                return lambda kb: pe.wait_ge(y_ready, 8 * n + kb + 1)

            def z_block(layer):
                return lambda kb: pe.wait_ge(z_ready, HEADS * layer + kb + 1)

            def part0(n1, j, kb0, kb1):
                first = isinstance(n1, int) and n1 == 0
                if first and j == 2:
                    pe.wait_ge(ln_done, 1)
                blocks(n1 * 3 + j, j, yh, yl, ALL, 2 * j if first else 0, 0 if first else n1 * 3 + j, kb0, kb1)

            def out_part0(k, kb0, kb1):
                if kb0 == 0 and k > 0:
                    pe.wait_ge(p_ready, HEADS)
                blocks(U_OUT0 + k, k, ah, al, ALL, 2 * k, U_OUT0, kb0, kb1, z_block(0))

            def weighted(par, passes, done):
                seen = set()
                for n, (j, t0, t1, _, _) in enumerate(PIECES):
                    rows = TILES0[j][1]
                    b, c = (B_ND, t0) if t1 <= QSPLIT else (B_ND + 1, t0 - QSPLIT)
                    for i, (what, lo) in enumerate(passes):
                        p = (plo if lo else phi)[0:rows, DCOL[n]:DCOL[n + 1]]
                        last = mm(ps[:, b, c:c + t1 - t0], what(rows, j), p, start=(b not in seen),
                                  stop=(n in (1, len(PIECES) - 1) and i == len(passes) - 1))
                        seen.add(b)
                last.then_inc(done, 1)

            def step0(hd, par, pair):
                n1, nxt = hd + 1, exists(hd + 1)
                first = isinstance(hd, int) and hd < 0
                if exists(hd):
                    pe.wait_ge(stack_lo, hd + 1)
                    wait(pe, p_ready, hd)
                    if isinstance(hd, int) and hd == 0:
                        pe.wait_ge(evac, 3)
                    for j, t0, t1, b, c in PIECES:
                        s0, rows = TILES0[j]
                        for m, q in enumerate((qhs[par], qls[par])):
                            last = mm(ps[0:rows, b, c:c + t1 - t0], ks[par][:, s0:s0 + rows], q[:, t0:t1],
                                      start=(m == 0), stop=(m == 1))
                    last.then_inc(s_done, 1)
                if nxt and not first:
                    part0(n1, 0, 0, CB)
                elif not nxt:
                    out_part0(0, 0, 6)
                if exists(hd):
                    pe.wait_ge(p_ready, hd + 1)
                    pe.wait_ge(vl_done, hd + 1)
                    v_hi, v_lo = lambda rows, j: vh[par][0:rows, j, :], lambda rows, j: vl[par][0:rows, j, :]
                    weighted(par, ((v_hi, False), (v_hi, True), (v_lo, False)), pv_done)
                if nxt and not first:
                    part0(n1, 1, 0, CB)
                elif not nxt:
                    out_part0(1, 0, 4)
                if exists(hd):
                    pe.wait_ge(num_rd, hd + 1)
                    one = lambda rows, j: ones_r[0:rows, :]
                    weighted(par, ((one, False), (one, True)), den_done)
                if nxt:
                    part0(n1, 2, 0, 4)
                else:
                    out_part0(1, 4, 7)
                if exists(hd):
                    pe.wait_ge(den_sq, hd + 1)
                    pe.wait_ge(sq_lo, hd + 1)
                    for b, t0, t1 in ((B_ND, 0, QSPLIT), (B_ND + 1, QSPLIT, T)):
                        for m, sq in enumerate((sqh, sql)):
                            last = mm(ps[:, b, 0:t1 - t0], head_mean[:, :], sq[:, t0:t1], start=(m == 0), stop=(m == 1))
                    last.then_inc(ssq_done, 1)
                if nxt:
                    part0(n1, 2, 4, CB)
                if first:
                    pe.wait_ge(gate_dve, 7)
                    pe.wait_ge(rb_ready, 1)
                    for s, (t0, w) in enumerate(TILES0):
                        last = nc.tensor.transpose(ps[0:w, B_SUM, 8 * s:8 * s + 8], gu[:, t0:t0 + w],
                                                   ident[0:HEADS, 0:HEADS])
                    pe.wait_ge(more_in, 3 * 16)
                    nc.tensor.transpose(ps[:, B_SUM, 64:88], more_rows[:, :], ident[0:24, 0:24]).then_inc(u_t, 1)
                    pe.wait_ge(ucol_rd, 1)
                if nxt:
                    pe.wait_ge(evac, n1 * 3 + 2)
                    wait(pe, t_rd, n1)
                    for s, (t0, w) in enumerate(TILES0):
                        o = ps[:, B_ND, P * s:P * (s + 1)] if w == P else ps[0:w, B_ND + 1, 0:P]
                        last = nc.tensor.transpose(o, vf0[:, t0:t0 + w], ident[:, :])
                    last.then_inc(v_t, 1)

            def turn_x(c):
                pe.wait_ge(x_in[c // 2], 16)
                wait(pe, hx_rd, c - 1)
                for i in range(4):
                    last = nc.tensor.transpose(ps[:, 4 + c % 2, P * i:P * (i + 1)], xin[:, i, P * c:P * (c + 1)], ident[:, :])
                last.then_inc(x_t, 1)

            pe.wait_ge(ident_made, 1)
            pe.wait_ge(gains_in, 16)
            nc.tensor.transpose(ps[:, 6, 0:32], gain_rows[:, :], ident[0:32, 0:32]).then_inc(gain_t, 1)
            pe.wait_ge(meta_come, 16)
            for c in range(CB):
                last = nc.tensor.transpose(ps[:, 7, NMETA * c:NMETA * (c + 1)], meta_in[:, P * c:P * (c + 1)],
                                           ident[0:NMETA, 0:NMETA])
            last.then_inc(meta_t0, 1)
            turn_x(0)
            turn_x(1)
            pe.wait_ge(gw_ready, 1)
            pe.wait_ge(gain_rd, 1)
            pe.wait_ge(hm_rd, 1)
            for kb in range(CB):
                if kb + 2 < CB:
                    turn_x(kb + 2)
                pe.wait_ge(y_ready, kb + 1)
                for n, (w, m) in enumerate(((gwh, yh), (gwh, yl), (gwl, yh))):
                    for s, (t0, w_) in enumerate(ALL):
                        last = mm(ps[0:40, 6 + s, 0:w_], w[:, kb, :], m[:, kb, t0:t0 + w_],
                                  start=(kb == 0 and n == 0), stop=(kb == CB - 1 and n == 2))
                if kb == CB - 1:
                    last.then_inc(gate_mm, 1)
                    mean_squares(0, ALL, 4)
                if kb >= 1:
                    part0(0, 0, kb - 1, kb)
                if kb >= 4:
                    part0(0, 1, kb - 4, kb - 3)
            part0(0, 0, 7, CB)
            part0(0, 1, 4, CB)
            heads_loop(pe, 1, step0, tail=0)
            out_part0(0, 6, 7)
            out_part0(2, 0, 7)
            for k in range(3):
                out_part0(k, 7, CB)
            pe.wait_ge(t_rd, HEADS)
            for k in range(3, 8):
                blocks(U_OUT0 + k, k % 4, ah, al, ALL, 2 * (k % 4), U_OUT0 + k - 3)

            def mlp(layer, base, spans):
                g0 = 4 * layer

                def group(u0, g, first=False):
                    for k in range(8):
                        unit(u0 + k, k, yh, yl, spans, y_block(2 * layer + 1) if first and k == 0 else None)
                        if first and k == 0:
                            mean_squares(2 * layer + 1, spans)
                    for k in range(8):
                        unit(u0 + (8 + k), k, ah, al, spans,
                             (lambda kb: pe.wait_ge(a_ready, g * 8 + (kb + 1))) if k == 0 else None)

                group(base, g0, True)
                with pe.Fori(1, GROUPS - layer) as g:
                    group(g * 16 + base, g + g0)

            mlp(0, U_MLP0, ALL)

            def part(n1, j, kb0, kb1, block_wait=None):
                free = n1 * 3 + (U_IN1 + (-2, 0, 2)[j])
                first = isinstance(n1, int) and n1 == 0
                bank = B_Q1 if j == 0 else 0
                if first:
                    free, bank = (U_IN1 - 1, U_IN1 - 1, U_IN1)[j], (4, 0, 2)[j]
                blocks(n1 * 3 + (U_IN1 + j), j, yh, yl, SEQ if j == 0 else ALL, bank, free, kb0, kb1, block_wait)

            def scores(n, i, par):
                w = NMETA + P * (i + 1)
                cuts = [(0, w)] if i < 3 else ALL
                for c in range(2):
                    wait(pe, exp_done[c], n)
                    q = qst[par][c][:, P * i:P * (i + 1)]
                    for s, (t0, w_) in enumerate(cuts):
                        o = ps[:, B_SC[c] + s, 0:w_]
                        masked = s == len(cuts) - 1
                        mm(o, q, khs[par][c][:, t0:t0 + w_], start=True, stop=False)
                        last = mm(o, q, kls[par][c][:, t0:t0 + w_], start=False, stop=not masked)
                        if masked:
                            last = mm(o[:, w_ - 64:w_], neg_row[:, :], one_row[:, :], start=False, stop=True)
                    last.then_inc(sc_done[c], 1)

            def turn(n, i):
                pe.wait_ge(attn_rd, n + 1)
                wait(pe, at_rd, n)
                for s in range(i + 1):
                    last = nc.tensor.transpose(ps[:, B_TR1, P * s:P * (s + 1)],
                                               attn[:, i, NMETA + P * s:NMETA + P * (s + 1)], ident[:, :])
                last.then_inc(at_t, 1)

            def output(n, par):
                pe.wait_ge(meta_rd, n + 1)
                mm(ps[:, B_PV1, :], vth1[par][0:NMETA, 4, :], att_meta[:, :], start=True, stop=False)
                for s in range(4):
                    last = mm(ps[:, B_PV1, P * s:X], vth1[par][:, s, :], att[:, s, P * s:X], start=False, stop=(s == 3))
                last.then_inc(pv_done1, 1)

            def turn_meta(n):
                pe.wait_ge(vt_rd1, min(n + 2, HEADS) if isinstance(n, int) else n + 2)
                pe.wait_ge(at_rd, n * 4 + 4)
                for i in range(4):
                    last = nc.tensor.transpose(ps[0:NMETA, B_TR1, P * i:P * (i + 1)], attn[:, i, 0:NMETA], ident[:, :])
                last.then_inc(meta_t, 1)

            def squares(n):
                pe.wait_ge(pv_rd1, n + 1)
                pe.wait_ge(sq_lo1, n + 1)
                for m, sq in enumerate((sqh1, sql1)):
                    last = mm(ps[:, B_PV1, :], head_mean[:, :], sq[:, :], start=(m == 0), stop=(m == 1))
                last.then_inc(ssq_done1, 1)

            def out_part(k, kb0, kb1):
                if kb0 == 0 and k == 2:
                    pe.wait_ge(exp_done[0], 4 * HEADS)
                blocks(U_OUT1 + k, k, ah, al, SEQ, k, U_OUT1, kb0, kb1, z_block(1))

            def step1(hd, par, pair):
                n1, nxt = hd + 1, exists(hd + 1)
                last_head = isinstance(hd, int) and hd == HEADS - 1
                if exists(hd):
                    pe.wait_ge(qlo_done, n1)
                    pe.wait_ge(klo_done, n1 * 2)
                    if isinstance(hd, int) and hd == 0:
                        pe.wait_ge(evac, U_IN1 + 3)
                    scores(hd * 4, 0, par)
                if not exists(hd) and exists(hd - 1):
                    out_part(2, 0, 6)
                if exists(hd - 1):
                    turn(hd * 4 - 1, 3)
                if nxt:
                    if isinstance(hd, int) and hd < 0:
                        part(n1, 0, 0, CB, y_block(2))
                        mean_squares(2, ALL)
                    else:
                        part(n1, 0, 0, 2)
                elif last_head:
                    out_part(0, 0, 3)
                if exists(hd):
                    pe.wait_ge(evac, hd * 3 + (U_IN1 + 3))
                    wait(pe, at_rd, hd * 4)
                    wait(pe, hln_done1, hd - 1)
                    for s, (t0, w) in enumerate(TILES1):
                        o = ps[:, B_TR1, P * s:P * (s + 1)] if w == P else ps[0:w, B_PV1, 0:P]
                        last = nc.tensor.transpose(o, vf1[:, t0:t0 + w], ident[:, :])
                    last.then_inc(v_t1, 1)
                    if nxt:
                        part(n1, 0, 2, 5)
                    elif last_head:
                        out_part(0, 3, 5)
                if exists(hd - 1):
                    turn_meta(hd - 1)
                    if not exists(hd):
                        out_part(3, 0, 3)
                if exists(hd):
                    if nxt:
                        part(n1, 0, 5, 6)
                    scores(hd * 4 + 1, 1, par)
                if exists(hd - 1):
                    output(hd - 1, 1 - par)
                if exists(hd):
                    if nxt:
                        part(n1, 0, 6, CB)
                    elif last_head:
                        out_part(0, 5, 6)
                        out_part(1, 0, 1)
                    wait(pe, meta_rd, hd)
                    wait(pe, vt_rd1, hd + 1)
                    turn(hd * 4, 0)
                if nxt:
                    part(n1, 1, 0, 2)
                elif last_head:
                    out_part(1, 1, 3)
                if exists(hd):
                    scores(hd * 4 + 2, 2, par)
                    turn(hd * 4 + 1, 1)
                if nxt:
                    part(n1, 1, 2, CB)
                elif last_head:
                    out_part(1, 3, 5)
                if exists(hd - 1):
                    if not exists(hd):
                        out_part(3, 3, 6)
                if exists(hd):
                    if nxt:
                        pe.wait_ge(evac, n1 * 3 + (U_IN1 + 1))
                    scores(hd * 4 + 3, 3, par)
                if exists(hd - 1):
                    squares(hd - 1)
                if exists(hd):
                    turn(hd * 4 + 2, 2)
                if nxt:
                    part(n1, 2, 0, CB)
                elif last_head:
                    out_part(1, 5, 6)

            heads_loop(pe, 1, step1)
            for k in range(4):
                out_part(k, 6, 7)
            for k in range(4):
                out_part(k, 7, CB)
            for k in range(4, 8):
                unit(U_OUT1 + k, k, ah, al, SEQ)
            mlp(1, U_MLP1, SEQ)

            def turn_out(c, tiles):
                pe.wait_ge(hg_done, c + 1)
                for i in tiles:
                    last = nc.tensor.transpose(ps[:, OUT_BANKS[i][c // 4], P * (c % 4):P * (c % 4 + 1)],
                                               hg[:, c, P * i:P * (i + 1)], ident[:, :])
                    if c % 4 == 3:
                        last.then_inc(out_t[c // 4], 1)

            for k in range(8):
                unit(U_END - 16 + k, k, yh, yl, SEQ)
            for k in range(8):
                u = U_END - 8 + k
                blocks(u, k % 4, ah, al, SEQ, LAST_BANKS[k], u - 3 if k < 6 else u - 1, block_wait=
                       (lambda kb: pe.wait_ge(a_ready, 56 + kb + 1)) if k == 0 else None)
                if k >= 2:
                    turn_out(k - 2, (0, 1))
            turn_out(6, (0, 1))
            for c in range(7):
                turn_out(c, (2,))
            pe.wait_ge(evac, U_END)
            for c in range(4):
                turn_out(c, (3,))
            pe.wait_ge(acc_done, 40)
            for i in range(4):
                last = mm(ps[:, 0, i:i + 1], acc[:, NMETA + P * i:NMETA + P * (i + 1)], ones[:, 0:1], start=True, stop=True)
            last.then_inc(fsum, 1)
            turn_out(7, (0, 1, 2))
            pe.wait_ge(fln, 1)
            for c in range(4, 8):
                turn_out(c, (3,))


_INS = ["x", "meta_tokens", "norm_gains", "mlstm_w_in", "mlstm_b_gate", "mlstm_head_gain", "mlstm_w_out",
        "diff_w_in", "diff_lambda", "diff_head_gain", "diff_w_out", "mlp_w_up", "mlp_w_down", "final_gain"]
_OUTS = [((1, X, D), "float32")]


def kernel(**inputs):
    import numpy as _np
    import concourse.bacc as _bacc
    from concourse import mybir as _mybir
    from concourse.bass_utils import run_bass_kernel_spmd as _run

    nc = _bacc.Bacc("TRN2", target_bir_lowering=False, num_devices=1)
    arrays, args = {}, {}
    for name in _INS:
        arr = _np.ascontiguousarray(inputs[name])
        arrays[f"in_{name}_dram"] = arr
        args[name] = nc.dram_tensor(f"in_{name}_dram", arr.shape, _mybir.dt.from_np(arr.dtype), kind="ExternalInput").ap()
    shape, dtype = _OUTS[0]
    out = nc.dram_tensor("out_0_dram", shape, _mybir.dt.from_np(_np.dtype(dtype)), kind="ExternalOutput").ap()
    program(nc, args, out)
    r = _run(nc, [arrays], core_ids=[0])
    return r.results[0]["out_0_dram"]
```
